# Optimizing a Trainium2 kernel written in Bass

```python
import math
import jax, jax.numpy as jnp
from jax import lax
import numpy as np

D_MODEL = 1024
BATCH = 1
SEQ = 512
DEPTH = 1

HEAD_DIM = 64
A_HEADS = 6
A_PATTERNS = ((128, 1), (512, 4), (2048, 16))
A_BLOCK = 128
B_HEADS = 4
B_KEY_DIM = 128
B_VAL_DIM = 64
B_CHUNK = 64
C_HEADS = 6
C_BLOCK = 256
C_TOPK = 3
C_QCHUNK = 32
N_BUCKETS = 32
MAX_DISTANCE = 2048
D_FF = 2816
CONV_WIDTH = 3
PLE_DIM = 256
EPS = 1e-6
NEG_BIG = -1e30

A_WIDTH = A_HEADS * HEAD_DIM
B_QK_WIDTH = B_HEADS * B_KEY_DIM
B_V_WIDTH = B_HEADS * B_VAL_DIM
C_WIDTH = C_HEADS * HEAD_DIM
MIX_WIDTH = A_WIDTH + B_V_WIDTH + C_WIDTH
IN_SPLIT_SIZES = (A_WIDTH, A_WIDTH, A_WIDTH, B_QK_WIDTH, B_QK_WIDTH, B_V_WIDTH, B_V_WIDTH, C_WIDTH, C_WIDTH, C_WIDTH)
IN_WIDTH = sum(IN_SPLIT_SIZES)

kernel_name = 'hybrid_dilated_hgrn2_moba_convffn'

def rms_norm(x, g):
    xf = x.astype(jnp.float32)
    y = xf * lax.rsqrt(jnp.mean(xf * xf, axis=-1, keepdims=True) + EPS)
    return (y * g.astype(jnp.float32)).astype(x.dtype)

def rel_bucket(dist):
    max_exact = N_BUCKETS // 2
    d = jnp.maximum(dist, 0)
    df = jnp.maximum(d, max_exact).astype(jnp.float32)
    large = max_exact + (jnp.log(df / max_exact) / math.log(MAX_DISTANCE / max_exact)
                         * (N_BUCKETS - max_exact)).astype(jnp.int32)
    large = jnp.minimum(large, N_BUCKETS - 1)
    return jnp.where(d < max_exact, d, large)

def dilated_branch(q, k, v, bias_table, window, dilation):
    Bsz, T, H, E = q.shape
    span = dilation * A_BLOCK
    Tp = -(-T // span) * span
    nb = Tp // span

    def to_blocks(a):
        a = jnp.pad(a, ((0, 0), (0, Tp - T), (0, 0), (0, 0)))
        a = a.reshape(Bsz, Tp // dilation, dilation, H, E).transpose(0, 2, 1, 3, 4)
        return a.reshape(Bsz, dilation, nb, A_BLOCK, H, E)

    def with_prev(a):
        prev = jnp.pad(a[:, :, :-1], ((0, 0), (0, 0), (1, 0), (0, 0), (0, 0), (0, 0)))
        return jnp.concatenate([prev, a], axis=3)

    qs = to_blocks(q)
    kk = with_prev(to_blocks(k))
    vv = with_prev(to_blocks(v))
    max_step = window // dilation
    qi = jnp.arange(A_BLOCK)[:, None]
    kj = jnp.arange(2 * A_BLOCK)[None, :]
    delta = qi + A_BLOCK - kj
    band = (delta >= 0) & (delta <= max_step)
    blk = jnp.arange(nb)[:, None, None]
    valid = band[None] & ((blk > 0) | (kj[None] >= A_BLOCK))
    bias = bias_table[:, rel_bucket(delta * dilation)]
    s = jnp.einsum('brnqhe,brnkhe->brnhqk', qs, kk) * (E ** -0.5) + bias
    s = jnp.where(valid[:, None], s, NEG_BIG)
    m = lax.stop_gradient(jnp.max(s, axis=-1, keepdims=True))
    pexp = jnp.exp(s - m)
    den = jnp.sum(pexp, axis=-1, keepdims=True)
    o = jnp.einsum('brnhqk,brnkhe->brnqhe', pexp / den, vv)
    lse = (m + jnp.log(den))[..., 0].transpose(0, 1, 2, 4, 3)

    def from_blocks(a):
        a = a.reshape((Bsz, dilation, nb * A_BLOCK) + a.shape[4:])
        a = jnp.swapaxes(a, 1, 2).reshape((Bsz, Tp) + a.shape[3:])
        return a[:, :T]

    return from_blocks(o), from_blocks(lse)

def dilated_attention(q, k, v, bias_table):
    outs, lses = [], []
    for window, dilation in A_PATTERNS:
        o, lse = dilated_branch(q, k, v, bias_table, window, dilation)
        outs.append(o)
        lses.append(lse)
    w = jax.nn.softmax(jnp.stack(lses, axis=0), axis=0)
    return jnp.einsum('gbth,gbthe->bthe', w, jnp.stack(outs, axis=0))

def hgrn2(q, z, i, g, lb, gnorm):
    Bsz, T, H, K = q.shape
    V = i.shape[-1]
    lb = lb.reshape(H, K)
    q = jax.nn.silu(q)
    sig = jax.nn.sigmoid(z)
    f = lb + (1.0 - lb) * sig
    log_f = jnp.log(jnp.maximum(f, 1e-30))
    kin = (1.0 - lb) * (1.0 - sig)
    Tp = -(-T // B_CHUNK) * B_CHUNK
    nc = Tp // B_CHUNK

    def chunks(a):
        a = jnp.pad(a, ((0, 0), (0, Tp - T), (0, 0), (0, 0)))
        return a.reshape(Bsz, nc, B_CHUNK, H, a.shape[-1]).transpose(1, 0, 3, 2, 4)

    causal = jnp.tril(jnp.ones((B_CHUNK, B_CHUNK), bool))[:, :, None]

    def step(S, xs):
        qc, kc, vc, gc = xs
        b = jnp.cumsum(gc, axis=2)
        diff = b[:, :, :, None, :] - b[:, :, None, :, :]
        decay = jnp.exp(jnp.where(causal, jnp.minimum(diff, 0.0), NEG_BIG))
        attn = jnp.einsum('bhik,bhjk,bhijk->bhij', qc, kc, decay)
        o = (jnp.einsum('bhij,bhjv->bhiv', attn, vc)
             + jnp.einsum('bhik,bhkv->bhiv', qc * jnp.exp(b), S))
        b_last = b[:, :, -1:, :]
        S = (jnp.exp(b_last[:, :, 0, :, None]) * S
             + jnp.einsum('bhjk,bhjv->bhkv', kc * jnp.exp(b_last - b), vc))
        return S, o

    S0 = jnp.zeros((Bsz, H, K, V), jnp.float32)
    _, o = lax.scan(step, S0, (chunks(q), chunks(kin), chunks(i), chunks(log_f)))
    o = o.transpose(1, 0, 3, 2, 4).reshape(Bsz, Tp, H, V)[:, :T]
    return rms_norm(o, gnorm) * jax.nn.silu(g)

def moba_attention(q, k, v, bias_table):
    Bsz, T, H, E = q.shape
    Tp = -(-T // C_BLOCK) * C_BLOCK
    nb = Tp // C_BLOCK
    topk = min(C_TOPK, nb)

    def heads_first(a):
        return jnp.pad(a, ((0, 0), (0, Tp - T), (0, 0), (0, 0))).transpose(0, 2, 1, 3)

    qh, kh, vh = heads_first(q), heads_first(k), heads_first(v)
    kb = kh.reshape(Bsz, H, nb, C_BLOCK, E)
    vb = vh.reshape(Bsz, H, nb, C_BLOCK, E)
    gate = jnp.einsum('bhte,bhne->bhtn', qh, jnp.mean(kb, axis=3))
    pos = jnp.arange(Tp)
    fully_past = jnp.arange(nb)[None, :] < (pos // C_BLOCK)[:, None]
    gate = jnp.where(fully_past, gate, NEG_BIG)
    gsel, idx = lax.top_k(gate, topk)
    sel_ok = gsel > 0.5 * NEG_BIG
    nq = Tp // C_QCHUNK

    def by_chunk(a):
        return a.reshape(Bsz, H, nq, C_QCHUNK, a.shape[-1]).transpose(2, 0, 1, 3, 4)

    bi = jnp.arange(Bsz)[:, None, None, None]
    hi = jnp.arange(H)[None, :, None, None]
    offs = jnp.arange(C_BLOCK)
    scale = E ** -0.5
    n_sel = topk * C_BLOCK

    def one_chunk(xs):
        qc, ic, okc, start = xs
        qpos = start + jnp.arange(C_QCHUNK)
        ksel = kb[bi, hi, ic]
        vsel = vb[bi, hi, ic]
        kpos = ic[..., None] * C_BLOCK + offs
        s_sel = (jnp.einsum('bhqe,bhqnle->bhqnl', qc, ksel) * scale
                 + bias_table[hi[..., None], rel_bucket(qpos[:, None, None] - kpos)])
        s_sel = jnp.where(okc[..., None], s_sel, NEG_BIG).reshape(Bsz, H, C_QCHUNK, n_sel)
        own = (start // C_BLOCK) * C_BLOCK
        kown = lax.dynamic_slice_in_dim(kh, own, C_BLOCK, axis=2)
        vown = lax.dynamic_slice_in_dim(vh, own, C_BLOCK, axis=2)
        rel = qpos[:, None] - (own + offs)[None, :]
        s_own = jnp.einsum('bhqe,bhle->bhql', qc, kown) * scale + bias_table[:, rel_bucket(rel)]
        s_own = jnp.where(rel >= 0, s_own, NEG_BIG)
        pr = jax.nn.softmax(jnp.concatenate([s_sel, s_own], axis=-1), axis=-1)
        return (jnp.einsum('bhqn,bhqne->bhqe', pr[..., :n_sel], vsel.reshape(Bsz, H, C_QCHUNK, n_sel, E))
                + jnp.einsum('bhql,bhle->bhqe', pr[..., n_sel:], vown))

    o = lax.map(one_chunk, (by_chunk(qh), by_chunk(idx), by_chunk(sel_ok), jnp.arange(nq) * C_QCHUNK))
    return o.transpose(1, 0, 3, 2, 4).reshape(Bsz, Tp, H, E)[:, :T]

def causal_dwconv(u, w, b):
    C = u.shape[-1]
    y = lax.conv_general_dilated(u, w[:, None, :].astype(u.dtype), window_strides=(1,),
                                 padding=((CONV_WIDTH - 1, 0),),
                                 dimension_numbers=('NWC', 'WIO', 'NWC'),
                                 feature_group_count=C)
    return y + b.astype(u.dtype)

def setup_inputs(seed: int = 0) -> dict:
    key = jax.random.key(seed)
    ks = jax.random.split(key, 17)
    f32 = jnp.float32

    def nrm(k, shape, scale):
        return jax.random.normal(k, shape, f32) * scale

    def gain(k, shape):
        return 1.0 + 0.02 * jax.random.normal(k, shape, f32)

    return {
        'x': nrm(ks[0], (BATCH, SEQ, D_MODEL), 1.0),
        'p': nrm(ks[1], (DEPTH, BATCH, SEQ, PLE_DIM), 1.0),
        'rel_bias': nrm(ks[2], (A_HEADS + C_HEADS, N_BUCKETS), 0.5),
        'norm_mix': gain(ks[3], (DEPTH, D_MODEL)),
        'w_in': nrm(ks[4], (DEPTH, D_MODEL, IN_WIDTH), D_MODEL ** -0.5),
        'w_out': nrm(ks[5], (DEPTH, MIX_WIDTH, D_MODEL), MIX_WIDTH ** -0.5),
        'lower_bounds': nrm(ks[6], (DEPTH, B_QK_WIDTH), 0.1),
        'hgrn_gnorm': gain(ks[7], (DEPTH, B_VAL_DIM)),
        'norm_ffn': gain(ks[8], (DEPTH, D_MODEL)),
        'w_up': nrm(ks[9], (DEPTH, D_MODEL, 2 * D_FF), D_MODEL ** -0.5),
        'conv_w': nrm(ks[10], (DEPTH, CONV_WIDTH, 2 * D_FF), CONV_WIDTH ** -0.5),
        'conv_b': nrm(ks[11], (DEPTH, 2 * D_FF), 0.01),
        'w_down': nrm(ks[12], (DEPTH, D_FF, D_MODEL), D_FF ** -0.5),
        'norm_ple': gain(ks[13], (DEPTH, D_MODEL)),
        'w_pe': nrm(ks[14], (DEPTH, PLE_DIM, D_MODEL), PLE_DIM ** -0.5),
        'w_pg': nrm(ks[15], (DEPTH, D_MODEL, D_MODEL), D_MODEL ** -0.5),
        'norm_final': gain(ks[16], (D_MODEL,)),
    }

def reference(x, p, rel_bias, norm_mix, w_in, w_out, lower_bounds, hgrn_gnorm, norm_ffn,
              w_up, conv_w, conv_b, w_down, norm_ple, w_pe, w_pg, norm_final):
    Bsz, T, _ = x.shape
    f32 = jnp.float32
    lb_sm = jax.nn.softmax(lower_bounds.astype(f32), axis=0)
    lb_all = jnp.cumsum(lb_sm, axis=0) - lb_sm[0]
    bias_a = rel_bias[:A_HEADS].astype(f32)
    bias_c = rel_bias[A_HEADS:].astype(f32)
    split_at = [int(s) for s in np.cumsum(IN_SPLIT_SIZES)[:-1]]

    for i in range(DEPTH):
        h = rms_norm(x, norm_mix[i])
        proj = (h @ w_in[i]).astype(f32)
        qa, ka, va, qb, fb, ib, gb, qc, kc, vc = jnp.split(proj, split_at, axis=-1)
        ya = dilated_attention(qa.reshape(Bsz, T, A_HEADS, HEAD_DIM), ka.reshape(Bsz, T, A_HEADS, HEAD_DIM),
                               va.reshape(Bsz, T, A_HEADS, HEAD_DIM), bias_a)
        yb = hgrn2(qb.reshape(Bsz, T, B_HEADS, B_KEY_DIM), fb.reshape(Bsz, T, B_HEADS, B_KEY_DIM),
                   ib.reshape(Bsz, T, B_HEADS, B_VAL_DIM), gb.reshape(Bsz, T, B_HEADS, B_VAL_DIM),
                   lb_all[i], hgrn_gnorm[i].astype(f32))
        yc = moba_attention(qc.reshape(Bsz, T, C_HEADS, HEAD_DIM), kc.reshape(Bsz, T, C_HEADS, HEAD_DIM),
                            vc.reshape(Bsz, T, C_HEADS, HEAD_DIM), bias_c)
        mix = jnp.concatenate([ya.reshape(Bsz, T, A_WIDTH), yb.reshape(Bsz, T, B_V_WIDTH),
                               yc.reshape(Bsz, T, C_WIDTH)], axis=-1).astype(x.dtype)
        x = x + mix @ w_out[i]
        h = rms_norm(x, norm_ffn[i])
        u = causal_dwconv(h @ w_up[i], conv_w[i], conv_b[i])
        ug, uv = jnp.split(u, 2, axis=-1)
        x = x + (jax.nn.silu(ug) * uv) @ w_down[i]
        gate = jax.nn.sigmoid(rms_norm(x, norm_ple[i]) @ w_pg[i])
        x = x + gate * (p[i].astype(x.dtype) @ w_pe[i])

    return rms_norm(x, norm_final)


_drawn_inputs = setup_inputs


def setup_inputs(seed=0):
    import zlib

    import numpy as np

    out = dict(_drawn_inputs(seed))
    spreads = {}
    factors = {'norm_mix': 6.067,
     'hgrn_gnorm': 8.0,
     'norm_ffn': 15.294,
     'conv_b': 29.46,
     'norm_ple': 200.0,
     'norm_final': 23.335,
     'w_pg': 22.928,
     'p': 8.0,
     'w_pe': 8.0}
    for name, (base, spread) in spreads.items():
        noise = np.random.default_rng([zlib.crc32(name.encode()), seed]).standard_normal(out[name].shape)
        drawn = base * np.exp(spread * noise) if base else spread * noise
        out[name] = __import__('jax').numpy.asarray(drawn.astype(out[name].dtype))
    for name, factor in factors.items():
        out[name] = (out[name] * factor).astype(out[name].dtype)
    return out
```

```python
from contextlib import ExitStack

import numpy as np

import concourse.bass as bass
from concourse import mybir

ALU = mybir.AluOpType
ACT = mybir.ActivationFunctionType
F32 = mybir.dt.float32
F32R = mybir.dt.float32r
I32 = mybir.dt.int32

P = 128
SEQ = 512
D = 1024
KT = D // P
TT = SEQ // P
HEAD = 64
FF = 2816
FT = FF // P
PLE = 256
EPS = 1e-6
N_BUCKETS = 32
MAX_DISTANCE = 2048
HEADS = 12
PAIRS = HEADS // 2
B_HEADS = 4
LEVELS = 9
MASKED_LEVELS = 7
TABLE = SEQ + P
LOG_FLOOR = float(np.log(1e-30))
SCALE = HEAD ** -0.5
NEG_BIG = -1e30

A_Q, A_K, A_V, B_Q, B_Z, B_I, B_G, C_Q, C_K, C_V = 0, 3, 6, 9, 13, 17, 19, 21, 24, 27

UNITS = []
GROUPS = []


def _unit(matrix, k0, nk, c0, nc=P):
    UNITS.append((matrix, k0, nk, c0, nc))


def _group(kind, index):
    GROUPS.append((kind, index, len(UNITS) - 1))


for _h in range(B_HEADS):
    _unit("w_in", 0, KT, (B_Z + _h) * P)
    _group("z", _h)
for _b in range(2):
    _unit("w_in", 0, KT, (B_G + _b) * P)
    _group("g", _b)
for _h in range(B_HEADS):
    _unit("w_in", 0, KT, (B_Q + _h) * P)
    _group("bq", _h)
for _b in range(2):
    _unit("w_in", 0, KT, (B_I + _b) * P)
    _group("v", _b)
for _p in range(PAIRS):
    for _kind, _a, _c in (("q", A_Q, C_Q), ("k", A_K, C_K), ("v", A_V, C_V)):
        _unit("w_in", 0, KT, ((_a + _p) if _p < 3 else (_c + _p - 3)) * P)
        _group(_kind, _p + 2 if _kind == "v" else _p)
PROJ = len(UNITS)
for _f in range(KT):
    _unit("w_out", 0, KT, _f * P)
    _group("x", KT + _f)
UP = len(UNITS)
for _j in range(FT):
    _unit("w_up", 0, KT, _j * P)
    _group("gate", _j)
    _unit("w_up", 0, KT, FF + _j * P)
    _group("value", _j)
DOWN = len(UNITS)
for _f in range(KT):
    for _k0 in range(0, FT, KT):
        _unit("w_down", _k0, min(KT, FT - _k0), _f * P)
    _group("x", 2 * KT + _f)
PE_UNITS = len(UNITS)
for _c in range(2):
    _unit("w_pe", 0, PLE // P, _c * 512, 512)
PG = len(UNITS)
for _f in range(KT):
    _unit("w_pg", 0, KT, _f * P)
    _group("ple", _f)
N_UNITS = len(UNITS)

ON_ACT = ("g", "bq", "v", "q", "ple")
RAW = 4
SPLIT = 2

V_UNITS = [g[2] for g in GROUPS if g[0] == "v"]
ROUND_SLOT = 10
ROUNDS = 2 * (LEVELS + 1)


def rounds_in(slot):
    return [n for n in range(ROUNDS) if ROUND_SLOT + n * 2 // 5 == slot]


B_OUT_SLOT = ROUND_SLOT + ROUNDS * 2 // 5
HEAD_SLOTS = [B_OUT_SLOT + 1 + h for h in range(10)] + [30, 31]
FLUSH_SLOT = 29
STEPS = HEADS * TT
BATCH = [(0, 40), (40, 48)]


def steps_in(slot):
    return [TT * HEAD_SLOTS.index(slot) + i for i in range(TT)] if slot in HEAD_SLOTS else []


def batch_start(n):
    return 0 if n < BATCH[0][1] else BATCH[1][0]


def rel_bucket(d):
    exact = N_BUCKETS // 2
    d = max(d, 0)
    if d < exact:
        return d
    return min(N_BUCKETS - 1, exact + int(np.log(d / exact) / np.log(MAX_DISTANCE / exact) * (N_BUCKETS - exact)))


def shape_constants():
    square = np.concatenate([np.eye(P), np.ones((P, P)), np.kron(np.eye(2), np.ones((HEAD, HEAD))), np.eye(P)[::-1]], 1)
    onehot = np.zeros((N_BUCKETS, TABLE))
    extra = np.full((HEADS, TABLE), NEG_BIG)
    for j in range(TABLE):
        d = SEQ - 1 - j
        onehot[rel_bucket(d), j] = 1
        if d >= 0:
            seen = (d <= 128) + (d % 4 == 0) + (d % 16 == 0)
            if seen:
                extra[:6, j] = np.log(seen)
            extra[6:, j] = 0
    j, i = np.arange(P)[:, None], np.arange(P)[None, :]
    masks = [j == i]
    for level in range(MASKED_LEVELS):
        s = 1 << level
        masks.append((j // (2 * s) == i // (2 * s)) & (j % (2 * s) < s) & (i % (2 * s) >= s))
    return {
        "c_square": square.astype(np.float32),
        "c_onehot": onehot.astype(np.float32),
        "c_extra": extra.astype(np.float32),
        "c_masks": np.concatenate(masks, 1).astype(np.int32),
    }


def build(nc, a, out):
    bias_dram = nc.dram_tensor("bias_table", [HEADS, TABLE], F32, kind="Internal").ap()
    with ExitStack() as ctx:
        def sb(name, shape, dt=F32, stack=ctx):
            return stack.enter_context(nc.sbuf_tensor(name, shape, dt))

        def sem(name):
            return ctx.enter_context(nc.semaphore(name))

        x_t = sb("x_t", [P, KT, SEQ])
        h_hi = sb("h_hi", [P, KT, SEQ], F32R)
        h_lo = sb("h_lo", [P, KT, SEQ], F32R)
        raw = sb("raw", [P, RAW, 1024])
        w_hi = sb("w_hi", [P, SPLIT, 1024], F32R)
        w_lo = sb("w_lo", [P, SPLIT, 1024], F32R)
        square = sb("square", [P, 4 * P])
        ident, ones, half_ones, flip = (square[:, i * P:(i + 1) * P] for i in range(4))
        vec_cols = sb("vec_cols", [P, 4 * KT + 1])
        conv_cols = sb("conv_cols", [P, 4, 2 * FT])
        eps_col = sb("eps_col", [P, 1])
        sumsq = sb("sumsq", [P, SEQ])
        scratch = sb("scratch", [P, 4, SEQ])
        var = sb("var", [P, SEQ])
        rstd = sb("rstd", [P, SEQ])

        mixing = ExitStack()
        mix_b_hi = sb("mix_b_hi", [P, 2, SEQ], F32R, mixing)
        mix_b_lo = sb("mix_b_lo", [P, 2, SEQ], F32R, mixing)
        q_pad = sb("q_pad", [P, 3, 2, SEQ], F32, mixing)
        k_t = sb("k_t", [P, 3, SEQ], F32, mixing)
        v_tok = sb("v_tok", [P, 3, TT, P], F32, mixing)
        v_t = sb("v_t", [P, SEQ], F32, mixing)
        hgrn = ExitStack()
        b_fwd = sb("b_fwd", [P, 2, 1024], F32, hgrn)
        b_kin = sb("b_kin", [P, 2, 1024], F32, hgrn)
        b_q = sb("b_q", [P, 2, 1024], F32, hgrn)
        b_bwd = sb("b_bwd", [P, 2, 1024], F32, hgrn)
        b_qk = sb("b_qk", [P, 2, 1024], F32, hgrn)
        b_att = sb("b_att", [P, B_HEADS, 10 * P], F32, hgrn)
        b_v = sb("b_v", [P, 2, TT, P], F32, hgrn)
        b_gate = sb("b_gate", [P, 2, SEQ], F32, hgrn)
        masks = sb("masks", [P, 8 * P], I32, hgrn)
        hgrn.close()
        bias = sb("bias", [P, 2, 2, SEQ], F32, mixing)
        probs = sb("probs", [P, 3, SEQ], F32, mixing)
        probs_t = sb("probs_t", [P, 3, SEQ], F32, mixing)
        mix_a_hi = sb("mix_a_hi", [P, PAIRS, SEQ], F32R, mixing)
        mix_a_lo = sb("mix_a_lo", [P, PAIRS, SEQ], F32R, mixing)
        row_sum = sb("row_sum", [P, STEPS], F32, mixing)
        row_min = sb("row_min", [P, STEPS], F32, mixing)
        row_inv = sb("row_inv", [P, STEPS], F32, mixing)
        mixing.close()
        setup = ExitStack()
        sb("under_setup", [P, 66 * 1024 // 4], F32, setup)
        x_rows = sb("x_rows", [P, TT, D], F32, setup)
        vec_rows = sb("vec_rows", [4 * KT + 1, P], F32, setup)
        conv_rows = sb("conv_rows", [2 * FT, 4, P], F32, setup)
        rel_t = sb("rel_t", [N_BUCKETS, HEADS], F32, setup)
        onehot = sb("onehot", [N_BUCKETS, TABLE], F32, setup)
        extra = sb("extra", [HEADS, TABLE], F32, setup)
        table = sb("table", [HEADS, TABLE], F32, setup)
        setup.close()
        conv_g = sb("conv_g", [P, 2, SEQ])
        conv_v = sb("conv_v", [P, 2, SEQ])
        p_hi = sb("p_hi", [P, 2, SEQ], F32R)
        p_lo = sb("p_lo", [P, 2, SEQ], F32R)
        mlp = ExitStack()
        act_hi = sb("act_hi", [P, FT, SEQ], F32R, mlp)
        act_lo = sb("act_lo", [P, FT, SEQ], F32R, mlp)
        mlp.close()
        pe_out = sb("pe_out", [P, KT, SEQ])
        y_rows = sb("y_rows", [P, TT, D])
        p_rows = conv_g[:, :, :].rearrange("p a n -> p (a n)").rearrange("p (t c) -> p t c", t=TT)

        banks = [ctx.enter_context(nc.psum_tensor(f"bank{i}", [P, 512], F32)) for i in range(8)]
        acc, score, turned, outs = banks[0:2], banks[2:4], banks[4:6], banks[6:8]

        raw_full = [sem(f"raw_full{i}") for i in range(RAW)]
        whi_ready, wlo_ready, unit_done = sem("whi_ready"), sem("wlo_ready"), sem("unit_done")
        acc_read_act, acc_read_dve = sem("acc_read_act"), sem("acc_read_dve")
        square_in, masks_in, x_in, vec_in, table_in = (sem(s) for s in ("square_in", "masks_in", "x_in", "vec_in", "table_in"))
        filled = sem("filled")
        vec_turned, vec_ready = sem("vec_turned"), sem("vec_ready")
        table_sum, table_ready, table_out = sem("table_sum"), sem("table_ready"), sem("table_out")
        x_turned, x_ready, sq_ready, sumsq_ready = (sem(s) for s in ("x_turned", "x_ready", "sq_ready", "sumsq_ready"))
        norm_sum, var_ready, ln_ready, rstd_ready, newton = (sem(s) for s in ("norm_sum", "var_ready", "ln_ready", "rstd_ready", "newton"))
        h_full, h_hi_ready, h_lo_dve, h_lo_pool = (sem(s) for s in ("h_full", "h_hi_ready", "h_lo_dve", "h_lo_pool"))
        v_turned, v_ready = sem("v_turned"), sem("v_ready")
        z_chain, kin_arg, g_ready, kin_ready = (sem(s) for s in ("z_chain", "kin_arg", "g_ready", "kin_ready"))
        decay_ready, qk_ready, sums_ready = sem("decay_ready"), sem("qk_ready"), sem("sums_ready")
        b_scored, b_kept, b_out, b_squared = (sem(s) for s in ("b_scored", "b_kept", "b_out", "b_squared"))
        b_normed, b_gated, b_hi_ready, b_mixed = (sem(s) for s in ("b_normed", "b_gated", "b_hi_ready", "b_mixed"))
        bias_in = [sem("bias_in0"), sem("bias_in1")]
        scored, logits, exped, inverted, normed = (sem(s) for s in ("scored", "logits", "exped", "inverted", "normed"))
        probs_turned, probs_t_ready, weighted = (sem(s) for s in ("probs_turned", "probs_t_ready", "weighted"))
        mix_hi_ready, mix_ready = sem("mix_hi_ready"), sem("mix_ready")
        tap2_ready, tap1_ready, silu_ready, prod_ready = (sem(s) for s in ("tap2_ready", "tap1_ready", "silu_ready", "prod_ready"))
        act_hi_ready, act_ready = sem("act_hi_ready"), sem("act_ready")
        p_in, p_turned, p_hi_ready, p_ready = (sem(s) for s in ("p_in", "p_turned", "p_hi_ready", "p_ready"))
        pe_done, pe_kept, gated = sem("pe_done"), sem("pe_kept"), sem("gated")
        y_full, y_turned, y_kept, stored = (sem(s) for s in ("y_full", "y_turned", "y_kept", "stored"))

        block = ctx.enter_context(nc.Block())
        GROUP_OF = {g[2]: i for i, g in enumerate(GROUPS)}
        GROUP_AT = {(g[0], g[1]): i for i, g in enumerate(GROUPS)}

        def wait_taken(eng, group):
            kind, index, _ = GROUPS[group]
            if kind == "x":
                eng.wait_ge(x_ready, index + 1)
                return
            on_act = kind in ON_ACT
            n = sum((g[0] in ON_ACT) == on_act for g in GROUPS[:group + 1] if g[0] != "x")
            eng.wait_ge(acc_read_act if on_act else acc_read_dve, n)

        def halves(tile, pair, s):
            v = tile[:, pair, :].rearrange("p (b t) -> p b t", t=2 * s)
            return v[:, :, 0:s], v[:, :, s:2 * s]

        ATT_AT = {(b, b): b for b in range(TT)}
        ATT_AT.update({(0, 1): 4, (2, 3): 5, (0, 2): 6, (0, 3): 7, (1, 2): 8, (1, 3): 9})

        def turned_before(n):
            at, i = HEAD_SLOTS[n // TT], n % TT
            return sum(u + 1 < at or (u + 1 == at and i > 0) for u in V_UNITS)

        w_dram = {name: a[name][0] for name in ("w_in", "w_out", "w_up", "w_down", "w_pe", "w_pg")}

        @block.sync
        def _(sp):
            for t in range(TT):
                sp.dma_start(x_rows[:, t, :], a["x"][0, t * P:(t + 1) * P, :]).then_inc(x_in, 16)
            for u, (name, k0, nk, c0, ncol) in enumerate(UNITS):
                if u >= RAW:
                    sp.wait_ge(wlo_ready, u - RAW + 1)
                src = w_dram[name][k0 * P:(k0 + nk) * P, c0:c0 + ncol].rearrange("(k p) c -> p k c", p=P)
                dst = raw[:, u % RAW, 0:nk * ncol].rearrange("p (k c) -> p k c", c=ncol)
                sp.dma_start(dst, src).then_inc(raw_full[u % RAW], 16)
                if u == DOWN + RAW:
                    sp.wait_ge(prod_ready, FT)
                    sp.dma_start(p_rows, a["p"][0, 0].rearrange("(t p) c -> p t c", p=P)).then_inc(p_in, 16)
            for half in range(2):
                sp.wait_ge(y_kept, (half + 1) * KT // 2)
                sp.dma_start(out[0].rearrange("(t p) c -> p t c", p=P)[:, :, half * 512:(half + 1) * 512],
                             y_rows[:, :, half * 512:(half + 1) * 512]).then_inc(stored, 16)
            sp.wait_ge(stored, 32)

        @block.tensor
        def _(pe):
            def products(bank, slot, k, nc_cols, c, x_hi, x_lo, first, last):
                at = k * nc_cols + c
                hi, lo = w_hi[:, slot, at:at + P], w_lo[:, slot, at:at + P]
                pe.matmul(bank[:, :], hi, x_hi, start=first, stop=False)
                pe.matmul(bank[:, :], hi, x_lo, start=False, stop=False)
                return pe.matmul(bank[:, :], lo, x_hi, start=False, stop=last)

            def wait_h(stage, k):
                if k % 2:
                    pe.wait_ge(h_lo_pool, stage * KT // 2 + k // 2 + 1)
                else:
                    pe.wait_ge(h_lo_dve, stage * KT // 2 + k // 2 + 1)

            def begin_unit(u, group):
                pe.wait_ge(wlo_ready, u + 1)
                if group >= 2:
                    wait_taken(pe, group - 2)

            def norm_sum_of(stage):
                pe.wait_ge(sumsq_ready, KT * (stage + 1))
                pe.matmul(score[0][:, :], ones, sumsq[:, :], start=True, stop=True).then_inc(norm_sum, 1)

            def b_round(n):
                level, pair = n // 2, n % 2
                if n < 2:
                    for h in range(2 * pair, 2 * pair + 2):
                        wait_taken(pe, GROUP_AT["bq", h])
                    pe.wait_ge(kin_ready, B_HEADS)
                else:
                    pe.wait_ge(qk_ready, 2 * (n - 1))
                for hh in range(2):
                    use = 2 * n + hh
                    if use >= 2:
                        pe.wait_ge(b_kept, use - 1)
                    bank, at = score[hh], hh * SEQ
                    keys, queries = (b_kin, b_q) if level == 0 else (b_qk, b_qk)
                    if level <= MASKED_LEVELS:
                        parts = [(b, b, 1, b) for b in range(TT)]
                    elif level == MASKED_LEVELS + 1:
                        parts = [(0, 1, 1, 0), (2, 3, 1, 1)]
                    else:
                        parts = [(0, 2, 2, 0), (1, 2, 2, 2)]
                    for jb, ib, nb, to in parts:
                        mm = pe.matmul(bank[:, to * P:(to + nb) * P],
                                       keys[:, pair, at + jb * P:at + (jb + 1) * P],
                                       queries[:, pair, at + ib * P:at + (ib + nb) * P],
                                       start=True, stop=True)
                    mm.then_inc(b_scored, 1)

            def b_values(pair):
                pe.wait_ge(b_kept, 2 * ROUNDS)
                pe.wait_ge(v_ready, pair + 1)
                for hh in range(2):
                    rows = slice(hh * HEAD, (hh + 1) * HEAD)
                    for ib in range(TT):
                        for jb in range(ib + 1):
                            at = ATT_AT[jb, ib] * P
                            mm = pe.matmul(outs[pair][rows, ib * P:(ib + 1) * P], b_v[:, pair, jb, rows],
                                           b_att[:, 2 * pair + hh, at:at + P], start=(jb == 0), stop=(jb == ib))
                mm.then_inc(b_out, 1)

            def b_norm_sum(pair):
                pe.wait_ge(b_squared, pair + 1)
                pe.matmul(score[pair][:, :], half_ones, scratch[:, pair, :], start=True, stop=True)\
                  .then_inc(norm_sum, 1)

            def turn_values(unit):
                g = V_UNITS.index(unit)
                wait_taken(pe, GROUP_OF[unit])
                steps = TT * sum(s < unit + 1 for s in HEAD_SLOTS)
                if steps:
                    done = steps - 1 if steps - 2 >= batch_start(steps) else steps
                    pe.wait_ge(probs_t_ready, done)
                if g:
                    pe.wait_ge(v_ready, g)
                for t in range(TT):
                    mm = pe.transpose(turned[0][:, t * P:(t + 1) * P], v_t[:, t * P:(t + 1) * P], ident)
                mm.then_inc(v_turned, 1)

            def step_score(n):
                head, i = n // TT, n % TT
                pair = head // 2
                if n % (2 * TT) == 0:
                    wait_taken(pe, GROUP_AT["q", pair])
                    wait_taken(pe, GROUP_AT["k", pair])
                if n < 2:
                    pe.wait_ge(var_ready, n + 2)
                else:
                    pe.wait_ge(logits, n - 1)
                keys = (i + 1) * P
                pe.matmul(score[n % 2][:, 0:keys], q_pad[:, pair % 3, head % 2, i * P:(i + 1) * P],
                          k_t[:, pair % 3, 0:keys], start=True, stop=True).then_inc(scored, 1)

            def step_turn(n):
                pe.wait_ge(normed, n + 1)
                if n >= 2:
                    pe.wait_ge(probs_t_ready, n - 1)
                if turned_before(n):
                    pe.wait_ge(v_ready, turned_before(n))
                for b in range(n % TT + 1):
                    mm = pe.transpose(turned[n % 2][:, b * P:(b + 1) * P], probs[:, n % 3, b * P:(b + 1) * P], flip)
                mm.then_inc(probs_turned, 1)

            def step_values(n):
                head, i = n // TT, n % TT
                pair, rows = head // 2, slice((head % 2) * HEAD, (head % 2 + 1) * HEAD)
                pe.wait_ge(probs_t_ready, n + 1)
                if n % (2 * TT) == 0:
                    pe.wait_ge(v_ready, 2 + pair + 1)
                    if pair < 2:
                        pe.wait_ge(b_normed, pair + 1)
                    else:
                        pe.wait_ge(mix_ready, pair - 1)
                for jb in range(i + 1):
                    mm = pe.matmul(outs[pair % 2][rows, i * P:(i + 1) * P], v_tok[:, pair % 3, jb, rows],
                                   probs_t[:, n % 3, jb * P:(jb + 1) * P], start=(jb == 0), stop=(jb == i))
                mm.then_inc(weighted, 1)

            def step(n):
                first = batch_start(n)
                step_score(n)
                if n - 2 >= first:
                    step_turn(n - 2)
                if n - 3 >= first:
                    step_values(n - 3)

            def flush(last):
                step_turn(last - 1)
                step_values(last - 2)
                step_turn(last)
                step_values(last - 1)
                step_values(last)

            def mixers(slot, k):
                for at, n in zip((1, 4, 6), rounds_in(slot)):
                    if k == at:
                        b_round(n)
                if slot == B_OUT_SLOT:
                    if k == 1:
                        b_values(0)
                    if k == 4:
                        b_values(1)
                    if k == 6:
                        b_norm_sum(0)
                if slot == B_OUT_SLOT + 1 and k == 0:
                    b_norm_sum(1)
                for i, n in enumerate(steps_in(slot)):
                    if k == (1 + 2 * i if slot < PROJ else 2 * i):
                        step(n)
                if slot == FLUSH_SLOT and k == 1:
                    flush(BATCH[0][1] - 1)
                if slot - 1 in V_UNITS and k == 2:
                    turn_values(slot - 1)

            pe.wait_ge(square_in, 16)
            pe.wait_ge(vec_in, 16 * 8)
            pe.transpose(banks[7][:, 0:4 * KT + 1], vec_rows[:, :], ident[0:4 * KT + 1, 0:4 * KT + 1])
            for c in range(4):
                mm = pe.transpose(banks[7][:, 64 + c * 2 * FT:64 + (c + 1) * 2 * FT], conv_rows[:, c, :],
                                  ident[0:2 * FT, 0:2 * FT])
            mm.then_inc(vec_turned, 1)
            pe.wait_ge(table_in, 16 * 3)
            pe.matmul(banks[6][0:HEADS, :], rel_t[:, :], onehot[:, 0:512], start=True, stop=True)
            pe.matmul(banks[5][0:HEADS, 0:TABLE - 512], rel_t[:, :], onehot[:, 512:TABLE], start=True, stop=True)\
              .then_inc(table_sum, 1)
            pe.wait_ge(x_in, 16 * TT)
            for f in range(KT):
                if f >= 3:
                    pe.wait_ge(x_ready, f - 2)
                for t in range(TT):
                    mm = pe.transpose(banks[2 + f % 3][:, t * P:(t + 1) * P], x_rows[:, t, f * P:(f + 1) * P], ident)
                mm.then_inc(x_turned, 1)
            norm_sum_of(0)

            for u in range(PROJ):
                begin_unit(u, GROUP_OF[u])
                for k in range(KT):
                    if u == 0:
                        wait_h(0, k)
                    mm = products(acc[u % 2], u % SPLIT, k, P, 0, h_hi[:, k, :], h_lo[:, k, :], k == 0, k == KT - 1)
                    if k == KT - 1:
                        mm.then_inc(unit_done, 1)
                    mixers(u, k)

            def mixed(k):
                if 3 <= k < 5:
                    return mix_b_hi[:, k - 3, :], mix_b_lo[:, k - 3, :]
                pair = k if k < 3 else k - 2
                return mix_a_hi[:, pair, :], mix_a_lo[:, pair, :]

            for u in range(PROJ, UP):
                early = u < PROJ + 2
                begin_unit(u, GROUP_OF[u])
                if u == PROJ:
                    pe.wait_ge(b_mixed, 2)
                    pe.wait_ge(mix_ready, PAIRS - 1)
                for k in range(KT - 1 if early else KT):
                    mm = products(acc[u % 2], u % SPLIT, k, P, 0, *mixed(k), k == 0, k == KT - 1)
                    if early:
                        mixers(u, k)
                if u == PROJ + 1:
                    flush(STEPS - 1)
                    pe.wait_ge(mix_ready, PAIRS)
                    for v in (PROJ, PROJ + 1):
                        products(acc[v % 2], v % SPLIT, KT - 1, P, 0, *mixed(KT - 1), False, True).then_inc(unit_done, 1)
                if not early:
                    mm.then_inc(unit_done, 1)
            norm_sum_of(1)

            for u in range(UP, DOWN):
                group = GROUP_OF[u]
                begin_unit(u, group)
                for k in range(KT):
                    if u == UP:
                        wait_h(1, k)
                    mm = products(acc[group % 2], u % SPLIT, k, P, 0, h_hi[:, k, :], h_lo[:, k, :], k == 0, k == KT - 1)
                mm.then_inc(unit_done, 1)

            for u in range(DOWN, PE_UNITS):
                _, k0, nk, _, _ = UNITS[u]
                f = (u - DOWN) // 3
                group = GROUP_AT["x", 2 * KT + f]
                pe.wait_ge(wlo_ready, u + 1)
                if k0 == 0:
                    wait_taken(pe, group - 2)
                for k in range(nk):
                    if f == 0:
                        pe.wait_ge(act_ready, k0 + k + 1)
                    mm = products(acc[group % 2], u % SPLIT, k, P, 0, act_hi[:, k0 + k, :], act_lo[:, k0 + k, :],
                                  k0 + k == 0, k0 + k == FT - 1)
                mm.then_inc(unit_done, 1)
                if u == DOWN + 8:
                    pe.wait_ge(p_in, 16)
                    for c in range(2):
                        for t in range(TT):
                            mm = pe.transpose(turned[c][:, t * P:(t + 1) * P], p_rows[:, t, c * P:(c + 1) * P], ident)
                    mm.then_inc(p_turned, 1)

            for u in range(PE_UNITS, PG):
                pe.wait_ge(wlo_ready, u + 1)
                if u == PE_UNITS:
                    pe.wait_ge(p_ready, 2)
                for c in range(4):
                    f = 4 * (u - PE_UNITS) + c
                    if f >= 5:
                        pe.wait_ge(pe_kept, f - 4)
                    for k in range(2):
                        mm = products(banks[3 + f % 5], u % SPLIT, k, 512, c * P, p_hi[:, k, :], p_lo[:, k, :], k == 0, k == 1)
                    mm.then_inc(unit_done if c == 3 else pe_done, 1)
                if u == PE_UNITS:
                    norm_sum_of(2)

            for f in range(KT):
                u, group = PG + f, GROUP_AT["ple", f]
                begin_unit(u, group)
                for k in range(KT):
                    if f == 0:
                        wait_h(2, k)
                    mm = products(acc[group % 2], u % SPLIT, k, P, 0, h_hi[:, k, :], h_lo[:, k, :], k == 0, k == KT - 1)
                mm.then_inc(unit_done, 1)
            norm_sum_of(3)

            for f in range(KT):
                pe.wait_ge(y_full, f + 1)
                if f >= 3:
                    pe.wait_ge(y_kept, f - 2)
                for t in range(TT):
                    mm = pe.transpose(banks[4 + f % 3][:, t * P:(t + 1) * P], scratch[:, f % 4, t * P:(t + 1) * P], ident)
                mm.then_inc(y_turned, 1)

        @block.scalar
        def _(act):
            act.dma_start(square[:, :], a["c_square"]).then_inc(square_in, 16)
            for i, name in enumerate(("norm_mix", "norm_ffn", "norm_ple", "norm_final")):
                src = a[name] if name == "norm_final" else a[name][0]
                act.dma_start(vec_rows[i * KT:(i + 1) * KT, :], src.rearrange("(k p) -> k p", p=P)).then_inc(vec_in, 16)
            for h in range(2):
                act.dma_start(vec_rows[4 * KT:4 * KT + 1, h * HEAD:(h + 1) * HEAD], a["hgrn_gnorm"]).then_inc(vec_in, 16)
            act.dma_start(conv_rows[:, 0:3, :], a["conv_w"][0].rearrange("t (b p) -> b t p", p=P)).then_inc(vec_in, 16)
            act.dma_start(conv_rows[:, 3, :], a["conv_b"][0].rearrange("(b p) -> b p", p=P)).then_inc(vec_in, 16)
            act.dma_start(rel_t[:, :], a["rel_bias"].rearrange("h b -> b h"), allow_slow_non_contiguous=True).then_inc(table_in, 16)
            act.dma_start(onehot[:, :], a["c_onehot"]).then_inc(table_in, 16)
            act.dma_start(extra[:, :], a["c_extra"]).then_inc(table_in, 16)
            act.dma_start(masks[:, :], a["c_masks"]).then_inc(masks_in, 16)

            def split_hi(u):
                _, _, nk, _, ncol = UNITS[u]
                act.wait_ge(raw_full[u % RAW], 16 * (u // RAW + 1))
                if u >= SPLIT:
                    act.wait_ge(unit_done, u - SPLIT + 1)
                act.activation(w_hi[:, u % SPLIT, 0:nk * ncol], raw[:, u % RAW, 0:nk * ncol], ACT.Copy)\
                   .then_inc(whi_ready, 1)

            def square_x(n):
                act.wait_ge(x_ready, n + 1)
                if n >= 2:
                    act.wait_ge(sumsq_ready, n - 1)
                act.activation(scratch[:, n % 2, :], x_t[:, n % KT, :], ACT.Square).then_inc(sq_ready, 1)

            def rstd_of(index, bank, count):
                act.wait_ge(norm_sum, index + 1)
                act.activation(var[:, :], bank[:, :], ACT.Identity, bias=eps_col[:, :], scale=1.0 / count).then_inc(var_ready, 1)
                act.wait_ge(var_ready, index + 1)
                act.activation(rstd[:, :], var[:, :], ACT.Ln).then_inc(ln_ready, 1)
                act.wait_ge(ln_ready, index + 1)
                act.activation(rstd[:, :], rstd[:, :], ACT.Exp, scale=-0.5).then_inc(rstd_ready, 1)

            def split_h(stage):
                for k in range(KT):
                    n = stage * KT + k
                    act.wait_ge(h_full, n + 1)
                    act.activation(h_hi[:, k, :], scratch[:, k % 4, :], ACT.Copy).then_inc(h_hi_ready, 1)

            def take(group):
                kind, i, unit = GROUPS[group]
                if kind == "x":
                    square_x(i)
                    return
                act.wait_ge(unit_done, unit + 1)
                bank = acc[group % 2]
                if kind == "z":
                    t = scratch[:, i, :]
                    act.activation(t, bank[:, :], ACT.Abs).then_inc(z_chain, 1)
                    act.wait_ge(z_chain, 3 * i + 1)
                    act.activation(t, t, ACT.Exp, scale=-1.0).then_inc(z_chain, 1)
                    act.wait_ge(z_chain, 3 * i + 2)
                    act.activation(t, t, ACT.Ln, bias=1.0).then_inc(z_chain, 1)
                elif kind == "g":
                    act.activation(b_gate[:, i, :], bank[:, :], ACT.Silu).then_inc(acc_read_act, 1)
                elif kind == "bq":
                    act.activation(b_q[:, i // 2, (i % 2) * SEQ:(i % 2 + 1) * SEQ], bank[:, :], ACT.Silu)\
                       .then_inc(acc_read_act, 1)
                elif kind == "v":
                    if i:
                        act.wait_ge(v_turned, i)
                    act.activation(v_t[:, :], bank[:, :], ACT.Copy).then_inc(acc_read_act, 1)
                elif kind == "q":
                    act.wait_ge(filled, 3)
                    if i >= 3:
                        act.wait_ge(scored, 2 * TT * (i - 2))
                    low, high = (bass.AP(tensor=bank[:, :].tensor, offset=bank[r:r + 1, :].offset + P - 1,
                                         ap=[[512, HEAD], [P, TT], [-1, P]]) for r in (0, HEAD))
                    act.activation(q_pad[0:HEAD, i % 3, 0, :].rearrange("p (t q) -> p t q", t=TT), low, ACT.Copy, scale=-SCALE)
                    act.activation(q_pad[HEAD:P, i % 3, 1, :].rearrange("p (t q) -> p t q", t=TT), high, ACT.Copy, scale=-SCALE)\
                       .then_inc(acc_read_act, 1)
                elif kind in ("gate", "value"):
                    c = i if kind == "gate" else FT + i
                    dst = (conv_g if kind == "gate" else conv_v)[:, i % 2, :]
                    if i >= 2:
                        if kind == "gate":
                            act.wait_ge(prod_ready, i - 1)
                        else:
                            act.wait_ge(act_ready, i - 1)
                    act.activation(dst, bank[:, :], ACT.Identity, bias=conv_cols[:, 3, c:c + 1],
                                   scale=conv_cols[:, 2, c:c + 1]).then_inc(tap2_ready, 1)
                    if kind == "value":
                        wait_taken(act, group - 1)
                        act.activation(conv_g[:, i % 2, :], conv_g[:, i % 2, :], ACT.Silu).then_inc(silu_ready, 1)
                elif kind == "ple":
                    if i >= 2:
                        act.wait_ge(gated, i - 1)
                    act.activation(conv_g[:, i % 2, :], bank[:, :], ACT.Sigmoid).then_inc(acc_read_act, 1)
                    if i >= 1:
                        square_x(3 * KT + i - 1)

            def key_of(h):
                act.wait_ge(kin_arg, h + 1)
                part = b_kin[:, h // 2, (h % 2) * SEQ:(h % 2 + 1) * SEQ]
                act.activation(part, part, ACT.Exp, scale=-1.0).then_inc(kin_ready, 1)

            def decays(n):
                level, pair = n // 2, n % 2
                if n < 4:
                    act.wait_ge(g_ready, B_HEADS)
                    act.wait_ge(filled, 4)
                else:
                    act.wait_ge(sums_ready, 2 * (n - 3))
                    act.wait_ge(b_scored, 2 * (n - 1))
                s = 1 << (level - 1)
                to, back, ahead = halves(b_qk, pair, s), halves(b_bwd, pair, s)[0], halves(b_fwd, pair, s)[1]
                act.activation(to[0], back, ACT.Exp).then_inc(decay_ready, 1)
                act.activation(to[1], ahead, ACT.Exp).then_inc(decay_ready, 1)

            def b_square(pair):
                act.wait_ge(b_out, pair + 1)
                act.activation(scratch[:, pair, :], outs[pair][:, :], ACT.Square).then_inc(b_squared, 1)

            def load_bias(pair):
                act.dma_start(bias[:, pair % 2, :, :], bias_of(pair)).then_inc(bias_in[pair % 2], 16)

            def step_exp(n):
                keys = (n % TT + 1) * P
                act.wait_ge(logits, n + 1)
                act.activation(probs[:, n % 3, 0:keys], probs[:, n % 3, 0:keys], ACT.Exp, scale=-1.0,
                               bias=row_min[:, n:n + 1], accum_out=row_sum[:, n:n + 1]).then_inc(exped, 1)

            def step_keep(n):
                keys = (n % TT + 1) * P
                act.wait_ge(probs_turned, n + 1)
                if n >= 3:
                    act.wait_ge(weighted, n - 2)
                act.activation(probs_t[:, n % 3, 0:keys], turned[n % 2][:, 0:keys], ACT.Copy).then_inc(probs_t_ready, 1)

            def bias_of(pair):
                return bass.AP(tensor=bias_dram.tensor, offset=2 * pair * TABLE, ap=[[1, P], [TABLE, 2], [1, SEQ]])

            def mixers(slot):
                if slot == ROUND_SLOT - 1 or slot in range(ROUND_SLOT, B_OUT_SLOT):
                    for n in rounds_in(slot):
                        if 2 <= n + 1 < ROUNDS:
                            decays(n + 1)
                if slot == B_OUT_SLOT:
                    act.wait_ge(b_kept, 2 * ROUNDS)
                    act.wait_ge(table_out, 16)
                    load_bias(0)
                    load_bias(1)
                    b_square(0)
                    b_square(1)
                    rstd_of(1, score[0], HEAD)
                if slot == B_OUT_SLOT + 1:
                    act.wait_ge(b_normed, 1)
                    rstd_of(2, score[1], HEAD)
                for n in steps_in(slot):
                    if n % (2 * TT) == 0 and 2 * TT <= n < (PAIRS - 1) * 2 * TT:
                        act.wait_ge(logits, n)
                        load_bias(n // (2 * TT) + 1)
                    step_exp(n)
                    if n - 2 >= batch_start(n):
                        step_keep(n - 2)
                if slot == FLUSH_SLOT:
                    for n in (BATCH[0][1] - 2, BATCH[0][1] - 1):
                        step_keep(n)
                if slot == PROJ + 1:
                    for n in (STEPS - 2, STEPS - 1):
                        step_keep(n)

            act.wait_ge(vec_turned, 1)
            act.activation(vec_cols[:, :], banks[7][:, 0:4 * KT + 1], ACT.Copy, scale=-0.5).then_inc(vec_ready, 1)
            act.activation(conv_cols[:, :, :], banks[7][:, 64:64 + 8 * FT].rearrange("p (c b) -> p c b", c=4),
                           ACT.Copy).then_inc(vec_ready, 1)
            act.wait_ge(filled, 1)
            for f in range(KT):
                square_x(f)
            act.wait_ge(table_ready, 2)
            act.dma_start(bias_dram, table[:, :]).then_inc(table_out, 16)
            split_hi(0)
            rstd_of(0, score[0], D)
            split_h(0)

            for u in range(N_UNITS):
                beside = u == PROJ + 1
                if beside:
                    mixers(u)
                if u == UP:
                    take(GROUP_OF[u - 1])
                    rstd_of(3, score[0], D)
                    split_h(1)
                if u + 1 < N_UNITS:
                    split_hi(u + 1)
                if 2 <= u < 2 + B_HEADS:
                    key_of(u - 2)
                if u - 1 in GROUP_OF and u != UP and not PE_UNITS <= u < PG + 1:
                    take(GROUP_OF[u - 1])
                if u <= PROJ and not beside:
                    mixers(u)
                if u == DOWN + 10:
                    for c in range(2):
                        act.wait_ge(p_turned, 1)
                        act.activation(p_hi[:, c, :], turned[c][:, :], ACT.Copy).then_inc(p_hi_ready, 1)
                if u == PE_UNITS:
                    take(GROUP_OF[u - 1])
                if PE_UNITS <= u < PG:
                    for c in range(4):
                        f = 4 * (u - PE_UNITS) + c
                        if c < 3:
                            act.wait_ge(pe_done, 3 * (u - PE_UNITS) + c + 1)
                        else:
                            act.wait_ge(unit_done, u + 1)
                        act.activation(pe_out[:, f, :], banks[3 + f % 5][:, :], ACT.Copy).then_inc(pe_kept, 1)
                    if u == PE_UNITS:
                        rstd_of(4, score[0], D)
                    else:
                        split_h(2)
            take(GROUP_OF[N_UNITS - 1])
            square_x(4 * KT - 1)
            rstd_of(5, score[0], D)
            for f in range(KT):
                act.wait_ge(y_turned, f + 1)
                act.activation(y_rows[:, :, f * P:(f + 1) * P],
                               banks[4 + f % 3][:, :].rearrange("p (t c) -> p t c", t=TT), ACT.Copy).then_inc(y_kept, 1)

        @block.vector
        def _(dve):
            def split_lo(u):
                _, _, nk, _, ncol = UNITS[u]
                dve.wait_ge(whi_ready, u + 1)
                dve.tensor_tensor(w_lo[:, u % SPLIT, 0:nk * ncol], raw[:, u % RAW, 0:nk * ncol],
                                  w_hi[:, u % SPLIT, 0:nk * ncol].bitcast(F32), ALU.subtract).then_inc(wlo_ready, 1)

            def refine(index):
                dve.wait_ge(rstd_ready, index + 1)
                dve.tensor_tensor(sumsq[:, :], var[:, :], rstd[:, :], ALU.mult).then_inc(newton, 1)
                dve.wait_ge(newton, 3 * index + 1)
                dve.tensor_tensor(sumsq[:, :], sumsq[:, :], rstd[:, :], ALU.mult).then_inc(newton, 1)
                dve.wait_ge(newton, 3 * index + 2)
                dve.scalar_tensor_tensor(out=var[:, :], in0=sumsq[:, :], scalar=-3.0, in1=rstd[:, :],
                                         op0=ALU.add, op1=ALU.mult).then_inc(newton, 1)
                dve.wait_ge(newton, 3 * index + 3)

            def norm_x(stage, k, out, done):
                dve.scalar_tensor_tensor(out=out, in0=x_t[:, k, :], scalar=vec_cols[:, stage * KT + k:stage * KT + k + 1],
                                         in1=var[:, :], op0=ALU.mult, op1=ALU.mult).then_inc(done, 1)

            def make_h(stage):
                for k in range(KT + 1):
                    if k < KT:
                        if k >= 4:
                            if k % 2:
                                dve.wait_ge(h_lo_pool, stage * KT // 2 + (k - 4) // 2 + 1)
                            else:
                                dve.wait_ge(h_lo_dve, stage * KT // 2 + (k - 4) // 2 + 1)
                        norm_x(stage, k, scratch[:, k % 4, :], h_full)
                    if k % 2:
                        j = k - 1
                        dve.wait_ge(h_hi_ready, stage * KT + j + 1)
                        dve.tensor_tensor(h_lo[:, j, :], scratch[:, j % 4, :], h_hi[:, j, :].bitcast(F32), ALU.subtract)\
                           .then_inc(h_lo_dve, 1)

            def take(group):
                kind, i, unit = GROUPS[group]
                bank = acc[group % 2]
                if kind == "z":
                    part = slice((i % 2) * SEQ, (i % 2 + 1) * SEQ)
                    dve.wait_ge(z_chain, 3 * i + 3)
                    dve.scalar_tensor_tensor(out=b_kin[:, i // 2, part], in0=bank[:, :], scalar=0.0, in1=scratch[:, i, :],
                                             op0=ALU.max, op1=ALU.add).then_inc(kin_arg, 1)
                    dve.scalar_tensor_tensor(out=b_fwd[:, i // 2, part], in0=bank[:, :], scalar=0.0, in1=scratch[:, i, :],
                                             op0=ALU.min, op1=ALU.subtract).then_inc(acc_read_dve, 1)
                    wait_taken(dve, group)
                    dve.tensor_scalar(b_fwd[:, i // 2, part], b_fwd[:, i // 2, part], LOG_FLOOR, None, ALU.max)\
                       .then_inc(g_ready, 1)
                elif kind == "k":
                    dve.wait_ge(unit_done, unit + 1)
                    if i >= 3:
                        dve.wait_ge(scored, 2 * TT * (i - 2))
                    dve.tensor_copy(k_t[:, i % 3, :], bank[:, :]).then_inc(acc_read_dve, 1)
                elif kind == "x":
                    dve.wait_ge(unit_done, unit + 1)
                    dve.tensor_tensor(x_t[:, i % KT, :], bank[:, :], x_t[:, i % KT, :], ALU.add).then_inc(x_ready, 1)
                elif kind in ("gate", "value"):
                    c = i if kind == "gate" else FT + i
                    dst = (conv_g if kind == "gate" else conv_v)[:, i % 2, :]
                    n = 2 * i + (kind == "value")
                    dve.wait_ge(tap2_ready, n + 1)
                    dve.scalar_tensor_tensor(out=dst[:, 1:SEQ], in0=bank[:, 0:SEQ - 1], scalar=conv_cols[:, 1, c:c + 1],
                                             in1=dst[:, 1:SEQ], op0=ALU.mult, op1=ALU.add).then_inc(tap1_ready, 1)
                    dve.wait_ge(tap1_ready, n + 1)
                    dve.scalar_tensor_tensor(out=dst[:, 2:SEQ], in0=bank[:, 0:SEQ - 2], scalar=conv_cols[:, 0, c:c + 1],
                                             in1=dst[:, 2:SEQ], op0=ALU.mult, op1=ALU.add).then_inc(acc_read_dve, 1)

            def split_act(j):
                dve.wait_ge(prod_ready, j + 1)
                dve.tensor_copy(act_hi[:, j, :], conv_v[:, j % 2, :]).then_inc(act_hi_ready, 1)
                dve.wait_ge(act_hi_ready, j + 1)
                dve.tensor_tensor(act_lo[:, j, :], conv_v[:, j % 2, :], act_hi[:, j, :].bitcast(F32), ALU.subtract)\
                   .then_inc(act_ready, 1)

            def decayed(n):
                level, pair = n // 2, n % 2
                dve.wait_ge(decay_ready, 2 * (n - 1))
                s = 1 << (level - 1)
                to, q, k = halves(b_qk, pair, s), halves(b_q, pair, s)[1], halves(b_kin, pair, s)[0]
                dve.tensor_tensor(to[1], to[1], q, ALU.mult).then_inc(qk_ready, 1)
                dve.tensor_tensor(to[0], to[0], k, ALU.mult).then_inc(qk_ready, 1)

            def keep_scores(n):
                level, pair = n // 2, n % 2
                for hh in range(2):
                    use = 2 * n + hh
                    att, bank = b_att[:, 2 * pair + hh, :], score[hh]
                    dve.wait_ge(b_scored, use + 1)
                    if level <= MASKED_LEVELS:
                        if use >= 4:
                            dve.wait_ge(b_kept, use - 3)
                        else:
                            dve.wait_ge(masks_in, 16)
                            dve.wait_ge(table_out, 16)
                        mask = masks[:, level * P:(level + 1) * P].rearrange("p (o i) -> p o i", o=1).to_broadcast([P, TT, P])
                        to = att[:, 0:TT * P].rearrange("p (b i) -> p b i", b=TT)
                        new = bank[:, :].rearrange("p (b i) -> p b i", b=TT)
                        if level == 0:
                            ins = dve.tensor_tensor(to, new, mask, ALU.mult)
                        else:
                            ins = dve.copy_predicated(to, mask, new)
                    elif level == MASKED_LEVELS + 1:
                        ins = dve.tensor_copy(att[:, 4 * P:6 * P], bank[:, 0:2 * P])
                    else:
                        ins = dve.tensor_copy(att[:, 6 * P:10 * P], bank[:, :])
                    ins.then_inc(b_kept, 1)

            def b_mix(pair):
                t = scratch[:, 2 + pair, :]
                dve.scalar_tensor_tensor(out=t, in0=outs[pair][:, :], scalar=vec_cols[:, 4 * KT:4 * KT + 1], in1=var[:, :],
                                         op0=ALU.mult, op1=ALU.mult).then_inc(b_normed, 1)
                dve.wait_ge(b_normed, pair + 1)
                dve.tensor_tensor(t, t, b_gate[:, pair, :], ALU.mult).then_inc(b_gated, 1)
                dve.wait_ge(b_gated, pair + 1)
                dve.tensor_copy(mix_b_hi[:, pair, :], t).then_inc(b_hi_ready, 1)
                dve.wait_ge(b_hi_ready, pair + 1)
                dve.tensor_tensor(mix_b_lo[:, pair, :], t, mix_b_hi[:, pair, :].bitcast(F32), ALU.subtract).then_inc(b_mixed, 1)

            def keep_values(unit):
                g = V_UNITS.index(unit)
                dve.wait_ge(v_turned, g + 1)
                if g >= 5:
                    dve.wait_ge(weighted, 2 * TT * (g - 4))
                to = b_v[:, g, :, :] if g < 2 else v_tok[:, (g - 2) % 3, :, :]
                dve.tensor_copy(to, turned[0][:, :].rearrange("p (t c) -> p t c", t=TT)).then_inc(v_ready, 1)

            def step_logits(n):
                head, i = n // TT, n % TT
                pair, keys = head // 2, (i + 1) * P
                if n % (2 * TT) == 0:
                    dve.wait_ge(bias_in[pair % 2], 16 * (pair // 2 + 1))
                dve.wait_ge(scored, n + 1)
                if n >= 3:
                    dve.wait_ge(probs_turned, n - 2)
                dve.tensor_tensor_reduce(out=probs[:, n % 3, 0:keys], in0=score[n % 2][:, 0:keys],
                                         in1=bias[:, pair % 2, head % 2, SEQ - keys:SEQ], scale=1.0, scalar=3.0e38,
                                         op0=ALU.add, op1=ALU.min, accum_out=row_min[:, n:n + 1]).then_inc(logits, 1)

            def step_invert(n):
                dve.wait_ge(exped, n + 1)
                dve.reciprocal(row_inv[:, n:n + 1], row_sum[:, n:n + 1]).then_inc(inverted, 1)

            def keep_mixed(pair):
                dve.wait_ge(weighted, 2 * TT * (pair + 1))
                dve.tensor_copy(mix_a_hi[:, pair, :], outs[pair % 2][:, :]).then_inc(mix_hi_ready, 1)
                dve.wait_ge(mix_hi_ready, pair + 1)
                dve.tensor_tensor(mix_a_lo[:, pair, :], outs[pair % 2][:, :], mix_a_hi[:, pair, :].bitcast(F32), ALU.subtract)\
                   .then_inc(mix_ready, 1)

            def mixers(slot):
                for n in rounds_in(slot):
                    if 2 <= n + 1 < ROUNDS:
                        decayed(n + 1)
                    keep_scores(n)
                if slot == B_OUT_SLOT + 1:
                    for pair in range(2):
                        refine(1 + pair)
                        b_mix(pair)
                v_here = slot - 1 in V_UNITS
                for i, n in enumerate(steps_in(slot)):
                    step_logits(n)
                    if n - 1 >= batch_start(n):
                        step_invert(n - 1)
                    if n - 3 >= batch_start(n) and (n - 3) % (2 * TT) == 2 * TT - 1:
                        keep_mixed((n - 3) // (2 * TT))
                    if i == 0 and v_here:
                        keep_values(slot - 1)
                if v_here and not steps_in(slot):
                    keep_values(slot - 1)
                if slot == FLUSH_SLOT:
                    step_invert(BATCH[0][1] - 1)
                    keep_mixed(PAIRS - 2)
                if slot == PROJ + 1:
                    step_invert(STEPS - 1)
                    keep_mixed(PAIRS - 1)

            dve.wait_ge(table_in, 16 * 3)
            dve.wait_ge(table_sum, 1)
            dve.scalar_tensor_tensor(out=table[:, 0:512], in0=banks[6][0:HEADS, :], scalar=-1.0, in1=extra[:, 0:512],
                                     op0=ALU.mult, op1=ALU.subtract).then_inc(table_ready, 1)
            dve.scalar_tensor_tensor(out=table[:, 512:TABLE], in0=banks[5][0:HEADS, 0:TABLE - 512], scalar=-1.0,
                                     in1=extra[:, 512:TABLE], op0=ALU.mult, op1=ALU.subtract).then_inc(table_ready, 1)
            for f in range(KT):
                dve.wait_ge(x_turned, f + 1)
                dve.tensor_copy(x_t[:, f, :], banks[2 + f % 3][:, :]).then_inc(x_ready, 1)
            split_lo(0)
            dve.wait_ge(vec_ready, 2)
            refine(0)
            make_h(0)

            for u in range(N_UNITS):
                beside = u == PROJ + 1
                if beside:
                    mixers(u)
                if u == UP:
                    take(GROUP_OF[u - 1])
                    refine(3)
                    make_h(1)
                if u + 1 < N_UNITS:
                    split_lo(u + 1)
                if u - 1 in GROUP_OF and u not in (UP, PE_UNITS, PG) and GROUPS[GROUP_OF[u - 1]][0] in ("z", "k", "x", "gate", "value"):
                    take(GROUP_OF[u - 1])
                if UP < u <= DOWN + 1 and (u - UP) % 2 == 1 and u > UP + 1:
                    split_act((u - UP) // 2 - 1)
                if u <= PROJ and not beside:
                    mixers(u)
                if u == DOWN + 10:
                    for c in range(2):
                        dve.wait_ge(p_hi_ready, c + 1)
                        dve.tensor_tensor(p_lo[:, c, :], turned[c][:, :], p_hi[:, c, :].bitcast(F32), ALU.subtract).then_inc(p_ready, 1)
                if u == PE_UNITS:
                    take(GROUP_OF[u - 1])
                    refine(4)
                if u == PE_UNITS + 1:
                    make_h(2)
                if u > PG:
                    add_gated(dve, u - 1 - PG, x_t, conv_v, gated, x_ready)
            add_gated(dve, KT - 1, x_t, conv_v, gated, x_ready)
            refine(5)
            for f in range(KT):
                if f >= 4:
                    dve.wait_ge(y_turned, f - 3)
                norm_x(3, f, scratch[:, f % 4, :], y_full)

        @block.gpsimd
        def _(pool):
            pool.memset(eps_col[:, :], EPS).then_inc(filled, 1)
            pool.wait_ge(filled, 1)
            pool.memset(q_pad[0:HEAD, :, 1, :], 0.0).then_inc(filled, 1)
            pool.wait_ge(filled, 2)
            pool.memset(q_pad[HEAD:P, :, 0, :], 0.0).then_inc(filled, 1)
            pool.wait_ge(filled, 3)
            pool.memset(b_bwd[:, :, :], 0.0).then_inc(filled, 1)
            pool.wait_ge(filled, 4)

            def add_squares(n):
                pool.wait_ge(sq_ready, n + 1)
                if n % KT == 0:
                    if n:
                        pool.wait_ge(newton, 3 * (n // KT + 2))
                    pool.tensor_scalar(sumsq[:, :], scratch[:, n % 2, :], 1.0, None, ALU.mult).then_inc(sumsq_ready, 1)
                else:
                    pool.wait_ge(sumsq_ready, n)
                    pool.tensor_tensor(sumsq[:, :], sumsq[:, :], scratch[:, n % 2, :], ALU.add).then_inc(sumsq_ready, 1)

            def split_odd(stage):
                for k in range(1, KT, 2):
                    pool.wait_ge(h_hi_ready, stage * KT + k + 1)
                    pool.tensor_tensor(h_lo[:, k, :], scratch[:, k % 4, :], h_hi[:, k, :].bitcast(F32), ALU.subtract)\
                        .then_inc(h_lo_pool, 1)

            for f in range(KT):
                add_squares(f)
            split_odd(0)
            for n in range(2, ROUNDS - 2):
                level, pair = n // 2, n % 2
                s = 1 << (level - 1)
                (fwd1, fwd2), back = halves(b_fwd, pair, s), halves(b_bwd, pair, s)[0]
                like = [P, SEQ // s, s]
                pool.wait_ge(decay_ready, 2 * (n - 1))
                pool.tensor_tensor(back, back, fwd2[:, :, s - 1:s].to_broadcast(like), ALU.add).then_inc(sums_ready, 1)
                pool.wait_ge(sums_ready, 2 * (n - 2) + 1)
                pool.tensor_tensor(fwd2, fwd2, fwd1[:, :, s - 1:s].to_broadcast(like), ALU.add).then_inc(sums_ready, 1)
            for n in range(STEPS):
                keys = (n % TT + 1) * P
                pool.wait_ge(inverted, n + 1)
                pool.tensor_scalar(probs[:, n % 3, 0:keys], probs[:, n % 3, 0:keys], row_inv[:, n:n + 1], None, ALU.mult)\
                    .then_inc(normed, 1)
            for f in range(KT):
                add_squares(KT + f)
            split_odd(1)
            for j in range(FT):
                pool.wait_ge(silu_ready, j + 1)
                wait_taken(pool, GROUP_AT["value", j])
                pool.tensor_tensor(conv_v[:, j % 2, :], conv_g[:, j % 2, :], conv_v[:, j % 2, :], ALU.mult).then_inc(prod_ready, 1)
            for f in range(KT):
                add_squares(2 * KT + f)
            split_odd(2)
            for f in range(KT):
                wait_taken(pool, GROUP_AT["ple", f])
                pool.wait_ge(pe_kept, f + 1)
                if f >= 2:
                    pool.wait_ge(x_ready, 3 * KT + f - 1)
                pool.tensor_tensor(conv_v[:, f % 2, :], conv_g[:, f % 2, :], pe_out[:, f, :], ALU.mult).then_inc(gated, 1)
                if f:
                    add_squares(3 * KT + f - 1)
            add_squares(4 * KT - 1)


def add_gated(dve, f, x_t, conv_v, gated, x_ready):
    dve.wait_ge(gated, f + 1)
    dve.tensor_tensor(x_t[:, f, :], x_t[:, f, :], conv_v[:, f % 2, :], ALU.add).then_inc(x_ready, 1)


_INS = ["x", "p", "rel_bias", "norm_mix", "w_in", "w_out", "hgrn_gnorm", "norm_ffn", "w_up", "conv_w", "conv_b",
        "w_down", "norm_ple", "w_pe", "w_pg", "norm_final"]


def kernel(**inputs):
    import concourse.bacc as _bacc
    from concourse.bass_utils import run_bass_kernel_spmd as _run

    nc = _bacc.Bacc("TRN2", target_bir_lowering=False, num_devices=1)
    arrays = {f"in_{name}": np.ascontiguousarray(inputs[name]) for name in _INS}
    arrays.update({f"in_{name}": c for name, c in shape_constants().items()})
    aps = {name[3:]: nc.dram_tensor(name, v.shape, mybir.dt.from_np(v.dtype), kind="ExternalInput").ap()
           for name, v in arrays.items()}
    out = nc.dram_tensor("out", (1, SEQ, D), F32, kind="ExternalOutput").ap()
    build(nc, aps, out)
    return _run(nc, [arrays], core_ids=[0]).results[0]["out"]
```

```python
from contextlib import ExitStack

import numpy as np

import concourse.bass as bass
from concourse import mybir

ALU = mybir.AluOpType
ACT = mybir.ActivationFunctionType
F32 = mybir.dt.float32
F32R = mybir.dt.float32r
I32 = mybir.dt.int32

P = 128
SEQ = 512
D = 1024
KT = D // P
TT = SEQ // P
HEAD = 64
FF = 2816
FT = FF // P
PLE = 256
EPS = 1e-6
N_BUCKETS = 32
MAX_DISTANCE = 2048
HEADS = 12
PAIRS = HEADS // 2
B_HEADS = 4
LEVELS = 9
MASKED_LEVELS = 7
TABLE = SEQ + P
LOG_FLOOR = float(np.log(1e-30))
SCALE = HEAD ** -0.5
NEG_BIG = -1e30

A_Q, A_K, A_V, B_Q, B_Z, B_I, B_G, C_Q, C_K, C_V = 0, 3, 6, 9, 13, 17, 19, 21, 24, 27

UNITS = []
GROUPS = []


def _unit(matrix, k0, nk, c0, nc=P):
    UNITS.append((matrix, k0, nk, c0, nc))


def _group(kind, index):
    GROUPS.append((kind, index, len(UNITS) - 1))


for _h in range(B_HEADS):
    _unit("w_in", 0, KT, (B_Z + _h) * P)
    _group("z", _h)
for _b in range(2):
    _unit("w_in", 0, KT, (B_G + _b) * P)
    _group("g", _b)
for _h in range(B_HEADS):
    _unit("w_in", 0, KT, (B_Q + _h) * P)
    _group("bq", _h)
for _b in range(2):
    _unit("w_in", 0, KT, (B_I + _b) * P)
    _group("v", _b)
for _p in range(PAIRS):
    for _kind, _a, _c in (("q", A_Q, C_Q), ("k", A_K, C_K), ("v", A_V, C_V)):
        _unit("w_in", 0, KT, ((_a + _p) if _p < 3 else (_c + _p - 3)) * P)
        _group(_kind, _p + 2 if _kind == "v" else _p)
PROJ = len(UNITS)
for _f in range(KT):
    _unit("w_out", 0, KT, _f * P)
    _group("x", KT + _f)
UP = len(UNITS)
for _j in range(FT):
    _unit("w_up", 0, KT, _j * P)
    _group("gate", _j)
    _unit("w_up", 0, KT, FF + _j * P)
    _group("value", _j)
DOWN = len(UNITS)
for _f in range(KT):
    for _k0 in range(0, FT, KT):
        _unit("w_down", _k0, min(KT, FT - _k0), _f * P)
    _group("x", 2 * KT + _f)
PE_UNITS = len(UNITS)
for _c in range(2):
    _unit("w_pe", 0, PLE // P, _c * 512, 512)
PG = len(UNITS)
for _f in range(KT):
    _unit("w_pg", 0, KT, _f * P)
    _group("ple", _f)
N_UNITS = len(UNITS)

RAW = 3
SPLIT = 3
TURN_LAG, VALUE_LAG = 3, 4

V_UNITS = [g[2] for g in GROUPS if g[0] == "v"]
ROUND_SLOT = 10
ROUNDS = 2 * (LEVELS + 1)


def rounds_in(slot):
    return [n for n in range(ROUNDS) if ROUND_SLOT + n * 2 // 5 == slot]


B_OUT_SLOT = ROUND_SLOT + ROUNDS * 2 // 5
HEAD_SLOTS = [B_OUT_SLOT + 1 + h for h in range(10)] + [30, 31]
FLUSH_SLOT = 29
STEPS = HEADS * TT
BATCH = [(0, 40), (40, 48)]
STEP_AT = {PROJ: (0, 1, 3, 4), PROJ + 1: (0, 1, 2, 3)}


def steps_in(slot):
    return [TT * HEAD_SLOTS.index(slot) + i for i in range(TT)] if slot in HEAD_SLOTS else []


def tile_of(n):
    return TT - 1 - n % TT


def batch_start(n):
    return 0 if n < BATCH[0][1] else BATCH[1][0]


def rel_bucket(d):
    exact = N_BUCKETS // 2
    d = max(d, 0)
    if d < exact:
        return d
    return min(N_BUCKETS - 1, exact + int(np.log(d / exact) / np.log(MAX_DISTANCE / exact) * (N_BUCKETS - exact)))


def shape_constants():
    square = np.concatenate([np.eye(P), np.ones((P, P)), np.kron(np.eye(2), np.ones((HEAD, HEAD))), np.eye(P)[::-1]], 1)
    onehot = np.zeros((N_BUCKETS, TABLE))
    extra = np.full((HEADS, TABLE), NEG_BIG)
    for j in range(TABLE):
        d = SEQ - 1 - j
        onehot[rel_bucket(d), j] = 1
        if d >= 0:
            seen = (d <= 128) + (d % 4 == 0) + (d % 16 == 0)
            if seen:
                extra[:6, j] = np.log(seen)
            extra[6:, j] = 0
    j, i = np.arange(P)[:, None], np.arange(P)[None, :]
    masks = [j == i]
    for level in range(MASKED_LEVELS):
        s = 1 << level
        masks.append((j // (2 * s) == i // (2 * s)) & (j % (2 * s) < s) & (i % (2 * s) >= s))
    return {
        "c_square": square.astype(np.float32),
        "c_onehot": onehot.astype(np.float32),
        "c_extra": extra.astype(np.float32),
        "c_masks": np.concatenate(masks, 1).astype(np.int32),
    }


def build(nc, a, out):
    bias_dram = nc.dram_tensor("bias_table", [HEADS, TABLE], F32, kind="Internal").ap()
    with ExitStack() as ctx:
        def sb(name, shape, dt=F32, stack=ctx):
            return stack.enter_context(nc.sbuf_tensor(name, shape, dt))

        def sem(name):
            return ctx.enter_context(nc.semaphore(name))

        x_t = sb("x_t", [P, KT, SEQ])
        h_hi = sb("h_hi", [P, KT, SEQ], F32R)
        h_lo = sb("h_lo", [P, KT, SEQ], F32R)
        raw = sb("raw", [P, RAW, 1024])
        w_hi = sb("w_hi", [P, SPLIT, 1024], F32R)
        w_lo = sb("w_lo", [P, SPLIT, 1024], F32R)
        square = sb("square", [P, 4 * P])
        ident, ones, half_ones, flip = (square[:, i * P:(i + 1) * P] for i in range(4))
        vec_cols = sb("vec_cols", [P, 4 * KT + 1])
        conv_cols = sb("conv_cols", [P, 4, 2 * FT])
        eps_col = sb("eps_col", [P, 1])
        sumsq = sb("sumsq", [P, SEQ])
        scratch = sb("scratch", [P, 4, SEQ])
        r_row = sb("r_row", [P, SEQ])
        stat = sb("stat", [P, 4, TT])
        stat_bits = sb("stat_bits", [P, 2, TT], I32)

        mixing = ExitStack()
        mix_b_hi = sb("mix_b_hi", [P, 2, SEQ], F32R, mixing)
        mix_b_lo = sb("mix_b_lo", [P, 2, SEQ], F32R, mixing)
        q_pad = sb("q_pad", [P, 3, 2, SEQ], F32, mixing)
        k_t = sb("k_t", [P, 3, SEQ], F32, mixing)
        v_tok = sb("v_tok", [P, 3, TT, P], F32, mixing)
        v_t = sb("v_t", [P, SEQ], F32, mixing)
        hgrn = ExitStack()
        b_fwd = sb("b_fwd", [P, 2, 1024], F32, hgrn)
        b_kin = sb("b_kin", [P, 2, 1024], F32, hgrn)
        b_q = sb("b_q", [P, 2, 1024], F32, hgrn)
        b_bwd = sb("b_bwd", [P, 2, 1024], F32, hgrn)
        b_qk = sb("b_qk", [P, 2, 1024], F32, hgrn)
        b_att = sb("b_att", [P, B_HEADS, 10 * P], F32, hgrn)
        b_v = sb("b_v", [P, 2, TT, P], F32, hgrn)
        b_gate = sb("b_gate", [P, 2, SEQ], F32, hgrn)
        masks = sb("masks", [P, 8 * P], I32, hgrn)
        hgrn.close()
        bias = sb("bias", [P, 2, 2, SEQ], F32, mixing)
        probs = sb("probs", [P, 4, SEQ], F32, mixing)
        probs_t = sb("probs_t", [P, 4, SEQ], F32, mixing)
        mix_a_hi = sb("mix_a_hi", [P, PAIRS, SEQ], F32R, mixing)
        mix_a_lo = sb("mix_a_lo", [P, PAIRS, SEQ], F32R, mixing)
        row_sum = sb("row_sum", [P, STEPS], F32, mixing)
        row_min = sb("row_min", [P, STEPS], F32, mixing)
        row_inv = sb("row_inv", [P, STEPS], F32, mixing)
        mixing.close()
        setup = ExitStack()
        sb("under_setup", [P, 66 * 1024 // 4], F32, setup)
        x_rows = sb("x_rows", [P, TT, D], F32, setup)
        vec_rows = sb("vec_rows", [4 * KT + 1, P], F32, setup)
        conv_rows = sb("conv_rows", [2 * FT, 4, P], F32, setup)
        rel_t = sb("rel_t", [N_BUCKETS, HEADS], F32, setup)
        onehot = sb("onehot", [N_BUCKETS, TABLE], F32, setup)
        extra = sb("extra", [HEADS, TABLE], F32, setup)
        table = sb("table", [HEADS, TABLE], F32, setup)
        setup.close()
        conv_g = sb("conv_g", [P, 3, SEQ])
        conv_v = sb("conv_v", [P, 3, SEQ])
        p_hi = sb("p_hi", [P, 2, SEQ], F32R)
        p_lo = sb("p_lo", [P, 2, SEQ], F32R)
        mlp = ExitStack()
        act_hi = sb("act_hi", [P, FT, SEQ], F32R, mlp)
        act_lo = sb("act_lo", [P, FT, SEQ], F32R, mlp)
        mlp.close()
        pe_out = sb("pe_out", [P, KT, SEQ])
        y_rows = sb("y_rows", [P, TT, D])
        gain_row = sb("gain_row", [P, D])
        p_rows = conv_g[:, 0:2, :].rearrange("p a n -> p (a n)").rearrange("p (t c) -> p t c", t=TT)

        banks = [ctx.enter_context(nc.psum_tensor(f"bank{i}", [P, 512], F32)) for i in range(8)]
        acc, score, turned, outs = banks[0:2], banks[2:4], banks[4:6], banks[6:8]
        PE_BANK = (2, 3, 6, 7)

        raw_full = [sem(f"raw_full{i}") for i in range(RAW)]
        whi_ready, wlo_ready, unit_done = sem("whi_ready"), sem("wlo_ready"), sem("unit_done")
        acc_taken = sem("acc_taken")
        square_in, masks_in, vec_in, table_in = (sem(s) for s in ("square_in", "masks_in", "vec_in", "table_in"))
        x_in = [sem(f"x_in{t}") for t in range(TT)]
        filled = sem("filled")
        vec_turned, vec_ready, x_kept = sem("vec_turned"), sem("vec_ready"), sem("x_kept")
        table_sum, table_ready, table_out = sem("table_sum"), sem("table_ready"), sem("table_out")
        x_turned, x_ready, sq_ready, sumsq_ready = (sem(s) for s in ("x_turned", "x_ready", "sq_ready", "sumsq_ready"))
        h_hi_ready, h_lo_ready = sem("h_hi_ready"), sem("h_lo_ready")
        rows_squared, tokens_summed, newton, diag_ready, row_spread, r_ready = (
            sem(s) for s in ("rows_squared", "tokens_summed", "newton", "diag_ready", "row_spread", "r_ready"))
        v_turned, v_ready = sem("v_turned"), sem("v_ready")
        z_chain, kin_arg, log_f, g_ready, kin_ready = (sem(s) for s in ("z_chain", "kin_arg", "log_f", "g_ready", "kin_ready"))
        gate_ready, bq_ready = sem("gate_ready"), sem("bq_ready")
        decay_ready, qk_ready, sums_ready = sem("decay_ready"), sem("qk_ready"), sem("sums_ready")
        b_scored, b_kept, b_out, b_squared = (sem(s) for s in ("b_scored", "b_kept", "b_out", "b_squared"))
        b_summed, b_var, b_ln, b_rstd, b_newton = (sem(s) for s in ("b_summed", "b_var", "b_ln", "b_rstd", "b_newton"))
        b_normed, b_gated, b_hi_ready, b_mixed = (sem(s) for s in ("b_normed", "b_gated", "b_hi_ready", "b_mixed"))
        bias_in = [sem("bias_in0"), sem("bias_in1")]
        scored, logits, exped, inverted, normed = (sem(s) for s in ("scored", "logits", "exped", "inverted", "normed"))
        probs_turned, probs_t_ready, weighted = (sem(s) for s in ("probs_turned", "probs_t_ready", "weighted"))
        mix_hi_ready, mix_ready = sem("mix_hi_ready"), sem("mix_ready")
        tap2_ready, tap1_ready, tap0_ready, silu_ready, prod_ready = (
            sem(s) for s in ("tap2_ready", "tap1_ready", "tap0_ready", "silu_ready", "prod_ready"))
        act_hi_ready, act_ready = sem("act_hi_ready"), sem("act_ready")
        p_in, p_turned, p_hi_ready, p_ready = (sem(s) for s in ("p_in", "p_turned", "p_hi_ready", "p_ready"))
        pe_done, pe_kept, sig_ready, gated = sem("pe_done"), sem("pe_kept"), sem("sig_ready"), sem("gated")
        gain_in, y_turned, y_kept, y_dve, y_act, stored = (
            sem(s) for s in ("gain_in", "y_turned", "y_kept", "y_dve", "y_act", "stored"))

        block = ctx.enter_context(nc.Block())
        GROUP_OF = {g[2]: i for i, g in enumerate(GROUPS)}
        GROUP_AT = {(g[0], g[1]): i for i, g in enumerate(GROUPS)}

        def wait_taken(eng, group):
            kind, index, _ = GROUPS[group]
            if kind == "x":
                eng.wait_ge(x_ready, index - KT + 1)
            else:
                eng.wait_ge(acc_taken, sum(g[0] != "x" for g in GROUPS[:group + 1]))

        def halves(tile, pair, s):
            v = tile[:, pair, :].rearrange("p (b t) -> p b t", t=2 * s)
            return v[:, :, 0:s], v[:, :, s:2 * s]

        ATT_AT = {(b, b): b for b in range(TT)}
        ATT_AT.update({(0, 1): 4, (2, 3): 5, (0, 2): 6, (0, 3): 7, (1, 2): 8, (1, 3): 9})

        def turned_before(n):
            m = n + TURN_LAG
            if m >= BATCH[-1][1] or batch_start(m) != batch_start(n):
                return sum(u + 1 <= (FLUSH_SLOT if n < BATCH[0][1] else PROJ + 1) for u in V_UNITS)
            at, i = HEAD_SLOTS[m // TT], m % TT
            k = STEP_AT.get(at, (1, 3, 5, 7))[i]
            return sum(u + 1 < at or (u + 1 == at and k > 2) for u in V_UNITS)

        w_dram = {name: a[name][0] for name in ("w_in", "w_out", "w_up", "w_down", "w_pe", "w_pg")}

        @block.sync
        def _(sp):
            def load_unit(u):
                name, k0, nk, c0, ncol = UNITS[u]
                if u >= RAW:
                    sp.wait_ge(wlo_ready, u - RAW + 1)
                src = w_dram[name][k0 * P:(k0 + nk) * P, c0:c0 + ncol].rearrange("(k p) c -> p k c", p=P)
                dst = raw[:, u % RAW, 0:nk * ncol].rearrange("p (k c) -> p k c", c=ncol)
                sp.dma_start(dst, src).then_inc(raw_full[u % RAW], 16)

            sp.dma_start(square[:, :], a["c_square"]).then_inc(square_in, 16)
            for t in range(TT):
                sp.dma_start(x_rows[:, t, :], a["x"][0, t * P:(t + 1) * P, :]).then_inc(x_in[t], 16)
                if t == 1:
                    load_unit(0)
            for u in range(1, N_UNITS):
                load_unit(u)
                if u == DOWN + RAW:
                    sp.wait_ge(prod_ready, FT)
                    sp.dma_start(p_rows, a["p"][0, 0].rearrange("(t p) c -> p t c", p=P)).then_inc(p_in, 16)
                if u == PG + RAW:
                    sp.wait_ge(unit_done, PE_UNITS)
                    sp.dma_start(gain_row[:, :], a["norm_final"].rearrange("(o d) -> o d", o=1).to_broadcast([P, D]))\
                      .then_inc(gain_in, 16)
            for t in range(TT):
                if t < TT - 1:
                    sp.wait_ge(y_dve, t + 1)
                else:
                    sp.wait_ge(y_act, 1)
                sp.dma_start(out[0, t * P:(t + 1) * P, :], y_rows[:, t, :]).then_inc(stored, 16)
            sp.wait_ge(stored, 16 * TT)

        @block.tensor
        def _(pe):
            def products(bank, slot, k, nc_cols, c, x_hi, x_lo, first, last):
                at = k * nc_cols + c
                hi, lo = w_hi[:, slot, at:at + P], w_lo[:, slot, at:at + P]
                pe.matmul(bank[:, :], hi, x_hi, start=first, stop=False)
                pe.matmul(bank[:, :], hi, x_lo, start=False, stop=False)
                return pe.matmul(bank[:, :], lo, x_hi, start=False, stop=last)

            def wait_h(stage, k):
                pe.wait_ge(h_lo_ready, stage * KT + k + 1)

            def begin_unit(u, group):
                pe.wait_ge(wlo_ready, u + 1)
                if group >= 2:
                    wait_taken(pe, group - 2)

            def sum_tokens(stage):
                pe.wait_ge(sumsq_ready, (KT - 1) * stage)
                pe.wait_ge(sq_ready, KT * stage)
                for t in range(TT):
                    cols = slice(t * P, (t + 1) * P)
                    pe.matmul(turned[0][:, t:t + 1], sumsq[:, cols], ones[:, 0:1], start=True, stop=False)
                    mm = pe.matmul(turned[0][:, t:t + 1], scratch[:, 3, cols], ones[:, 0:1], start=False, stop=True)
                mm.then_inc(tokens_summed, 1)

            def spread_row(stage):
                pe.wait_ge(diag_ready, stage + 1)
                pe.matmul(turned[1][:, :], ones, scratch[:, 0, :], start=True, stop=True).then_inc(row_spread, 1)

            def b_round(n):
                level, pair = n // 2, n % 2
                if n < 2:
                    pe.wait_ge(bq_ready, B_HEADS)
                    pe.wait_ge(kin_ready, B_HEADS)
                else:
                    pe.wait_ge(qk_ready, 2 * (n - 1))
                for hh in range(2):
                    use = 2 * n + hh
                    if use >= 2:
                        pe.wait_ge(b_kept, use - 1)
                    bank, at = score[hh], hh * SEQ
                    keys, queries = (b_kin, b_q) if level == 0 else (b_qk, b_qk)
                    if level <= MASKED_LEVELS:
                        parts = [(b, b, 1, b) for b in range(TT)]
                    elif level == MASKED_LEVELS + 1:
                        parts = [(0, 1, 1, 0), (2, 3, 1, 1)]
                    else:
                        parts = [(0, 2, 2, 0), (1, 2, 2, 2)]
                    for jb, ib, nb, to in parts:
                        mm = pe.matmul(bank[:, to * P:(to + nb) * P],
                                       keys[:, pair, at + jb * P:at + (jb + 1) * P],
                                       queries[:, pair, at + ib * P:at + (ib + nb) * P],
                                       start=True, stop=True)
                    mm.then_inc(b_scored, 1)

            def b_values(pair):
                pe.wait_ge(b_kept, 2 * ROUNDS)
                pe.wait_ge(v_ready, pair + 1)
                for hh in range(2):
                    rows = slice(hh * HEAD, (hh + 1) * HEAD)
                    for ib in range(TT):
                        for jb in range(ib + 1):
                            at = ATT_AT[jb, ib] * P
                            mm = pe.matmul(outs[pair][rows, ib * P:(ib + 1) * P], b_v[:, pair, jb, rows],
                                           b_att[:, 2 * pair + hh, at:at + P], start=(jb == 0), stop=(jb == ib))
                mm.then_inc(b_out, 1)

            def b_norm_sum(pair):
                pe.wait_ge(b_squared, pair + 1)
                pe.wait_ge(v_ready, sum(u + 1 <= B_OUT_SLOT for u in V_UNITS))
                pe.matmul(turned[1 - pair][:, :], half_ones, scratch[:, pair, :], start=True, stop=True)\
                  .then_inc(b_summed, 1)

            def turn_values(unit):
                g = V_UNITS.index(unit)
                wait_taken(pe, GROUP_OF[unit])
                steps = TT * sum(s < unit + 1 for s in HEAD_SLOTS)
                if unit + 1 in HEAD_SLOTS:
                    steps += sum(k <= 2 for k in STEP_AT.get(unit + 1, (1, 3, 5, 7)))
                first = batch_start(steps - 1)
                turned_so_far = steps if steps == first else max(steps - TURN_LAG, first)
                if steps and turned_so_far:
                    pe.wait_ge(probs_t_ready, turned_so_far)
                elif unit + 1 > B_OUT_SLOT:
                    pe.wait_ge(b_var, 2)
                if g:
                    pe.wait_ge(v_ready, g)
                for t in range(TT):
                    mm = pe.transpose(turned[0][:, t * P:(t + 1) * P], v_t[:, t * P:(t + 1) * P], ident)
                mm.then_inc(v_turned, 1)

            def step_score(n):
                head, i = n // TT, tile_of(n)
                pair = head // 2
                if n % (2 * TT) == 0:
                    wait_taken(pe, GROUP_AT["q", pair])
                    wait_taken(pe, GROUP_AT["k", pair])
                if n >= 2:
                    pe.wait_ge(logits, n - 1)
                keys = (i + 1) * P
                pe.matmul(score[n % 2][:, 0:keys], q_pad[:, pair % 3, head % 2, i * P:(i + 1) * P],
                          k_t[:, pair % 3, 0:keys], start=True, stop=True).then_inc(scored, 1)

            def step_turn(n):
                pe.wait_ge(normed, n + 1)
                if n >= 2:
                    pe.wait_ge(probs_t_ready, n - 1)
                else:
                    pe.wait_ge(b_var, 2)
                if turned_before(n):
                    pe.wait_ge(v_ready, turned_before(n))
                for b in range(tile_of(n) + 1):
                    mm = pe.transpose(turned[n % 2][:, b * P:(b + 1) * P], probs[:, n % 4, b * P:(b + 1) * P], flip)
                mm.then_inc(probs_turned, 1)

            def step_values(n):
                head, i = n // TT, tile_of(n)
                pair, rows = head // 2, slice((head % 2) * HEAD, (head % 2 + 1) * HEAD)
                pe.wait_ge(probs_t_ready, n + 1)
                if n % (2 * TT) == 0:
                    pe.wait_ge(v_ready, 2 + pair + 1)
                    if pair < 2:
                        pe.wait_ge(b_normed, pair + 1)
                    else:
                        pe.wait_ge(mix_ready, pair - 1)
                for jb in range(i + 1):
                    mm = pe.matmul(outs[pair % 2][rows, i * P:(i + 1) * P], v_tok[:, pair % 3, jb, rows],
                                   probs_t[:, n % 4, jb * P:(jb + 1) * P], start=(jb == 0), stop=(jb == i))
                mm.then_inc(weighted, 1)

            def step(n):
                first = batch_start(n)
                if n - TURN_LAG >= first:
                    step_turn(n - TURN_LAG)
                if n - VALUE_LAG >= first:
                    step_values(n - VALUE_LAG)
                step_score(n)

            def flush(last):
                for n in range(last + 1 - TURN_LAG, last + 1):
                    step_turn(n)
                    step_values(n - 1)
                step_values(last)

            def mixers(slot, k):
                for at, n in zip((1, 4, 6), rounds_in(slot)):
                    if k == at:
                        b_round(n)
                if slot == B_OUT_SLOT:
                    if k == 1:
                        b_values(0)
                    if k == 4:
                        b_values(1)
                if slot == B_OUT_SLOT + 1 and k == 2:
                    b_norm_sum(0)
                if slot == B_OUT_SLOT + 1 and k == 4:
                    b_norm_sum(1)
                for at, n in zip(STEP_AT.get(slot, (1, 3, 5, 7)), steps_in(slot)):
                    if k == at:
                        step(n)
                if slot == FLUSH_SLOT and k == 1:
                    flush(BATCH[0][1] - 1)
                if slot - 1 in V_UNITS and k == 2:
                    turn_values(slot - 1)

            pe.wait_ge(square_in, 16)
            pe.wait_ge(vec_in, 16 * 8)
            pe.transpose(banks[4][:, 0:4 * KT + 1], vec_rows[:, :], ident[0:4 * KT + 1, 0:4 * KT + 1])
            for c in range(4):
                mm = pe.transpose(banks[4][:, 64 + c * 2 * FT:64 + (c + 1) * 2 * FT], conv_rows[:, c, :],
                                  ident[0:2 * FT, 0:2 * FT])
            mm.then_inc(vec_turned, 1)
            for t in range(TT):
                pe.wait_ge(x_in[t], 16)
                if t >= 2:
                    pe.wait_ge(x_kept, 2 * (t - 1))
                for f in range(KT):
                    bank = banks[(2, 3, 6, 7)[t % 2 * 2 + f // 4]]
                    mm = pe.transpose(bank[:, f % 4 * P:(f % 4 + 1) * P], x_rows[:, t, f * P:(f + 1) * P], ident)
                    if f % 4 == 3:
                        mm.then_inc(x_turned, 1)
            pe.wait_ge(table_in, 16 * 3)
            pe.matmul(banks[0][0:HEADS, :], rel_t[:, :], onehot[:, 0:512], start=True, stop=True)
            pe.matmul(banks[1][0:HEADS, 0:TABLE - 512], rel_t[:, :], onehot[:, 512:TABLE], start=True, stop=True)\
              .then_inc(table_sum, 1)

            for u in range(PROJ):
                begin_unit(u, GROUP_OF[u])
                if u == 0:
                    pe.wait_ge(table_ready, 2)
                for k in range(KT):
                    if u == 0:
                        wait_h(0, k)
                    if u == 1 and k == 5:
                        spread_row(0)
                    mm = products(acc[u % 2], u % SPLIT, k, P, 0, h_hi[:, k, :], h_lo[:, k, :], k == 0, k == KT - 1)
                    if k == KT - 1:
                        mm.then_inc(unit_done, 1)
                    mixers(u, k)

            def mixed(k):
                if 3 <= k < 5:
                    return mix_b_hi[:, k - 3, :], mix_b_lo[:, k - 3, :]
                pair = k if k < 3 else k - 2
                return mix_a_hi[:, pair, :], mix_a_lo[:, pair, :]

            for u in range(PROJ, UP):
                early = u < PROJ + 2
                begin_unit(u, GROUP_OF[u])
                if u == PROJ:
                    pe.wait_ge(b_mixed, 2)
                    pe.wait_ge(mix_ready, PAIRS - 1)
                for k in range(KT - 1 if early else KT):
                    mm = products(acc[u % 2], u % SPLIT, k, P, 0, *mixed(k), k == 0, k == KT - 1)
                    if early:
                        mixers(u, k)
                if u == PROJ + 1:
                    flush(STEPS - 1)
                    pe.wait_ge(mix_ready, PAIRS)
                    for v in (PROJ, PROJ + 1):
                        products(acc[v % 2], v % SPLIT, KT - 1, P, 0, *mixed(KT - 1), False, True).then_inc(unit_done, 1)
                if not early:
                    mm.then_inc(unit_done, 1)

            for u in range(UP, DOWN):
                group = GROUP_OF[u]
                begin_unit(u, group)
                for k in range(KT):
                    if u == UP:
                        wait_h(1, k)
                        if k == 6:
                            sum_tokens(1)
                    if u == UP + 1 and k == 5:
                        spread_row(1)
                    mm = products(acc[group % 2], u % SPLIT, k, P, 0, h_hi[:, k, :], h_lo[:, k, :], k == 0, k == KT - 1)
                mm.then_inc(unit_done, 1)

            for u in range(DOWN, PE_UNITS):
                _, k0, nk, _, _ = UNITS[u]
                f = (u - DOWN) // 3
                group = GROUP_AT["x", 2 * KT + f]
                pe.wait_ge(wlo_ready, u + 1)
                if k0 == 0:
                    wait_taken(pe, group - 2)
                for k in range(nk):
                    if f == 0:
                        pe.wait_ge(act_ready, k0 + k + 1)
                    mm = products(acc[group % 2], u % SPLIT, k, P, 0, act_hi[:, k0 + k, :], act_lo[:, k0 + k, :],
                                  k0 + k == 0, k0 + k == FT - 1)
                mm.then_inc(unit_done, 1)
                if u == DOWN + 8:
                    pe.wait_ge(p_in, 16)
                    for c in range(2):
                        for t in range(TT):
                            mm = pe.transpose(turned[c][:, t * P:(t + 1) * P], p_rows[:, t, c * P:(c + 1) * P], ident)
                    mm.then_inc(p_turned, 1)

            for u in range(PE_UNITS, PG):
                pe.wait_ge(wlo_ready, u + 1)
                if u == PE_UNITS:
                    pe.wait_ge(p_ready, 2)
                for c in range(4):
                    f = 4 * (u - PE_UNITS) + c
                    if f >= 4:
                        pe.wait_ge(pe_kept, f - 3)
                    for k in range(2):
                        mm = products(banks[PE_BANK[f % 4]], u % SPLIT, k, 512, c * P, p_hi[:, k, :], p_lo[:, k, :], k == 0, k == 1)
                    mm.then_inc(unit_done if c == 3 else pe_done, 1)
                if u == PE_UNITS:
                    sum_tokens(2)
                else:
                    spread_row(2)

            def turn_result(f):
                pe.wait_ge(x_ready, 2 * KT + f + 1)
                if f >= 3:
                    pe.wait_ge(y_kept, f - 2)
                for t in range(TT):
                    mm = pe.transpose(banks[(2, 3, 6)[f % 3]][:, t * P:(t + 1) * P], x_t[:, f, t * P:(t + 1) * P], ident)
                mm.then_inc(y_turned, 1)

            for f in range(KT):
                u, group = PG + f, GROUP_AT["ple", f]
                begin_unit(u, group)
                for k in range(KT):
                    if f == 0:
                        wait_h(2, k)
                    if f and k == 6:
                        turn_result(f - 1)
                    mm = products(acc[group % 2], u % SPLIT, k, P, 0, h_hi[:, k, :], h_lo[:, k, :], k == 0, k == KT - 1)
                mm.then_inc(unit_done, 1)
            turn_result(KT - 1)
            sum_tokens(3)

        @block.scalar
        def _(act):
            act.preload_act_table_set("natural_log_exp_and_others")
            for i, name in enumerate(("norm_mix", "norm_ffn", "norm_ple", "norm_final")):
                src = a[name] if name == "norm_final" else a[name][0]
                act.dma_start(vec_rows[i * KT:(i + 1) * KT, :], src.rearrange("(k p) -> k p", p=P)).then_inc(vec_in, 16)
            for h in range(2):
                act.dma_start(vec_rows[4 * KT:4 * KT + 1, h * HEAD:(h + 1) * HEAD], a["hgrn_gnorm"]).then_inc(vec_in, 16)
            act.dma_start(conv_rows[:, 0:3, :], a["conv_w"][0].rearrange("t (b p) -> b t p", p=P)).then_inc(vec_in, 16)
            act.dma_start(conv_rows[:, 3, :], a["conv_b"][0].rearrange("(b p) -> b p", p=P)).then_inc(vec_in, 16)
            act.dma_start(rel_t[:, :], a["rel_bias"].rearrange("h b -> b h"), allow_slow_non_contiguous=True).then_inc(table_in, 16)
            act.dma_start(onehot[:, :], a["c_onehot"]).then_inc(table_in, 16)
            act.dma_start(extra[:, :], a["c_extra"]).then_inc(table_in, 16)
            act.dma_start(masks[:, :], a["c_masks"]).then_inc(masks_in, 16)

            def split_hi(u):
                _, _, nk, _, ncol = UNITS[u]
                act.wait_ge(raw_full[u % RAW], 16 * (u // RAW + 1))
                if u >= SPLIT:
                    act.wait_ge(unit_done, u - SPLIT + 1)
                act.activation(w_hi[:, u % SPLIT, 0:nk * ncol], raw[:, u % RAW, 0:nk * ncol], ACT.Copy)\
                   .then_inc(whi_ready, 1)

            def gain_x(stage, f):
                act.activation(h_hi[:, f, :], x_t[:, f, :], ACT.Copy, scale=vec_cols[:, stage * KT + f:stage * KT + f + 1])\
                   .then_inc(h_hi_ready, 1)

            def square_x(n):
                if n >= 2:
                    if n % KT == 1 and n > KT:
                        act.wait_ge(tokens_summed, n // KT)
                    else:
                        act.wait_ge(sumsq_ready, (KT - 1) * (n // KT) + min(n % KT - 1, KT - 1) if n % KT else (KT - 1) * (n // KT))
                act.activation(scratch[:, 2 + n % 2, :], x_t[:, n % KT, :], ACT.Square).then_inc(sq_ready, 1)

            def spread(stage):
                act.wait_ge(row_spread, stage + 1)
                act.activation(r_row[:, :], turned[1][:, :], ACT.Copy).then_inc(r_ready, 1)

            def take(group):
                kind, i, unit = GROUPS[group]
                if kind == "x":
                    n = i - KT
                    act.wait_ge(x_ready, n + 1)
                    gain_x(n // KT + 1, n % KT)
                    square_x(n)
                elif kind == "z":
                    wait_taken(act, group)
                    t = scratch[:, 2 + i % 2, :]
                    if i >= 2:
                        act.wait_ge(log_f, i - 1)
                    act.activation(t, scratch[:, i % 2, :], ACT.Abs).then_inc(z_chain, 1)
                    act.wait_ge(z_chain, 3 * i + 1)
                    act.activation(t, t, ACT.Exp, scale=-1.0).then_inc(z_chain, 1)
                    act.wait_ge(z_chain, 3 * i + 2)
                    act.activation(t, t, ACT.Ln, bias=1.0).then_inc(z_chain, 1)
                elif kind == "g":
                    wait_taken(act, group)
                    act.activation(b_gate[:, i, :], b_gate[:, i, :], ACT.Silu).then_inc(gate_ready, 1)
                elif kind == "bq":
                    wait_taken(act, group)
                    part = b_q[:, i // 2, (i % 2) * SEQ:(i % 2 + 1) * SEQ]
                    act.activation(part, part, ACT.Silu).then_inc(bq_ready, 1)
                elif kind in ("gate", "value"):
                    c = i if kind == "gate" else FT + i
                    n = 2 * i + (kind == "value")
                    dst = (conv_g if kind == "gate" else conv_v)[:, i % 3, :]
                    if i >= 3:
                        if kind == "gate":
                            act.wait_ge(prod_ready, i - 2)
                        else:
                            act.wait_ge(act_ready, i - 2)
                    wait_taken(act, group)
                    act.activation(dst, scratch[:, n % 3, :], ACT.Identity, bias=conv_cols[:, 3, c:c + 1],
                                   scale=conv_cols[:, 2, c:c + 1]).then_inc(tap2_ready, 1)
                    if kind == "value":
                        act.wait_ge(tap0_ready, n)
                        act.activation(conv_g[:, i % 3, :], conv_g[:, i % 3, :], ACT.Silu).then_inc(silu_ready, 1)
                elif kind == "ple":
                    wait_taken(act, group)
                    act.activation(conv_g[:, i % 3, :], conv_g[:, i % 3, :], ACT.Sigmoid).then_inc(sig_ready, 1)

            def key_of(h):
                act.wait_ge(kin_arg, h + 1)
                part = b_kin[:, h // 2, (h % 2) * SEQ:(h % 2 + 1) * SEQ]
                act.activation(part, part, ACT.Exp, scale=-1.0).then_inc(kin_ready, 1)

            def decays(n):
                level, pair = n // 2, n % 2
                if n < 4:
                    act.wait_ge(g_ready, B_HEADS)
                    act.wait_ge(filled, 4)
                else:
                    act.wait_ge(sums_ready, 2 * (n - 3))
                    act.wait_ge(b_scored, 2 * (n - 1))
                s = 1 << (level - 1)
                to, back, ahead = halves(b_qk, pair, s), halves(b_bwd, pair, s)[0], halves(b_fwd, pair, s)[1]
                act.activation(to[0], back, ACT.Exp).then_inc(decay_ready, 1)
                act.activation(to[1], ahead, ACT.Exp).then_inc(decay_ready, 1)

            def b_square(pair):
                act.wait_ge(b_out, pair + 1)
                act.activation(scratch[:, pair, :], outs[pair][:, :], ACT.Square).then_inc(b_squared, 1)

            def b_rstd_of(pair):
                v, r = b_qk[:, pair, 0:SEQ], b_qk[:, pair, SEQ:2 * SEQ]
                act.wait_ge(b_summed, pair + 1)
                act.activation(v, turned[1 - pair][:, :], ACT.Identity, bias=eps_col[:, :], scale=1.0 / HEAD).then_inc(b_var, 1)
                act.wait_ge(b_var, pair + 1)
                act.activation(r, v, ACT.Ln).then_inc(b_ln, 1)
                act.wait_ge(b_ln, pair + 1)
                act.activation(r, r, ACT.Exp, scale=-0.5).then_inc(b_rstd, 1)

            def load_bias(pair):
                act.dma_start(bias[:, pair % 2, :, :], bias_of(pair)).then_inc(bias_in[pair % 2], 16)

            def step_exp(n):
                keys = (tile_of(n) + 1) * P
                act.wait_ge(logits, n + 1)
                act.activation(probs[:, n % 4, 0:keys], probs[:, n % 4, 0:keys], ACT.Exp, scale=-1.0,
                               bias=row_min[:, n:n + 1], accum_out=row_sum[:, n:n + 1]).then_inc(exped, 1)

            def step_keep(n):
                keys = (tile_of(n) + 1) * P
                act.wait_ge(probs_turned, n + 1)
                if n >= 4:
                    act.wait_ge(weighted, n - 3)
                act.activation(probs_t[:, n % 4, 0:keys], turned[n % 2][:, 0:keys], ACT.Copy).then_inc(probs_t_ready, 1)

            def bias_of(pair):
                return bass.AP(tensor=bias_dram.tensor, offset=2 * pair * TABLE, ap=[[1, P], [TABLE, 2], [1, SEQ]])

            def mixers(slot):
                for n in rounds_in(slot):
                    if 2 <= n + 1 < ROUNDS:
                        decays(n + 1)
                if slot == B_OUT_SLOT:
                    act.wait_ge(b_kept, 2 * ROUNDS)
                    act.wait_ge(table_out, 16)
                    load_bias(0)
                    load_bias(1)
                    b_square(0)
                    b_square(1)
                for i, n in enumerate(steps_in(slot)):
                    if n % (2 * TT) == 0 and 2 * TT <= n < (PAIRS - 1) * 2 * TT:
                        act.wait_ge(logits, n)
                        load_bias(n // (2 * TT) + 1)
                    if n - TURN_LAG >= batch_start(n):
                        step_keep(n - TURN_LAG)
                    step_exp(n)
                    if slot == B_OUT_SLOT + 1 and i in (1, 2):
                        b_rstd_of(i - 1)
                if slot == FLUSH_SLOT:
                    for n in range(BATCH[0][1] - TURN_LAG, BATCH[0][1]):
                        step_keep(n)
                if slot == PROJ + 1:
                    for n in range(STEPS - TURN_LAG, STEPS):
                        step_keep(n)

            act.wait_ge(filled, 1)
            act.wait_ge(vec_turned, 1)
            act.activation(vec_cols[:, :], banks[4][:, 0:4 * KT + 1], ACT.Copy, scale=-0.5).then_inc(vec_ready, 1)
            act.activation(conv_cols[:, :, :], banks[4][:, 64:64 + 8 * FT].rearrange("p (c b) -> p c b", c=4),
                           ACT.Copy).then_inc(vec_ready, 1)
            act.wait_ge(vec_ready, 2)

            def square_rows(t):
                act.wait_ge(x_in[t], 16)
                if t:
                    act.wait_ge(rows_squared, t)
                act.activation(scratch[:, 2:4, :].rearrange("p a n -> p (a n)"), x_rows[:, t, :], ACT.Square,
                               accum_out=stat[:, 0, t:t + 1]).then_inc(rows_squared, 1)

            square_rows(0)
            split_hi(0)
            square_rows(1)
            act.wait_ge(x_kept, 2 * TT)
            for f in range(KT):
                gain_x(0, f)
            square_rows(2)
            square_rows(3)
            split_hi(1)
            act.wait_ge(table_ready, 2)
            act.dma_start(bias_dram, table[:, :]).then_inc(table_out, 16)

            for u in range(N_UNITS):
                beside = u == PROJ + 1
                if beside:
                    mixers(u)
                if u - 1 in GROUP_OF and GROUPS[GROUP_OF[u - 1]][0] == "x":
                    take(GROUP_OF[u - 1])
                if u + 2 < N_UNITS:
                    split_hi(u + 2)
                if u == ROUND_SLOT:
                    act.preload_act_table_set("natural_log_exp_and_others")
                if u == UP:
                    act.preload_act_table(ACT.Silu)
                if u == PE_UNITS:
                    act.preload_act_table(ACT.Sigmoid)
                if u == 1:
                    spread(0)
                if u == UP + 1:
                    spread(1)
                if u == PG:
                    spread(2)
                if 2 <= u < 2 + B_HEADS:
                    key_of(u - 2)
                if u - 1 in GROUP_OF and GROUPS[GROUP_OF[u - 1]][0] != "x":
                    take(GROUP_OF[u - 1])
                if u <= PROJ and not beside:
                    mixers(u)
                if u == DOWN + 10:
                    act.wait_ge(p_turned, 1)
                    for c in range(2):
                        act.activation(p_hi[:, c, :], turned[c][:, :], ACT.Copy).then_inc(p_hi_ready, 1)
                if PE_UNITS <= u < PG:
                    for c in range(4):
                        f = 4 * (u - PE_UNITS) + c
                        if c < 3:
                            act.wait_ge(pe_done, 3 * (u - PE_UNITS) + c + 1)
                        else:
                            act.wait_ge(unit_done, u + 1)
                        act.activation(pe_out[:, f, :], banks[PE_BANK[f % 4]][:, :], ACT.Copy).then_inc(pe_kept, 1)
                if u > PG:
                    act.wait_ge(x_ready, 2 * KT + u - PG)
                    square_x(2 * KT + u - 1 - PG)
            take(GROUP_OF[N_UNITS - 1])
            act.wait_ge(x_ready, 3 * KT)
            square_x(3 * KT - 1)
            act.wait_ge(y_kept, KT)
            act.wait_ge(newton, 12 * 4)
            act.activation(y_rows[:, TT - 1, :], y_rows[:, TT - 1, :], ACT.Copy, scale=stat[:, 2, TT - 1:TT]).then_inc(y_act, 1)

        @block.vector
        def _(dve):
            def split_lo(u):
                _, _, nk, _, ncol = UNITS[u]
                dve.wait_ge(whi_ready, u + 1)
                dve.tensor_tensor(w_lo[:, u % SPLIT, 0:nk * ncol], raw[:, u % RAW, 0:nk * ncol],
                                  w_hi[:, u % SPLIT, 0:nk * ncol].bitcast(F32), ALU.subtract).then_inc(wlo_ready, 1)

            def lo_x(stage, f):
                dve.wait_ge(h_hi_ready, stage * KT + f + 1)
                dve.scalar_tensor_tensor(out=h_lo[:, f, :], in0=x_t[:, f, :], scalar=vec_cols[:, stage * KT + f:stage * KT + f + 1],
                                         in1=h_hi[:, f, :].bitcast(F32), op0=ALU.mult, op1=ALU.subtract).then_inc(h_lo_ready, 1)

            def rstd_of(stage):
                if stage == 0:
                    dve.wait_ge(rows_squared, TT)
                else:
                    dve.wait_ge(tokens_summed, stage)
                sums = stat[:, 0, :] if stage == 0 else turned[0][:, 0:TT]
                v, y, t = stat[:, 1, :], stat[:, 2, :], stat[:, 3, :]
                n = [12 * stage]

                def link(ins):
                    n[0] += 1
                    ins.then_inc(newton, 1)
                    dve.wait_ge(newton, n[0])

                link(dve.tensor_scalar(v, sums, 1.0 / D, EPS, ALU.mult, ALU.add))
                link(dve.tensor_scalar(stat_bits[:, 0, :], v.bitcast(I32), 1, None, ALU.logical_shift_right))
                link(dve.tensor_scalar(stat_bits[:, 1, :], stat_bits[:, 0, :], -1.0, float(0x5F3759DF), ALU.mult, ALU.add))
                guess = stat_bits[:, 1, :].bitcast(F32)
                for step in range(3):
                    y0 = guess if step == 0 else y
                    link(dve.tensor_tensor(t, v, y0, ALU.mult))
                    if step < 2 or stage == 3:
                        link(dve.scalar_tensor_tensor(out=t, in0=t, scalar=-0.5, in1=y0, op0=ALU.mult, op1=ALU.mult))
                        link(dve.scalar_tensor_tensor(out=y, in0=t, scalar=1.5, in1=y0, op0=ALU.add, op1=ALU.mult))
                    else:
                        link(dve.tensor_tensor(t, t, y0, ALU.mult))
                        link(dve.scalar_tensor_tensor(out=y, in0=t, scalar=-3.0, in1=y0, op0=ALU.add, op1=ALU.mult))

            def diagonal():
                to = scratch[:, 0, :].rearrange("p (t c) -> p t c", t=TT)
                dve.tensor_tensor(to, ident.rearrange("p (o c) -> p o c", o=1).to_broadcast([P, TT, P]),
                                  stat[:, 2, :].rearrange("p (t o) -> p t o", o=1).to_broadcast([P, TT, P]), ALU.mult)\
                   .then_inc(diag_ready, 1)

            def times_r(out, bank):
                return dve.tensor_tensor(out, bank, r_row[:, :], ALU.mult)

            def take(group):
                kind, i, unit = GROUPS[group]
                bank = acc[group % 2]
                dve.wait_ge(unit_done, unit + 1)
                if group == 0:
                    dve.wait_ge(r_ready, 1)
                if kind == "z":
                    z, log1p = scratch[:, i % 2, :], scratch[:, 2 + i % 2, :]
                    part = slice((i % 2) * SEQ, (i % 2 + 1) * SEQ)
                    if i >= 2:
                        dve.wait_ge(log_f, i - 1)
                    times_r(z, bank[:, :]).then_inc(acc_taken, 1)
                    dve.wait_ge(z_chain, 3 * i + 3)
                    dve.scalar_tensor_tensor(out=b_kin[:, i // 2, part], in0=z, scalar=0.0, in1=log1p,
                                             op0=ALU.max, op1=ALU.add).then_inc(kin_arg, 1)
                    dve.scalar_tensor_tensor(out=b_fwd[:, i // 2, part], in0=z, scalar=0.0, in1=log1p,
                                             op0=ALU.min, op1=ALU.subtract).then_inc(log_f, 1)
                    dve.wait_ge(log_f, i + 1)
                    dve.tensor_scalar(b_fwd[:, i // 2, part], b_fwd[:, i // 2, part], LOG_FLOOR, None, ALU.max)\
                       .then_inc(g_ready, 1)
                elif kind == "g":
                    times_r(b_gate[:, i, :], bank[:, :]).then_inc(acc_taken, 1)
                elif kind == "bq":
                    times_r(b_q[:, i // 2, (i % 2) * SEQ:(i % 2 + 1) * SEQ], bank[:, :]).then_inc(acc_taken, 1)
                elif kind == "v":
                    if i:
                        dve.wait_ge(v_turned, i)
                    times_r(v_t[:, :], bank[:, :]).then_inc(acc_taken, 1)
                elif kind == "q":
                    if i == 0:
                        dve.wait_ge(filled, 3)
                    if i >= 3:
                        dve.wait_ge(scored, 2 * TT * (i - 2))
                    for hh in range(2):
                        r = hh * HEAD
                        queries, r_back = (bass.AP(tensor=t.tensor, offset=t[r:r + 1, :].offset + P - 1,
                                                   ap=[[SEQ, HEAD], [P, TT], [-1, P]]) for t in (bank[:, :], r_row[:, :]))
                        ins = dve.scalar_tensor_tensor(
                            out=q_pad[r:r + HEAD, i % 3, hh, :].rearrange("p (t q) -> p t q", t=TT), in0=queries,
                            scalar=-SCALE, in1=r_back, op0=ALU.mult, op1=ALU.mult)
                    ins.then_inc(acc_taken, 1)
                elif kind == "k":
                    if i >= 3:
                        dve.wait_ge(scored, 2 * TT * (i - 2))
                    times_r(k_t[:, i % 3, :], bank[:, :]).then_inc(acc_taken, 1)
                elif kind == "x":
                    dve.tensor_tensor(x_t[:, i % KT, :], bank[:, :], x_t[:, i % KT, :], ALU.add).then_inc(x_ready, 1)
                elif kind in ("gate", "value"):
                    c = i if kind == "gate" else FT + i
                    dst = (conv_g if kind == "gate" else conv_v)[:, i % 3, :]
                    n = 2 * i + (kind == "value")
                    u = scratch[:, n % 3, :]
                    if n == 0:
                        dve.wait_ge(r_ready, 2)
                    elif n >= 3:
                        dve.wait_ge(tap0_ready, n - 2)
                    times_r(u, bank[:, :]).then_inc(acc_taken, 1)
                    dve.wait_ge(tap2_ready, n + 1)
                    dve.scalar_tensor_tensor(out=dst[:, 1:SEQ], in0=u[:, 0:SEQ - 1], scalar=conv_cols[:, 1, c:c + 1],
                                             in1=dst[:, 1:SEQ], op0=ALU.mult, op1=ALU.add).then_inc(tap1_ready, 1)
                    dve.wait_ge(tap1_ready, n + 1)
                    dve.scalar_tensor_tensor(out=dst[:, 2:SEQ], in0=u[:, 0:SEQ - 2], scalar=conv_cols[:, 0, c:c + 1],
                                             in1=dst[:, 2:SEQ], op0=ALU.mult, op1=ALU.add).then_inc(tap0_ready, 1)
                elif kind == "ple":
                    if i == 0:
                        dve.wait_ge(r_ready, 3)
                    if i >= 3:
                        dve.wait_ge(x_ready, 2 * KT + i - 2)
                    times_r(conv_g[:, i % 3, :], bank[:, :]).then_inc(acc_taken, 1)

            def add_gated(f):
                dve.wait_ge(sig_ready, f + 1)
                dve.wait_ge(pe_kept, f + 1)
                g = conv_g[:, f % 3, :]
                dve.tensor_tensor(g, g, pe_out[:, f, :], ALU.mult).then_inc(gated, 1)
                dve.wait_ge(gated, f + 1)
                dve.tensor_tensor(x_t[:, f, :], x_t[:, f, :], g, ALU.add).then_inc(x_ready, 1)

            def keep_result(f):
                dve.wait_ge(y_turned, f + 1)
                cols = slice(f * P, (f + 1) * P)
                dve.tensor_tensor(y_rows[:, :, cols], banks[(2, 3, 6)[f % 3]][:, :].rearrange("p (t c) -> p t c", t=TT),
                                  gain_row[:, cols].rearrange("p (o c) -> p o c", o=1).to_broadcast([P, TT, P]), ALU.mult)\
                   .then_inc(y_kept, 1)

            def split_act(j):
                dve.wait_ge(prod_ready, j + 1)
                dve.tensor_copy(act_hi[:, j, :], conv_v[:, j % 3, :]).then_inc(act_hi_ready, 1)
                dve.wait_ge(act_hi_ready, j + 1)
                dve.tensor_tensor(act_lo[:, j, :], conv_v[:, j % 3, :], act_hi[:, j, :].bitcast(F32), ALU.subtract)\
                   .then_inc(act_ready, 1)

            def decayed(n):
                level, pair = n // 2, n % 2
                dve.wait_ge(decay_ready, 2 * (n - 1))
                s = 1 << (level - 1)
                to, q, k = halves(b_qk, pair, s), halves(b_q, pair, s)[1], halves(b_kin, pair, s)[0]
                dve.tensor_tensor(to[1], to[1], q, ALU.mult).then_inc(qk_ready, 1)
                dve.tensor_tensor(to[0], to[0], k, ALU.mult).then_inc(qk_ready, 1)

            def keep_scores(n):
                level, pair = n // 2, n % 2
                for hh in range(2):
                    use = 2 * n + hh
                    att, bank = b_att[:, 2 * pair + hh, :], score[hh]
                    dve.wait_ge(b_scored, use + 1)
                    if level <= MASKED_LEVELS:
                        if use >= 4:
                            dve.wait_ge(b_kept, use - 3)
                        else:
                            dve.wait_ge(masks_in, 16)
                            dve.wait_ge(table_out, 16)
                        mask = masks[:, level * P:(level + 1) * P].rearrange("p (o i) -> p o i", o=1).to_broadcast([P, TT, P])
                        to = att[:, 0:TT * P].rearrange("p (b i) -> p b i", b=TT)
                        new = bank[:, :].rearrange("p (b i) -> p b i", b=TT)
                        if level == 0:
                            ins = dve.tensor_tensor(to, new, mask, ALU.mult)
                        else:
                            ins = dve.copy_predicated(to, mask, new)
                    elif level == MASKED_LEVELS + 1:
                        ins = dve.tensor_copy(att[:, 4 * P:6 * P], bank[:, 0:2 * P])
                    else:
                        ins = dve.tensor_copy(att[:, 6 * P:10 * P], bank[:, :])
                    ins.then_inc(b_kept, 1)

            def b_mix(pair):
                v, r, c = b_qk[:, pair, 0:SEQ], b_qk[:, pair, SEQ:2 * SEQ], b_bwd[:, pair, 0:SEQ]
                dve.wait_ge(b_rstd, pair + 1)
                dve.tensor_tensor(c, v, r, ALU.mult).then_inc(b_newton, 1)
                dve.wait_ge(b_newton, 3 * pair + 1)
                dve.tensor_tensor(c, c, r, ALU.mult).then_inc(b_newton, 1)
                dve.wait_ge(b_newton, 3 * pair + 2)
                dve.scalar_tensor_tensor(out=v, in0=c, scalar=-3.0, in1=r, op0=ALU.add, op1=ALU.mult).then_inc(b_newton, 1)
                dve.wait_ge(b_newton, 3 * pair + 3)
                dve.wait_ge(gate_ready, 2)
                t = scratch[:, 2 + pair, :]
                dve.scalar_tensor_tensor(out=t, in0=outs[pair][:, :], scalar=vec_cols[:, 4 * KT:4 * KT + 1], in1=v,
                                         op0=ALU.mult, op1=ALU.mult).then_inc(b_normed, 1)
                dve.wait_ge(b_normed, pair + 1)
                dve.tensor_tensor(t, t, b_gate[:, pair, :], ALU.mult).then_inc(b_gated, 1)
                dve.wait_ge(b_gated, pair + 1)
                dve.tensor_copy(mix_b_hi[:, pair, :], t).then_inc(b_hi_ready, 1)
                dve.wait_ge(b_hi_ready, pair + 1)
                dve.tensor_tensor(mix_b_lo[:, pair, :], t, mix_b_hi[:, pair, :].bitcast(F32), ALU.subtract).then_inc(b_mixed, 1)

            def keep_values(unit):
                g = V_UNITS.index(unit)
                dve.wait_ge(v_turned, g + 1)
                if g >= 5:
                    dve.wait_ge(weighted, 2 * TT * (g - 4))
                to = b_v[:, g, :, :] if g < 2 else v_tok[:, (g - 2) % 3, :, :]
                dve.tensor_copy(to, turned[0][:, :].rearrange("p (t c) -> p t c", t=TT)).then_inc(v_ready, 1)

            def step_logits(n):
                head, i = n // TT, tile_of(n)
                pair, keys = head // 2, (i + 1) * P
                if n % (2 * TT) == 0:
                    dve.wait_ge(bias_in[pair % 2], 16 * (pair // 2 + 1))
                dve.wait_ge(scored, n + 1)
                if n >= 4:
                    dve.wait_ge(probs_turned, n - 3)
                dve.tensor_tensor_reduce(out=probs[:, n % 4, 0:keys], in0=score[n % 2][:, 0:keys],
                                         in1=bias[:, pair % 2, head % 2, SEQ - keys:SEQ], scale=1.0, scalar=3.0e38,
                                         op0=ALU.add, op1=ALU.min, accum_out=row_min[:, n:n + 1]).then_inc(logits, 1)

            def step_invert(n):
                dve.wait_ge(exped, n + 1)
                dve.reciprocal(row_inv[:, n:n + 1], row_sum[:, n:n + 1]).then_inc(inverted, 1)

            def keep_mixed(pair):
                dve.wait_ge(weighted, 2 * TT * (pair + 1))
                dve.tensor_copy(mix_a_hi[:, pair, :], outs[pair % 2][:, :]).then_inc(mix_hi_ready, 1)
                dve.wait_ge(mix_hi_ready, pair + 1)
                dve.tensor_tensor(mix_a_lo[:, pair, :], outs[pair % 2][:, :], mix_a_hi[:, pair, :].bitcast(F32), ALU.subtract)\
                   .then_inc(mix_ready, 1)

            def mixers(slot):
                for n in rounds_in(slot):
                    if 2 <= n + 1 < ROUNDS:
                        decayed(n + 1)
                    keep_scores(n)
                v_here = slot - 1 in V_UNITS
                for i, n in enumerate(steps_in(slot)):
                    step_logits(n)
                    if n - 1 >= batch_start(n):
                        step_invert(n - 1)
                    m = n - VALUE_LAG
                    if m >= batch_start(n) and m % (2 * TT) == 2 * TT - 1:
                        keep_mixed(m // (2 * TT))
                    if i == (2 if slot >= PROJ else 0) and v_here:
                        keep_values(slot - 1)
                    if (slot, i) in ((B_OUT_SLOT + 1, 3), (B_OUT_SLOT + 2, 3)):
                        b_mix(slot - B_OUT_SLOT - 1)
                if v_here and not steps_in(slot):
                    keep_values(slot - 1)
                if slot == FLUSH_SLOT:
                    step_invert(BATCH[0][1] - 1)
                    keep_mixed(PAIRS - 2)
                if slot == PROJ + 1:
                    step_invert(STEPS - 1)
                    keep_mixed(PAIRS - 1)

            for t in range(TT):
                for half in range(2):
                    dve.wait_ge(x_turned, 2 * t + half + 1)
                    dve.tensor_copy(x_t[:, 4 * half:4 * half + 4, t * P:(t + 1) * P],
                                    banks[(2, 3, 6, 7)[t % 2 * 2 + half]][:, :].rearrange("p (f c) -> p f c", f=4))\
                       .then_inc(x_kept, 1)
                if t == 1:
                    split_lo(0)
            dve.wait_ge(x_kept, 2 * TT)
            dve.wait_ge(table_in, 16 * 3)
            dve.wait_ge(table_sum, 1)
            dve.scalar_tensor_tensor(out=table[:, 0:512], in0=banks[0][0:HEADS, :], scalar=-1.0, in1=extra[:, 0:512],
                                     op0=ALU.mult, op1=ALU.subtract).then_inc(table_ready, 1)
            dve.scalar_tensor_tensor(out=table[:, 512:TABLE], in0=banks[1][0:HEADS, 0:TABLE - 512], scalar=-1.0,
                                     in1=extra[:, 512:TABLE], op0=ALU.mult, op1=ALU.subtract).then_inc(table_ready, 1)
            for f in range(KT):
                lo_x(0, f)
            split_lo(1)
            rstd_of(0)
            diagonal()

            for u in range(N_UNITS):
                beside = u == PROJ + 1
                if beside:
                    mixers(u)
                before = GROUPS[GROUP_OF[u - 1]] if u - 1 in GROUP_OF else ("none", 0, 0)
                if before[0] == "x":
                    take(GROUP_OF[u - 1])
                if u + 2 < N_UNITS:
                    split_lo(u + 2)
                if before[0] == "x":
                    lo_x(before[1] // KT, before[1] % KT)
                elif before[0] != "none":
                    take(GROUP_OF[u - 1])
                if UP + 2 < u <= DOWN + 1 and (u - UP) % 2 == 1:
                    split_act((u - UP) // 2 - 1)
                if u <= PROJ and not beside:
                    mixers(u)
                if u == UP:
                    rstd_of(1)
                    diagonal()
                if u == DOWN + 10:
                    for c in range(2):
                        dve.wait_ge(p_hi_ready, c + 1)
                        dve.tensor_tensor(p_lo[:, c, :], turned[c][:, :], p_hi[:, c, :].bitcast(F32), ALU.subtract).then_inc(p_ready, 1)
                if u == PE_UNITS:
                    rstd_of(2)
                    diagonal()
                if u > PG:
                    add_gated(u - 1 - PG)
                    if u > PG + 1:
                        if u == PG + 2:
                            dve.wait_ge(gain_in, 16)
                        keep_result(u - 2 - PG)
            take(GROUP_OF[N_UNITS - 1])
            add_gated(KT - 1)
            keep_result(KT - 2)
            keep_result(KT - 1)
            rstd_of(3)
            dve.wait_ge(y_kept, KT)
            for t in range(TT - 1):
                dve.tensor_scalar(y_rows[:, t, :], y_rows[:, t, :], stat[:, 2, t:t + 1], None, ALU.mult).then_inc(y_dve, 1)

        @block.gpsimd
        def _(pool):
            pool.memset(eps_col[:, :], EPS).then_inc(filled, 1)
            pool.wait_ge(filled, 1)
            pool.memset(q_pad[0:HEAD, :, 1, :], 0.0).then_inc(filled, 1)
            pool.wait_ge(filled, 2)
            pool.memset(q_pad[HEAD:P, :, 0, :], 0.0).then_inc(filled, 1)
            pool.wait_ge(filled, 3)
            pool.memset(b_bwd[:, :, :], 0.0).then_inc(filled, 1)
            pool.wait_ge(filled, 4)

            def add_squares(n):
                f, count = n % KT, (KT - 1) * (n // KT)
                if f == KT - 1:
                    return
                pool.wait_ge(sq_ready, n + 1)
                if f == 0:
                    if n:
                        pool.wait_ge(tokens_summed, n // KT)
                    pool.tensor_scalar(sumsq[:, :], scratch[:, 2, :], 1.0, None, ALU.mult).then_inc(sumsq_ready, 1)
                else:
                    pool.wait_ge(sumsq_ready, count + f)
                    pool.tensor_tensor(sumsq[:, :], sumsq[:, :], scratch[:, 2 + f % 2, :], ALU.add).then_inc(sumsq_ready, 1)

            for n in range(2, ROUNDS - 2):
                level, pair = n // 2, n % 2
                s = 1 << (level - 1)
                (fwd1, fwd2), back = halves(b_fwd, pair, s), halves(b_bwd, pair, s)[0]
                like = [P, SEQ // s, s]
                pool.wait_ge(decay_ready, 2 * (n - 1))
                pool.tensor_tensor(back, back, fwd2[:, :, s - 1:s].to_broadcast(like), ALU.add).then_inc(sums_ready, 1)
                pool.wait_ge(sums_ready, 2 * (n - 2) + 1)
                pool.tensor_tensor(fwd2, fwd2, fwd1[:, :, s - 1:s].to_broadcast(like), ALU.add).then_inc(sums_ready, 1)
            for n in range(STEPS):
                keys = (tile_of(n) + 1) * P
                pool.wait_ge(inverted, n + 1)
                pool.tensor_scalar(probs[:, n % 4, 0:keys], probs[:, n % 4, 0:keys], row_inv[:, n:n + 1], None, ALU.mult)\
                    .then_inc(normed, 1)
            for f in range(KT):
                add_squares(f)
            for j in range(FT):
                pool.wait_ge(silu_ready, j + 1)
                pool.wait_ge(tap0_ready, 2 * j + 2)
                pool.tensor_tensor(conv_v[:, j % 3, :], conv_g[:, j % 3, :], conv_v[:, j % 3, :], ALU.mult).then_inc(prod_ready, 1)
            for n in range(KT, 3 * KT):
                add_squares(n)


_INS = ["x", "p", "rel_bias", "norm_mix", "w_in", "w_out", "hgrn_gnorm", "norm_ffn", "w_up", "conv_w", "conv_b",
        "w_down", "norm_ple", "w_pe", "w_pg", "norm_final"]


def kernel(**inputs):
    import concourse.bacc as _bacc
    from concourse.bass_utils import run_bass_kernel_spmd as _run

    nc = _bacc.Bacc("TRN2", target_bir_lowering=False, num_devices=1)
    arrays = {f"in_{name}": np.ascontiguousarray(inputs[name]) for name in _INS}
    arrays.update({f"in_{name}": c for name, c in shape_constants().items()})
    aps = {name[3:]: nc.dram_tensor(name, v.shape, mybir.dt.from_np(v.dtype), kind="ExternalInput").ap()
           for name, v in arrays.items()}
    out = nc.dram_tensor("out", (1, SEQ, D), F32, kind="ExternalOutput").ap()
    build(nc, aps, out)
    return _run(nc, [arrays], core_ids=[0]).results[0]["out"]
```

```python
from contextlib import ExitStack

import numpy as np

import concourse.bass as bass
from concourse import mybir

ALU = mybir.AluOpType
ACT = mybir.ActivationFunctionType
F32 = mybir.dt.float32
F32R = mybir.dt.float32r
I32 = mybir.dt.int32

P = 128
SEQ = 512
D = 1024
KT = D // P
TT = SEQ // P
HEAD = 64
FF = 2816
FT = FF // P
PLE = 256
EPS = 1e-6
N_BUCKETS = 32
MAX_DISTANCE = 2048
HEADS = 12
PAIRS = HEADS // 2
B_HEADS = 4
LEVELS = 9
MASKED_LEVELS = 6
HALF_LEVEL = 7
TABLE = SEQ + P
LOG_FLOOR = float(np.log(1e-30))
SCALE = HEAD ** -0.5
NEG_BIG = -1e30

A_Q, A_K, A_V, B_Q, B_Z, B_I, B_G, C_Q, C_K, C_V = 0, 3, 6, 9, 13, 17, 19, 21, 24, 27

UNITS = []
GROUPS = []


def _unit(matrix, k0, nk, c0, nc=P):
    UNITS.append((matrix, k0, nk, c0, nc))


def _group(kind, index):
    GROUPS.append((kind, index, len(UNITS) - 1))


for _h in range(B_HEADS):
    _unit("w_in", 0, KT, (B_Z + _h) * P)
    _group("z", _h)
for _h in range(B_HEADS):
    _unit("w_in", 0, KT, (B_Q + _h) * P)
    _group("bq", _h)
for _b in range(2):
    _unit("w_in", 0, KT, (B_G + _b) * P)
    _group("g", _b)
for _b in range(2):
    _unit("w_in", 0, KT, (B_I + _b) * P)
    _group("v", _b)
for _p in range(PAIRS):
    for _kind, _a, _c in (("q", A_Q, C_Q), ("k", A_K, C_K), ("v", A_V, C_V)):
        _unit("w_in", 0, KT, ((_a + _p) if _p < 3 else (_c + _p - 3)) * P)
        _group(_kind, _p + 2 if _kind == "v" else _p)
PROJ = len(UNITS)
for _f in range(KT):
    _unit("w_out", 0, KT, _f * P)
    _group("x", KT + _f)
UP = len(UNITS)
for _j in range(FT):
    _unit("w_up", 0, KT, _j * P)
    _group("gate", _j)
    _unit("w_up", 0, KT, FF + _j * P)
    _group("value", _j)
DOWN = len(UNITS)
for _f in range(KT):
    for _k0 in range(0, FT, KT):
        _unit("w_down", _k0, min(KT, FT - _k0), _f * P)
    _group("x", 2 * KT + _f)
PE_UNITS = len(UNITS)
for _c in range(2):
    _unit("w_pe", 0, PLE // P, _c * 512, 512)
PG = len(UNITS)
for _f in range(KT):
    _unit("w_pg", 0, KT, _f * P)
    _group("ple", _f)
N_UNITS = len(UNITS)

UP_PEELED, UP_ROUND = 8, 6
UP_PAIRS = UP_ROUND // 2
UP_ROUNDS = (2 * FT - UP_PEELED) // UP_ROUND
assert UP_PEELED + UP_ROUNDS * UP_ROUND == 2 * FT

RAW = 3
SPLIT = 3
TURN_LAG, VALUE_LAG = 4, 5
PROBS = 5

V_UNITS = [g[2] for g in GROUPS if g[0] == "v"]
ROUND_SLOT = 10
ROUNDS = 2 * (LEVELS + 1)


def rounds_in(slot):
    return [n for n in range(ROUNDS) if ROUND_SLOT + n * 2 // 5 == slot]


B_OUT_SLOT = ROUND_SLOT + ROUNDS * 2 // 5
STEPS = HEADS * TT
TICKS = STEPS + TURN_LAG
TICK_SLOTS = range(B_OUT_SLOT + 1, B_OUT_SLOT + 1 + TICKS // TT)


def tick_places(slot):
    return {PROJ - 1: (4, 5, 6, 7), PROJ: (1, 3, 4, 6), PROJ + 1: (0, 1, 2, 3)}.get(slot, (1, 3, 5, 7))


LAST_VALUES = 4


def values_place(slot):
    return 2


def ticks_in(slot):
    return [TT * TICK_SLOTS.index(slot) + i for i in range(TT)] if slot in TICK_SLOTS else []


def ticks_before_values(slot):
    here = sum(k <= values_place(slot) for k in tick_places(slot)) if slot in TICK_SLOTS else 0
    return TT * sum(s < slot for s in TICK_SLOTS) + here


def split_late(slot):
    return TICK_SLOTS[0] < slot < PROJ - 1


def tile_of(n):
    return TT - 1 - n % TT


def rel_bucket(d):
    exact = N_BUCKETS // 2
    d = max(d, 0)
    if d < exact:
        return d
    return min(N_BUCKETS - 1, exact + int(np.log(d / exact) / np.log(MAX_DISTANCE / exact) * (N_BUCKETS - exact)))


def shape_constants():
    square = np.concatenate([np.eye(P), np.ones((P, P)), np.kron(np.eye(2), np.ones((HEAD, HEAD))), np.eye(P)[::-1]], 1)
    onehot = np.zeros((N_BUCKETS, TABLE))
    extra = np.full((HEADS, TABLE), NEG_BIG)
    for j in range(TABLE):
        d = SEQ - 1 - j
        onehot[rel_bucket(d), j] = 1
        if d >= 0:
            seen = (d <= 128) + (d % 4 == 0) + (d % 16 == 0)
            if seen:
                extra[:6, j] = np.log(seen)
            extra[6:, j] = 0
    j, i = np.arange(P)[:, None], np.arange(P)[None, :]
    masks = [j == i]
    for level in range(MASKED_LEVELS):
        s = 1 << level
        masks.append((j // (2 * s) == i // (2 * s)) & (j % (2 * s) < s) & (i % (2 * s) >= s))
    return {
        "c_square": square.astype(np.float32),
        "c_onehot": onehot.astype(np.float32),
        "c_extra": extra.astype(np.float32),
        "c_masks": np.concatenate(masks, 1).astype(np.int32),
    }


def build(nc, a, out):
    bias_dram = nc.dram_tensor("bias_table", [HEADS, TABLE], F32, kind="Internal").ap()
    with ExitStack() as ctx:
        def sb(name, shape, dt=F32, stack=ctx):
            return stack.enter_context(nc.sbuf_tensor(name, shape, dt))

        def sem(name):
            return ctx.enter_context(nc.semaphore(name))

        x_t = sb("x_t", [P, KT, SEQ])
        h_hi = sb("h_hi", [P, KT, SEQ], F32R)
        h_lo = sb("h_lo", [P, KT, SEQ], F32R)
        raw = sb("raw", [P, RAW, 1024])
        w_hi = sb("w_hi", [P, SPLIT, 1024], F32R)
        w_lo = sb("w_lo", [P, SPLIT, 1024], F32R)
        square = sb("square", [P, 4 * P])
        ident, ones, half_ones, flip = (square[:, i * P:(i + 1) * P] for i in range(4))
        vec_cols = sb("vec_cols", [P, 4 * KT + 1])
        conv_cols = sb("conv_cols", [P, 4, 2 * FT])
        eps_col = sb("eps_col", [P, 1])
        sumsq = sb("sumsq", [P, SEQ])
        scratch = sb("scratch", [P, 4, SEQ])
        r_row = sb("r_row", [P, SEQ])
        stat = sb("stat", [P, 4, TT])
        stat_bits = sb("stat_bits", [P, 2, TT], I32)
        parts = sb("parts", [P, TT, KT])

        mixing = ExitStack()
        q_both = sb("q_both", [P, 3, 2, SEQ], F32R, mixing)
        k_both = sb("k_both", [P, 3, 2, SEQ], F32R, mixing)
        k_lo = sb("k_lo", [P, 3, SEQ], F32R, mixing)
        v_tok = sb("v_tok", [P, 3, TT, P], F32, mixing)
        v_t = sumsq
        hgrn = ExitStack()
        b_fwd = sb("b_fwd", [P, 2, 1024], F32, hgrn)
        b_kin = sb("b_kin", [P, 2, 1024], F32, hgrn)
        b_q = sb("b_q", [P, 2, 1024], F32, hgrn)
        b_bwd = sb("b_bwd", [P, 2, 1024], F32, hgrn)
        b_qk = sb("b_qk", [P, 2, 1024], F32, hgrn)
        b_att = sb("b_att", [P, B_HEADS, 10 * P], F32, hgrn)
        b_v = sb("b_v", [P, 2, TT, P], F32, hgrn)
        b_gate = sb("b_gate", [P, 2, SEQ], F32, hgrn)
        masks = sb("masks", [P, (MASKED_LEVELS + 1) * P], I32, hgrn)
        hgrn.close()
        bias = sb("bias", [P, 2, 2, SEQ], F32, mixing)
        probs = sb("probs", [P, PROBS, SEQ], F32, mixing)
        probs_t = sb("probs_t", [P, 4, SEQ], F32, mixing)
        mix_a_hi = sb("mix_a_hi", [P, PAIRS, SEQ], F32R, mixing)
        mix_a_lo = sb("mix_a_lo", [P, PAIRS, SEQ], F32R, mixing)
        mix_b_hi = sb("mix_b_hi", [P, 2, SEQ], F32R, mixing)
        mix_b_lo = sb("mix_b_lo", [P, 2, SEQ], F32R, mixing)
        row_sum = sb("row_sum", [P, STEPS], F32, mixing)
        row_min = sb("row_min", [P, STEPS], F32, mixing)
        row_inv = sb("row_inv", [P, STEPS], F32, mixing)
        mixing.close()
        setup = ExitStack()
        sb("under_setup", [P, 68 * 1024 // 4], F32, setup)
        x_rows = sb("x_rows", [P, TT, D], F32, setup)
        vec_rows = sb("vec_rows", [4 * KT + 1, P], F32, setup)
        conv_rows = sb("conv_rows", [2 * FT, 4, P], F32, setup)
        rel_t = sb("rel_t", [N_BUCKETS, HEADS], F32, setup)
        onehot = sb("onehot", [N_BUCKETS, TABLE], F32, setup)
        extra = sb("extra", [HEADS, TABLE], F32, setup)
        table = sb("table", [HEADS, TABLE], F32, setup)
        setup.close()
        conv_g = sb("conv_g", [P, 3, SEQ])
        conv_v = sb("conv_v", [P, 3, SEQ])
        p_hi = sb("p_hi", [P, 2, SEQ], F32R)
        p_lo = sb("p_lo", [P, 2, SEQ], F32R)
        mlp = ExitStack()
        act_hi = sb("act_hi", [P, FT, SEQ], F32R, mlp)
        act_lo = sb("act_lo", [P, FT, SEQ], F32R, mlp)
        mlp.close()
        pe_out = sb("pe_out", [P, KT, SEQ])
        y_rows = sb("y_rows", [P, TT, D])
        gain_row = sb("gain_row", [P, D])
        p_rows = conv_g[:, 0:2, :].rearrange("p a n -> p (a n)").rearrange("p (t c) -> p t c", t=TT)

        banks = [ctx.enter_context(nc.psum_tensor(f"bank{i}", [P, 512], F32)) for i in range(8)]
        acc, score, turned, outs = banks[0:2], banks[2:4], banks[4:6], banks[6:8]
        PE_BANK = (2, 3, 6, 7)
        HALF_BANKS = ((banks[3], banks[7]), (banks[4], banks[5]))

        raw_full = [sem(f"raw_full{i}") for i in range(RAW)]
        whi_ready, wlo_ready, unit_done = sem("whi_ready"), sem("wlo_ready"), sem("unit_done")
        acc_taken = sem("acc_taken")
        ident_in, square_in, masks_in, vec_in, conv_in, table_in = (
            sem(s) for s in ("ident_in", "square_in", "masks_in", "vec_in", "conv_in", "table_in"))
        x_in = [sem(f"x_in{t}") for t in range(TT)]
        filled = sem("filled")
        vec_turned, vec_ready, conv_turned, conv_ready = (
            sem(s) for s in ("vec_turned", "vec_ready", "conv_turned", "conv_ready"))
        x_kept_dve, x_kept_act = sem("x_kept_dve"), sem("x_kept_act")
        table_sum, table_ready, table_out = sem("table_sum"), sem("table_ready"), sem("table_out")
        x_turned, x_ready, sq_ready, sumsq_ready = (sem(s) for s in ("x_turned", "x_ready", "sq_ready", "sumsq_ready"))
        h_hi_ready, h_lo_ready = sem("h_hi_ready"), sem("h_lo_ready")
        rows_squared, newton, diag_ready, row_spread, r_ready = (
            sem(s) for s in ("rows_squared", "newton", "diag_ready", "row_spread", "r_ready"))
        squares_summed, root_chain, root_ready = sem("squares_summed"), sem("root_chain"), sem("root_ready")
        v_turned, v_ready = sem("v_turned"), sem("v_ready")
        z_chain, kin_arg, log_f, g_ready, kin_ready = (sem(s) for s in ("z_chain", "kin_arg", "log_f", "g_ready", "kin_ready"))
        gate_ready, bq_ready = sem("gate_ready"), sem("bq_ready")
        decay_ready, qk_ready, sums_ready = sem("decay_ready"), sem("qk_ready"), sem("sums_ready")
        b_scored, b_kept, b_out, b_squared = (sem(s) for s in ("b_scored", "b_kept", "b_out", "b_squared"))
        b_summed, b_var, b_ln, b_rstd, b_newton = (sem(s) for s in ("b_summed", "b_var", "b_ln", "b_rstd", "b_newton"))
        b_normed, b_gated, b_hi_ready, b_mixed = (sem(s) for s in ("b_normed", "b_gated", "b_hi_ready", "b_mixed"))
        q_hi_ready, q_ready, k_hi_ready, k_ready = (sem(s) for s in ("q_hi_ready", "q_ready", "k_hi_ready", "k_ready"))
        bias_in = [sem("bias_in0"), sem("bias_in1")]
        scored, logits, exped, inverted, normed = (sem(s) for s in ("scored", "logits", "exped", "inverted", "normed"))
        probs_turned, probs_t_ready, weighted = (sem(s) for s in ("probs_turned", "probs_t_ready", "weighted"))
        mix_hi_ready, mix_ready = sem("mix_hi_ready"), sem("mix_ready")
        tap2_ready, tap1_ready, tap0_ready, silu_ready, prod_ready = (
            sem(s) for s in ("tap2_ready", "tap1_ready", "tap0_ready", "silu_ready", "prod_ready"))
        act_hi_ready, act_ready = sem("act_hi_ready"), sem("act_ready")
        p_in, p_turned, p_hi_ready, p_ready = (sem(s) for s in ("p_in", "p_turned", "p_hi_ready", "p_ready"))
        pe_done, pe_kept, sig_ready, gated = sem("pe_done"), sem("pe_kept"), sem("sig_ready"), sem("gated")
        gain_in, y_turned, y_kept, y_squared = (sem(s) for s in ("gain_in", "y_turned", "y_kept", "y_squared"))
        half_done, half_taken, half_sig, half_gated, half_x, half_turned, half_kept = (
            sem(s) for s in ("half_done", "half_taken", "half_sig", "half_gated", "half_x", "half_turned", "half_kept"))
        mean_sum, mean_ready, y_ln, y_guess, y_rstd = (
            sem(s) for s in ("mean_sum", "mean_ready", "y_ln", "y_guess", "y_rstd"))
        y_dve, y_act, stored = (sem(s) for s in ("y_dve", "y_act", "stored"))

        block = ctx.enter_context(nc.Block())
        GROUP_OF = {g[2]: i for i, g in enumerate(GROUPS)}
        GROUP_AT = {(g[0], g[1]): i for i, g in enumerate(GROUPS)}

        def wait_taken(eng, group, rnd=0):
            kind, index, _ = GROUPS[group]
            if kind == "x":
                eng.wait_ge(x_ready, index - KT + 1)
            else:
                eng.wait_ge(acc_taken, rnd * UP_ROUND + sum(g[0] != "x" for g in GROUPS[:group + 1]))

        def halves(tile, pair, s):
            v = tile[:, pair, :].rearrange("p (b t) -> p b t", t=2 * s)
            return v[:, :, 0:s], v[:, :, s:2 * s]

        ATT_AT = {(b, b): b for b in range(TT)}
        ATT_AT.update({(0, 1): 4, (2, 3): 5, (0, 2): 6, (0, 3): 7, (1, 2): 8, (1, 3): 9})

        def values_before_tick(m):
            return sum(ticks_before_values(u + 1) <= m for u in V_UNITS)

        w_dram = {name: a[name][0] for name in ("w_in", "w_out", "w_up", "w_down", "w_pe", "w_pg")}

        @block.sync
        def _(sp):
            def load_unit(u, rnd=0):
                name, k0, nk, c0, ncol = UNITS[u]
                if u >= RAW:
                    sp.wait_ge(wlo_ready, rnd * UP_ROUND + (u - RAW + 1))
                src = w_dram[name][k0 * P:(k0 + nk) * P, bass.ds(rnd * (UP_PAIRS * P) + c0, ncol)]\
                    .rearrange("(k p) c -> p k c", p=P)
                dst = raw[:, u % RAW, 0:nk * ncol].rearrange("p (k c) -> p k c", c=ncol)
                sp.dma_start(dst, src).then_inc(raw_full[u % RAW], 16)

            for t in range(TT):
                sp.dma_start(x_rows[:, t, :], a["x"][0, t * P:(t + 1) * P, :]).then_inc(x_in[t], 16)
                if t == 0:
                    sp.dma_start(square[:, 0:P], a["c_square"][:, 0:P]).then_inc(ident_in, 16)
            load_unit(0)
            load_unit(1)
            sp.dma_start(square[:, P:4 * P], a["c_square"][:, P:4 * P]).then_inc(square_in, 16)
            load_unit(2)
            sp.dma_start(conv_rows[:, 0:3, :], a["conv_w"][0].rearrange("t (b p) -> b t p", p=P)).then_inc(conv_in, 16)
            sp.dma_start(conv_rows[:, 3, :], a["conv_b"][0].rearrange("(b p) -> b p", p=P)).then_inc(conv_in, 16)
            sp.dma_start(rel_t[:, :], a["rel_bias"].rearrange("h b -> b h"), allow_slow_non_contiguous=True).then_inc(table_in, 16)
            sp.dma_start(onehot[:, :], a["c_onehot"]).then_inc(table_in, 16)
            sp.dma_start(extra[:, :], a["c_extra"]).then_inc(table_in, 16)
            sp.dma_start(masks[:, :], a["c_masks"]).then_inc(masks_in, 16)
            for u in range(3, UP + UP_PEELED):
                load_unit(u)
            with sp.Fori(0, UP_ROUNDS, 1) as rnd:
                for u in range(UP + UP_PEELED, UP + UP_PEELED + UP_ROUND):
                    load_unit(u, rnd)
            for u in range(DOWN, N_UNITS):
                load_unit(u)
                if u == DOWN + RAW:
                    sp.wait_ge(prod_ready, FT)
                    sp.dma_start(p_rows, a["p"][0, 0].rearrange("(t p) c -> p t c", p=P)).then_inc(p_in, 16)
                if u == PG + RAW:
                    sp.wait_ge(unit_done, PE_UNITS)
                    sp.dma_start(gain_row[:, :], a["norm_final"].rearrange("(o d) -> o d", o=1).to_broadcast([P, D]))\
                      .then_inc(gain_in, 16)
            for t, done, count in ((0, y_dve, 1), (1, y_act, 1), (2, y_dve, 2), (3, y_act, 2)):
                sp.wait_ge(done, count)
                sp.dma_start(out[0, t * P:(t + 1) * P, :], y_rows[:, t, :]).then_inc(stored, 16)
            sp.wait_ge(stored, 16 * TT)

        @block.tensor
        def _(pe):
            def products(bank, slot, k, nc_cols, c, x_hi, x_lo, first, last):
                at = k * nc_cols + c
                hi, lo = w_hi[:, slot, at:at + P], w_lo[:, slot, at:at + P]
                pe.matmul(bank, hi, x_hi, start=first, stop=False)
                pe.matmul(bank, hi, x_lo, start=False, stop=False)
                return pe.matmul(bank, lo, x_hi, start=False, stop=last)

            def wait_h(stage, k):
                pe.wait_ge(h_lo_ready, stage * KT + k + 1)

            def begin_unit(u, group, rnd=0):
                pe.wait_ge(wlo_ready, rnd * UP_ROUND + (u + 1))
                if group >= 2:
                    wait_taken(pe, group - 2, rnd)

            def sum_squares(stage):
                pe.wait_ge(sumsq_ready, KT * stage)
                pe.matmul(turned[0][:, :], ones, sumsq[:, :], start=True, stop=True).then_inc(squares_summed, 1)

            def spread_row():
                pe.wait_ge(diag_ready, 1)
                pe.matmul(turned[1][:, :], ones, scratch[:, 0, :], start=True, stop=True).then_inc(row_spread, 1)

            def b_round(n):
                level, pair = n // 2, n % 2
                if n < 2:
                    pe.wait_ge(bq_ready, B_HEADS)
                    pe.wait_ge(kin_ready, B_HEADS)
                else:
                    pe.wait_ge(qk_ready, 2 * (n - 1))
                for hh in range(2):
                    use = 2 * n + hh
                    if use >= 2:
                        pe.wait_ge(b_kept, use - 1)
                    bank, at = score[hh], hh * SEQ
                    keys, queries = (b_kin, b_q) if level == 0 else (b_qk, b_qk)
                    if level == HALF_LEVEL:
                        for b in range(TT):
                            first = at + b * P
                            mm = pe.matmul(bank[0:P // 2, b * P // 2:(b + 1) * P // 2],
                                           keys[:, pair, first:first + P // 2], queries[:, pair, first + P // 2:first + P],
                                           start=True, stop=True)
                        mm.then_inc(b_scored, 1)
                        continue
                    if level <= MASKED_LEVELS:
                        places = [(b, b, 1, b) for b in range(TT)]
                    elif level == HALF_LEVEL + 1:
                        places = [(0, 1, 1, 0), (2, 3, 1, 1)]
                    else:
                        places = [(0, 2, 2, 0), (1, 2, 2, 2)]
                    for jb, ib, nb, to in places:
                        mm = pe.matmul(bank[:, to * P:(to + nb) * P],
                                       keys[:, pair, at + jb * P:at + (jb + 1) * P],
                                       queries[:, pair, at + ib * P:at + (ib + nb) * P],
                                       start=True, stop=True)
                    mm.then_inc(b_scored, 1)

            def b_values(pair):
                pe.wait_ge(b_kept, 2 * ROUNDS)
                pe.wait_ge(v_ready, pair + 1)
                for hh in range(2):
                    rows = slice(hh * HEAD, (hh + 1) * HEAD)
                    for ib in range(TT):
                        for jb in range(ib + 1):
                            at = ATT_AT[jb, ib] * P
                            mm = pe.matmul(outs[pair][rows, ib * P:(ib + 1) * P], b_v[:, pair, jb, rows],
                                           b_att[:, 2 * pair + hh, at:at + P], start=(jb == 0), stop=(jb == ib))
                mm.then_inc(b_out, 1)

            def b_norm_sum(pair):
                pe.wait_ge(b_squared, pair + 1)
                pe.wait_ge(v_ready, sum(u + 1 <= B_OUT_SLOT for u in V_UNITS))
                pe.matmul(turned[1 - pair][:, :], half_ones, b_bwd[:, pair, SEQ:2 * SEQ], start=True, stop=True)\
                  .then_inc(b_summed, 1)

            def turn_values(unit):
                g = V_UNITS.index(unit)
                wait_taken(pe, GROUP_OF[unit])
                steps_turned = ticks_before_values(unit + 1) - TURN_LAG
                if steps_turned > 0:
                    pe.wait_ge(probs_t_ready, min(steps_turned, STEPS))
                if g:
                    pe.wait_ge(v_ready, g)
                for t in range(TT):
                    mm = pe.transpose(turned[0][:, t * P:(t + 1) * P], v_t[:, t * P:(t + 1) * P], ident)
                mm.then_inc(v_turned, 1)

            def step_score(n):
                head, i = n // TT, tile_of(n)
                pair = head // 2
                if n % (2 * TT) == 0:
                    pe.wait_ge(q_ready, 2 * (pair + 1))
                    pe.wait_ge(k_ready, 4 * (pair + 1))
                if n >= 2:
                    pe.wait_ge(logits, n - 1)
                keys, hh, queries = (i + 1) * P, head % 2, slice(i * P, (i + 1) * P)
                rows = slice(hh * HEAD, (hh + 1) * HEAD)
                pe.matmul(score[n % 2][:, 0:keys], q_both[:, pair % 3, hh, queries], k_both[:, pair % 3, hh, 0:keys],
                          start=True, stop=False)
                pe.matmul(score[n % 2][:, 0:keys], q_both[rows, pair % 3, hh, queries], k_lo[rows, pair % 3, 0:keys],
                          start=False, stop=True).then_inc(scored, 1)

            def step_turn(n):
                pe.wait_ge(normed, n + 1)
                if n >= 2:
                    pe.wait_ge(probs_t_ready, n - 1)
                else:
                    pe.wait_ge(b_var, 2)
                if n % 2 == 0:
                    pe.wait_ge(v_ready, values_before_tick(n + TURN_LAG))
                for b in range(tile_of(n) + 1):
                    mm = pe.transpose(turned[n % 2][:, b * P:(b + 1) * P], probs[:, n % PROBS, b * P:(b + 1) * P], flip)
                mm.then_inc(probs_turned, 1)

            def step_values(n):
                head, i = n // TT, tile_of(n)
                pair, rows = head // 2, slice((head % 2) * HEAD, (head % 2 + 1) * HEAD)
                pe.wait_ge(probs_t_ready, n + 1)
                if n % (2 * TT) == 0:
                    pe.wait_ge(v_ready, 2 + pair + 1)
                    if pair < 2:
                        pe.wait_ge(b_normed, pair + 1)
                    else:
                        pe.wait_ge(mix_ready, pair - 1)
                for jb in range(i + 1):
                    mm = pe.matmul(outs[pair % 2][rows, i * P:(i + 1) * P], v_tok[:, pair % 3, jb, rows],
                                   probs_t[:, n % 4, jb * P:(jb + 1) * P], start=(jb == 0), stop=(jb == i))
                mm.then_inc(weighted, 1)

            def tick(m):
                if 0 <= m - TURN_LAG < STEPS:
                    step_turn(m - TURN_LAG)
                if m >= VALUE_LAG:
                    step_values(m - VALUE_LAG)
                if m < STEPS:
                    step_score(m)

            def mixers(slot, k):
                for at, n in zip((1, 4, 6), rounds_in(slot)):
                    if k == at:
                        b_round(n)
                if slot == B_OUT_SLOT:
                    if k == 1:
                        b_values(0)
                    if k == 4:
                        b_values(1)
                if slot == B_OUT_SLOT + 1 and k == 2:
                    b_norm_sum(0)
                if slot == B_OUT_SLOT + 1 and k == 4:
                    b_norm_sum(1)
                for at, m in zip(tick_places(slot), ticks_in(slot)):
                    if k == at:
                        tick(m)
                if slot == TICK_SLOTS[-1] and k == LAST_VALUES:
                    step_values(STEPS - 1)
                if slot - 1 in V_UNITS and k == values_place(slot):
                    turn_values(slot - 1)

            pe.wait_ge(ident_in, 16)
            for t in range(TT):
                pe.wait_ge(x_in[t], 16)
                if t >= 2:
                    pe.wait_ge(x_kept_dve, t - 1)
                    pe.wait_ge(x_kept_act, t - 1)
                for f in range(KT):
                    bank = banks[(2, 3, 6, 7)[t % 2 * 2 + f // 4]]
                    mm = pe.transpose(bank[:, f % 4 * P:(f % 4 + 1) * P], x_rows[:, t, f * P:(f + 1) * P], ident)
                    if f % 4 == 3:
                        mm.then_inc(x_turned, 1)
                if t == 2:
                    pe.wait_ge(vec_in, 16 * 5)
                    pe.transpose(banks[4][:, 0:4 * KT + 1], vec_rows[:, :], ident[0:4 * KT + 1, 0:4 * KT + 1])\
                      .then_inc(vec_turned, 1)

            def turn_conv():
                pe.wait_ge(conv_in, 16 * 2)
                pe.wait_ge(vec_ready, 1)
                for c in range(4):
                    mm = pe.transpose(banks[4][:, c * 2 * FT:(c + 1) * 2 * FT], conv_rows[:, c, :], ident[0:2 * FT, 0:2 * FT])
                mm.then_inc(conv_turned, 1)

            def look_up_bias():
                pe.wait_ge(table_in, 16 * 3)
                pe.matmul(outs[0][0:HEADS, :], rel_t[:, :], onehot[:, 0:512], start=True, stop=True)
                pe.matmul(outs[1][0:HEADS, 0:TABLE - 512], rel_t[:, :], onehot[:, 512:TABLE], start=True, stop=True)\
                  .then_inc(table_sum, 1)

            for u in range(PROJ):
                begin_unit(u, GROUP_OF[u])
                for k in range(KT):
                    if u == 0:
                        wait_h(0, k)
                    if u == 1 and k == 5:
                        pe.wait_ge(square_in, 16)
                        spread_row()
                    if u == 2 and k == 5:
                        turn_conv()
                    if u == 3 and k == 5:
                        look_up_bias()
                    mm = products(acc[u % 2][:, :], u % SPLIT, k, P, 0, h_hi[:, k, :], h_lo[:, k, :], k == 0, k == KT - 1)
                    if k == KT - 1:
                        mm.then_inc(unit_done, 1)
                    mixers(u, k)

            def mixed(k):
                if 3 <= k < 5:
                    return mix_b_hi[:, k - 3, :], mix_b_lo[:, k - 3, :]
                pair = k if k < 3 else k - 2
                return mix_a_hi[:, pair, :], mix_a_lo[:, pair, :]

            for u in range(PROJ, UP):
                early = u < PROJ + 2
                begin_unit(u, GROUP_OF[u])
                for k in range(KT - 1 if early else KT):
                    if u == PROJ and k == 3:
                        pe.wait_ge(b_mixed, 2)
                    elif u == PROJ and k < 7:
                        pe.wait_ge(mix_ready, k + 1 if k < 3 else k - 1)
                    mm = products(acc[u % 2][:, :], u % SPLIT, k, P, 0, *mixed(k), k == 0, k == KT - 1)
                    if early:
                        mixers(u, k)
                if u == PROJ + 1:
                    pe.wait_ge(mix_ready, PAIRS)
                    for v in (PROJ, PROJ + 1):
                        products(acc[v % 2][:, :], v % SPLIT, KT - 1, P, 0, *mixed(KT - 1), False, True).then_inc(unit_done, 1)
                if not early:
                    mm.then_inc(unit_done, 1)

            def up_unit(u, rnd=0):
                group = GROUP_OF[u]
                begin_unit(u, group, rnd)
                for k in range(KT):
                    if u == UP:
                        wait_h(1, k)
                        if k == 6:
                            sum_squares(1)
                    mm = products(acc[group % 2][:, :], u % SPLIT, k, P, 0, h_hi[:, k, :], h_lo[:, k, :], k == 0, k == KT - 1)
                mm.then_inc(unit_done, 1)

            for u in range(UP, UP + UP_PEELED):
                up_unit(u)
            with pe.Fori(0, UP_ROUNDS, 1) as rnd:
                for u in range(UP + UP_PEELED, UP + UP_PEELED + UP_ROUND):
                    up_unit(u, rnd)

            for u in range(DOWN, PE_UNITS):
                _, k0, nk, _, _ = UNITS[u]
                f = (u - DOWN) // 3
                group = GROUP_AT["x", 2 * KT + f]
                pe.wait_ge(wlo_ready, u + 1)
                if k0 == 0:
                    wait_taken(pe, group - 2)
                for k in range(nk):
                    if f == 0:
                        pe.wait_ge(act_ready, k0 + k + 1)
                    mm = products(acc[group % 2][:, :], u % SPLIT, k, P, 0, act_hi[:, k0 + k, :], act_lo[:, k0 + k, :],
                                  k0 + k == 0, k0 + k == FT - 1)
                mm.then_inc(unit_done, 1)
                if u == DOWN + 8:
                    pe.wait_ge(p_in, 16)
                    for c in range(2):
                        for t in range(TT):
                            mm = pe.transpose(turned[c][:, t * P:(t + 1) * P], p_rows[:, t, c * P:(c + 1) * P], ident)
                    mm.then_inc(p_turned, 1)

            for u in range(PE_UNITS, PG):
                pe.wait_ge(wlo_ready, u + 1)
                if u == PE_UNITS:
                    pe.wait_ge(p_ready, 2)
                for c in range(4):
                    f = 4 * (u - PE_UNITS) + c
                    if f >= 4:
                        pe.wait_ge(pe_kept, f - 3)
                    for k in range(2):
                        mm = products(banks[PE_BANK[f % 4]][:, :], u % SPLIT, k, 512, c * P, p_hi[:, k, :], p_lo[:, k, :], k == 0, k == 1)
                    mm.then_inc(unit_done if c == 3 else pe_done, 1)
                if u == PE_UNITS:
                    sum_squares(2)

            def turn_result(f):
                pe.wait_ge(x_ready, 2 * KT + f + 1)
                if f >= 3:
                    pe.wait_ge(y_squared, TT * (f - 2))
                for t in range(TT):
                    mm = pe.transpose(banks[(2, 3, 6)[f % 3]][:, t * P:(t + 1) * P], x_t[:, f, t * P:(t + 1) * P], ident)
                mm.then_inc(y_turned, 1)

            for f in range(KT - 1):
                u, group = PG + f, GROUP_AT["ple", f]
                begin_unit(u, group)
                for k in range(KT):
                    if f == 0:
                        wait_h(2, k)
                    if f and k == 6:
                        turn_result(f - 1)
                    mm = products(acc[group % 2][:, :], u % SPLIT, k, P, 0, h_hi[:, k, :], h_lo[:, k, :], k == 0, k == KT - 1)
                mm.then_inc(unit_done, 1)

            def turn_half(h):
                pe.wait_ge(half_x, h + 1)
                for bank in HALF_BANKS[h]:
                    for t in (2 * h, 2 * h + 1):
                        mm = pe.transpose(bank[:, t * P:(t + 1) * P], x_t[:, KT - 1, t * P:(t + 1) * P], ident)
                    mm.then_inc(half_turned, 1)

            u, group = N_UNITS - 1, GROUP_AT["ple", KT - 1]
            begin_unit(u, group)
            for h in range(2):
                half = slice(h * SEQ // 2, (h + 1) * SEQ // 2)
                if h:
                    wait_taken(pe, group - 1)
                for k in range(KT):
                    mm = products(acc[(group + h) % 2][:, half], u % SPLIT, k, P, 0, h_hi[:, k, half], h_lo[:, k, half],
                                  k == 0, k == KT - 1)
                    if h and k == 2:
                        turn_result(KT - 2)
                    if h and k == 6:
                        pe.wait_ge(y_squared, TT * (KT - 3))
                        turn_half(0)
                mm.then_inc(half_done, 1)
            turn_half(1)

        @block.scalar
        def _(act):
            act.preload_act_table_set("natural_log_exp_and_others")
            for i, name in enumerate(("norm_mix", "norm_ffn", "norm_ple", "norm_final")):
                src = a[name] if name == "norm_final" else a[name][0]
                act.dma_start(vec_rows[i * KT:(i + 1) * KT, :], src.rearrange("(k p) -> k p", p=P)).then_inc(vec_in, 16)
            act.dma_start(vec_rows[4 * KT:4 * KT + 1, :].rearrange("o (h c) -> o h c", h=2),
                          a["hgrn_gnorm"].rearrange("(o u) c -> o u c", u=1).to_broadcast([1, 2, HEAD])).then_inc(vec_in, 16)

            def split_hi(u, rnd=0):
                _, _, nk, _, ncol = UNITS[u]
                act.wait_ge(raw_full[u % RAW], rnd * (16 * UP_ROUND // RAW) + 16 * (u // RAW + 1))
                if u >= SPLIT:
                    act.wait_ge(unit_done, rnd * UP_ROUND + (u - SPLIT + 1))
                act.activation(w_hi[:, u % SPLIT, 0:nk * ncol], raw[:, u % RAW, 0:nk * ncol], ACT.Copy)\
                   .then_inc(whi_ready, 1)

            def gain_x(stage, f):
                act.activation(h_hi[:, f, :], x_t[:, f, :], ACT.Copy, scale=vec_cols[:, stage * KT + f:stage * KT + f + 1])\
                   .then_inc(h_hi_ready, 1)

            def square_x(n):
                stage, f = n // KT, n % KT
                if f == 0:
                    if stage:
                        act.wait_ge(squares_summed, stage)
                    act.activation(sumsq[:, :], x_t[:, 0, :], ACT.Square).then_inc(sumsq_ready, 1)
                else:
                    if n > 1:
                        act.wait_ge(sumsq_ready, KT * stage + f - 1)
                    act.activation(scratch[:, 2 + f % 2, :], x_t[:, f, :], ACT.Square).then_inc(sq_ready, 1)

            def spread():
                act.wait_ge(row_spread, 1)
                act.activation(r_row[:, :], turned[1][:, :], ACT.Copy).then_inc(r_ready, 1)

            def root(stage):
                v, guess = scratch[:, 0, :], scratch[:, 1, :]
                act.wait_ge(squares_summed, stage)
                act.activation(v, turned[0][:, :], ACT.Identity, bias=eps_col[:, :], scale=1.0 / D).then_inc(root_chain, 1)
                act.wait_ge(root_chain, 3 * stage - 2)
                act.activation(guess, v, ACT.Ln).then_inc(root_chain, 1)
                act.wait_ge(root_chain, 3 * stage - 1)
                act.activation(guess, guess, ACT.Exp, scale=-0.5).then_inc(root_chain, 1)

            def take(group, rnd=0):
                kind, i, unit = GROUPS[group]
                if kind == "x":
                    n = i - KT
                    act.wait_ge(x_ready, n + 1)
                    gain_x(n // KT + 1, n % KT)
                    square_x(n)
                elif kind == "z":
                    wait_taken(act, group)
                    t = scratch[:, 2 + i % 2, :]
                    if i >= 2:
                        act.wait_ge(log_f, i - 1)
                    act.activation(t, scratch[:, i % 2, :], ACT.Abs).then_inc(z_chain, 1)
                    act.wait_ge(z_chain, 3 * i + 1)
                    act.activation(t, t, ACT.Exp, scale=-1.0).then_inc(z_chain, 1)
                    act.wait_ge(z_chain, 3 * i + 2)
                    act.activation(t, t, ACT.Ln, bias=1.0).then_inc(z_chain, 1)
                elif kind == "g":
                    wait_taken(act, group)
                    act.activation(b_gate[:, i, :], b_gate[:, i, :], ACT.Silu).then_inc(gate_ready, 1)
                elif kind == "bq":
                    wait_taken(act, group)
                    part = b_q[:, i // 2, (i % 2) * SEQ:(i % 2 + 1) * SEQ]
                    act.activation(part, part, ACT.Silu).then_inc(bq_ready, 1)
                elif kind in ("gate", "value"):
                    c = i if kind == "gate" else FT + i
                    n = 2 * i + (kind == "value")
                    dst = (conv_g if kind == "gate" else conv_v)[:, i % 3, :]
                    if i >= 3:
                        if kind == "gate":
                            act.wait_ge(prod_ready, rnd * UP_PAIRS + (i - 2))
                        else:
                            act.wait_ge(act_ready, rnd * UP_PAIRS + (i - 2))
                    if n == 0:
                        act.wait_ge(conv_ready, 1)
                    wait_taken(act, group, rnd)
                    col = bass.ds(rnd * UP_PAIRS + c, 1)
                    act.activation(dst, scratch[:, n % 3, :], ACT.Identity, bias=conv_cols[:, 3, col],
                                   scale=conv_cols[:, 2, col]).then_inc(tap2_ready, 1)
                    if kind == "value":
                        act.wait_ge(tap0_ready, rnd * UP_ROUND + n)
                        act.activation(conv_g[:, i % 3, :], conv_g[:, i % 3, :], ACT.Silu).then_inc(silu_ready, 1)
                elif kind == "ple":
                    wait_taken(act, group)
                    act.activation(conv_g[:, i % 3, :], conv_g[:, i % 3, :], ACT.Sigmoid).then_inc(sig_ready, 1)

            def split_piece(slot, n):
                kind, i, _ = GROUPS[GROUP_OF[slot - 1]]
                if kind not in ("q", "k") or n >= 2:
                    return
                if n == 0:
                    wait_taken(act, GROUP_OF[slot - 1])
                    if i >= 3:
                        act.wait_ge(scored, 2 * TT * (i - 2))
                own = slice(n * HEAD, (n + 1) * HEAD)
                if kind == "q":
                    act.activation(q_both[own, i % 3, n, :], scratch[own, 0, :], ACT.Copy).then_inc(q_hi_ready, 1)
                else:
                    act.activation(k_both[own, i % 3, n, :], scratch[own, 1, :], ACT.Copy).then_inc(k_hi_ready, 1)

            def key_of(h):
                act.wait_ge(kin_arg, h + 1)
                part = b_kin[:, h // 2, (h % 2) * SEQ:(h % 2 + 1) * SEQ]
                act.activation(part, part, ACT.Exp, scale=-1.0).then_inc(kin_ready, 1)

            def decays(n):
                level, pair = n // 2, n % 2
                if n < 4:
                    act.wait_ge(g_ready, B_HEADS)
                    act.wait_ge(filled, 2)
                else:
                    act.wait_ge(sums_ready, 2 * (n - 3))
                    act.wait_ge(b_scored, 2 * (n - 1))
                s = 1 << (level - 1)
                to, back, ahead = halves(b_qk, pair, s), halves(b_bwd, pair, s)[0], halves(b_fwd, pair, s)[1]
                act.activation(to[0], back, ACT.Exp).then_inc(decay_ready, 1)
                act.activation(to[1], ahead, ACT.Exp).then_inc(decay_ready, 1)

            def b_square(pair):
                act.wait_ge(b_out, pair + 1)
                act.activation(b_bwd[:, pair, SEQ:2 * SEQ], outs[pair][:, :], ACT.Square).then_inc(b_squared, 1)

            def b_rstd_of(pair):
                v, r = b_qk[:, pair, 0:SEQ], b_qk[:, pair, SEQ:2 * SEQ]
                act.wait_ge(b_summed, pair + 1)
                act.activation(v, turned[1 - pair][:, :], ACT.Identity, bias=eps_col[:, :], scale=1.0 / HEAD).then_inc(b_var, 1)
                act.wait_ge(b_var, pair + 1)
                act.activation(r, v, ACT.Ln).then_inc(b_ln, 1)
                act.wait_ge(b_ln, pair + 1)
                act.activation(r, r, ACT.Exp, scale=-0.5).then_inc(b_rstd, 1)

            def square_block(f, bank, tiles):
                if f:
                    act.wait_ge(y_squared, TT * f)
                for t in tiles:
                    cols = slice(t * P, (t + 1) * P)
                    act.activation(scratch[:, 2, cols], bank[:, cols], ACT.Square, accum_out=parts[:, t, f:f + 1])\
                       .then_inc(y_squared, 1)

            def square_result(f):
                act.wait_ge(y_kept, f + 1)
                square_block(f, banks[(2, 3, 6)[f % 3]], range(TT))

            def load_bias(pair):
                act.dma_start(bias[:, pair % 2, :, :], bias_of(pair)).then_inc(bias_in[pair % 2], 16)

            def step_exp(n):
                keys = (tile_of(n) + 1) * P
                act.wait_ge(logits, n + 1)
                act.activation(probs[:, n % PROBS, 0:keys], probs[:, n % PROBS, 0:keys], ACT.Exp, scale=-1.0,
                               bias=row_min[:, n:n + 1], accum_out=row_sum[:, n:n + 1]).then_inc(exped, 1)

            def step_keep(n):
                keys = (tile_of(n) + 1) * P
                act.wait_ge(probs_turned, n + 1)
                if n >= 4:
                    act.wait_ge(weighted, n - 3)
                act.activation(probs_t[:, n % 4, 0:keys], turned[n % 2][:, 0:keys], ACT.Copy).then_inc(probs_t_ready, 1)

            def bias_of(pair):
                return bass.AP(tensor=bias_dram.tensor, offset=2 * pair * TABLE, ap=[[1, P], [TABLE, 2], [1, SEQ]])

            def mixers(slot):
                for i, n in enumerate(rounds_in(slot)):
                    if 2 <= n + 1 < ROUNDS:
                        decays(n + 1)
                    split_piece(slot, i)
                if slot == B_OUT_SLOT:
                    act.wait_ge(b_kept, 2 * ROUNDS)
                    act.wait_ge(table_out, 16)
                    load_bias(0)
                    load_bias(1)
                    b_square(0)
                    b_square(1)
                for i, m in enumerate(ticks_in(slot)):
                    if m % (2 * TT) == 0 and 2 * TT <= m < (PAIRS - 1) * 2 * TT:
                        act.wait_ge(logits, m)
                        load_bias(m // (2 * TT) + 1)
                    if 0 <= m - TURN_LAG < STEPS:
                        step_keep(m - TURN_LAG)
                    if m < STEPS:
                        step_exp(m)
                    if slot == B_OUT_SLOT + 1 and i in (1, 2):
                        b_rstd_of(i - 1)
                    if slot < PROJ - 1:
                        split_piece(slot, i)
                if ROUND_SLOT <= slot < PROJ - 1:
                    for n in range(len(rounds_in(slot) or ticks_in(slot)), 2):
                        split_piece(slot, n)

            def square_rows(t):
                act.wait_ge(x_in[t], 16)
                if t:
                    act.wait_ge(rows_squared, t)
                act.activation(scratch[:, 2:4, :].rearrange("p a n -> p (a n)"), x_rows[:, t, :], ACT.Square,
                               accum_out=stat[:, 0, t:t + 1]).then_inc(rows_squared, 1)

            for t in range(TT):
                if t < 3:
                    square_rows(t)
                else:
                    act.wait_ge(vec_turned, 1)
                    act.activation(vec_cols[:, :], banks[4][:, 0:4 * KT + 1], ACT.Copy, scale=-0.5).then_inc(vec_ready, 1)
                    split_hi(0)
                act.wait_ge(x_turned, 2 * t + 2)
                act.activation(x_t[:, 4:8, t * P:(t + 1) * P],
                               banks[(3, 7)[t % 2]][:, :].rearrange("p (f c) -> p f c", f=4), ACT.Copy).then_inc(x_kept_act, 1)
            act.wait_ge(x_kept_act, TT)
            act.wait_ge(x_kept_dve, TT)
            act.wait_ge(vec_ready, 1)
            for f in range(KT):
                gain_x(0, f)
            square_rows(3)
            split_hi(1)
            act.wait_ge(filled, 1)

            def beside_unit(u):
                beside = u == PROJ + 1
                kind = GROUPS[GROUP_OF[u - 1]][0] if u - 1 in GROUP_OF else None
                if beside:
                    mixers(u)
                if kind == "x":
                    take(GROUP_OF[u - 1])
                if u == UP + 1:
                    root(1)
                    act.preload_act_table(ACT.Silu)
                if u == PROJ - 1:
                    for n in range(2):
                        split_piece(u, n)
                if u + 2 < N_UNITS:
                    split_hi(u + 2)
                if u == PE_UNITS:
                    act.preload_act_table_set("natural_log_exp_and_others")
                if u == 1:
                    spread()
                if u == PE_UNITS + 1:
                    root(2)
                    act.preload_act_table(ACT.Sigmoid)
                if 2 <= u < 2 + B_HEADS:
                    key_of(u - 2)
                if kind not in (None, "x"):
                    take(GROUP_OF[u - 1])
                if u == ROUND_SLOT:
                    act.preload_act_table_set("natural_log_exp_and_others")
                if u == 3:
                    act.wait_ge(conv_turned, 1)
                    act.activation(conv_cols[:, :, :], banks[4][:, 0:8 * FT].rearrange("p (c b) -> p c b", c=4),
                                   ACT.Copy).then_inc(conv_ready, 1)
                if u == 6:
                    act.wait_ge(table_ready, 2)
                    act.dma_start(bias_dram, table[:, :]).then_inc(table_out, 16)
                if u <= PROJ and not beside:
                    mixers(u)
                if u == DOWN + 10:
                    act.wait_ge(p_turned, 1)
                    for c in range(2):
                        act.activation(p_hi[:, c, :], turned[c][:, :], ACT.Copy).then_inc(p_hi_ready, 1)
                if PE_UNITS <= u < PG:
                    for c in range(4):
                        f = 4 * (u - PE_UNITS) + c
                        if c < 3:
                            act.wait_ge(pe_done, 3 * (u - PE_UNITS) + c + 1)
                        else:
                            act.wait_ge(unit_done, u + 1)
                        act.activation(pe_out[:, f, :], banks[PE_BANK[f % 4]][:, :], ACT.Copy).then_inc(pe_kept, 1)
                if PG + 1 < u < N_UNITS - 1:
                    square_result(u - 2 - PG)
            for u in range(UP + UP_PEELED):
                beside_unit(u)
            with act.Fori(0, UP_ROUNDS, 1) as rnd:
                for u in range(UP + UP_PEELED, UP + UP_PEELED + UP_ROUND):
                    split_hi(u + 2, rnd)
                    take(GROUP_OF[u - 1], rnd)
            for u in range(DOWN, N_UNITS):
                beside_unit(u)

            def sigmoid_half(h):
                half = conv_g[:, (KT - 1) % 3, h * SEQ // 2:(h + 1) * SEQ // 2]
                act.wait_ge(half_taken, h + 1)
                act.activation(half, half, ACT.Sigmoid).then_inc(half_sig, 1)

            def square_half(h):
                act.wait_ge(half_turned, 2 * h + 2)
                square_block(KT - 1, HALF_BANKS[h][1], (2 * h, 2 * h + 1))

            def guess_half(h):
                v, guess = stat[:, 1, 2 * h:2 * h + 2], stat[:, 2, 2 * h:2 * h + 2]
                act.wait_ge(mean_ready, h + 1)
                act.activation(guess, v, ACT.Ln).then_inc(y_ln, 1)
                act.wait_ge(y_ln, h + 1)
                act.activation(guess, guess, ACT.Exp, scale=-0.5).then_inc(y_guess, 1)

            def scale_half(h):
                t = 2 * h + 1
                act.wait_ge(half_kept, h + 1)
                act.wait_ge(y_rstd, 3 * (h + 1))
                act.activation(y_rows[:, t, :], y_rows[:, t, :], ACT.Copy, scale=stat[:, 0, t:t + 1]).then_inc(y_act, 1)

            sigmoid_half(0)
            square_result(KT - 3)
            square_result(KT - 2)
            square_half(0)
            sigmoid_half(1)
            act.preload_act_table_set("natural_log_exp_and_others")
            guess_half(0)
            scale_half(0)
            square_half(1)
            guess_half(1)
            scale_half(1)

        @block.vector
        def _(dve):
            def split_lo(u, rnd=0):
                _, _, nk, _, ncol = UNITS[u]
                dve.wait_ge(whi_ready, rnd * UP_ROUND + (u + 1))
                dve.tensor_tensor(w_lo[:, u % SPLIT, 0:nk * ncol], raw[:, u % RAW, 0:nk * ncol],
                                  w_hi[:, u % SPLIT, 0:nk * ncol].bitcast(F32), ALU.subtract).then_inc(wlo_ready, 1)

            def lo_x(stage, f):
                dve.wait_ge(h_hi_ready, stage * KT + f + 1)
                dve.scalar_tensor_tensor(out=h_lo[:, f, :], in0=x_t[:, f, :], scalar=vec_cols[:, stage * KT + f:stage * KT + f + 1],
                                         in1=h_hi[:, f, :].bitcast(F32), op0=ALU.mult, op1=ALU.subtract).then_inc(h_lo_ready, 1)

            def rstd_of_rows():
                dve.wait_ge(rows_squared, TT)
                v, y, t = stat[:, 1, :], stat[:, 2, :], stat[:, 3, :]
                n = [0]

                def link(ins):
                    n[0] += 1
                    ins.then_inc(newton, 1)
                    dve.wait_ge(newton, n[0])

                link(dve.tensor_scalar(v, stat[:, 0, :], 1.0 / D, EPS, ALU.mult, ALU.add))
                link(dve.tensor_scalar(stat_bits[:, 0, :], v.bitcast(I32), 1, None, ALU.logical_shift_right))
                link(dve.tensor_scalar(stat_bits[:, 1, :], stat_bits[:, 0, :], -1.0, float(0x5F3759DF), ALU.mult, ALU.add))
                guess = stat_bits[:, 1, :].bitcast(F32)
                for step in range(3):
                    y0 = guess if step == 0 else y
                    link(dve.tensor_tensor(t, v, y0, ALU.mult))
                    if step < 2:
                        link(dve.scalar_tensor_tensor(out=t, in0=t, scalar=-0.5, in1=y0, op0=ALU.mult, op1=ALU.mult))
                        link(dve.scalar_tensor_tensor(out=y, in0=t, scalar=1.5, in1=y0, op0=ALU.add, op1=ALU.mult))
                    else:
                        link(dve.tensor_tensor(t, t, y0, ALU.mult))
                        link(dve.scalar_tensor_tensor(out=y, in0=t, scalar=-3.0, in1=y0, op0=ALU.add, op1=ALU.mult))

            def diagonal():
                to = scratch[:, 0, :].rearrange("p (t c) -> p t c", t=TT)
                dve.tensor_tensor(to, ident.rearrange("p (o c) -> p o c", o=1).to_broadcast([P, TT, P]),
                                  stat[:, 2, :].rearrange("p (t o) -> p t o", o=1).to_broadcast([P, TT, P]), ALU.mult)\
                   .then_inc(diag_ready, 1)

            def root_step(stage):
                v, guess = scratch[:, 0, :], scratch[:, 1, :]
                dve.wait_ge(root_chain, 3 * stage)
                dve.tensor_tensor(v, v, guess, ALU.mult).then_inc(root_ready, 1)
                dve.wait_ge(root_ready, 3 * stage - 2)
                dve.tensor_tensor(v, v, guess, ALU.mult).then_inc(root_ready, 1)
                dve.wait_ge(root_ready, 3 * stage - 1)
                dve.scalar_tensor_tensor(out=r_row[:, :], in0=v, scalar=-3.0, in1=guess, op0=ALU.add, op1=ALU.mult)\
                   .then_inc(root_ready, 1)
                dve.wait_ge(root_ready, 3 * stage)

            def times_r(out, bank):
                return dve.tensor_tensor(out, bank, r_row[:, :], ALU.mult)

            def take(group, rnd=0):
                kind, i, unit = GROUPS[group]
                bank = acc[group % 2]
                dve.wait_ge(unit_done, rnd * UP_ROUND + (unit + 1))
                if group == 0:
                    dve.wait_ge(r_ready, 1)
                if kind == "z":
                    if i >= 2:
                        dve.wait_ge(log_f, i - 1)
                    times_r(scratch[:, i % 2, :], bank[:, :]).then_inc(acc_taken, 1)
                elif kind == "g":
                    times_r(b_gate[:, i, :], bank[:, :]).then_inc(acc_taken, 1)
                elif kind == "bq":
                    times_r(b_q[:, i // 2, (i % 2) * SEQ:(i % 2 + 1) * SEQ], bank[:, :]).then_inc(acc_taken, 1)
                elif kind == "v":
                    if i:
                        dve.wait_ge(v_turned, i)
                    times_r(v_t[:, :], bank[:, :]).then_inc(acc_taken, 1)
                elif kind == "q":
                    if i:
                        dve.wait_ge(q_ready, 2 * i)
                    queries, r_back = (bass.AP(tensor=t.tensor, offset=t.offset + P - 1, ap=[[SEQ, P], [P, TT], [-1, P]])
                                       for t in (bank[:, :], r_row[:, :]))
                    dve.scalar_tensor_tensor(out=scratch[:, 0, :].rearrange("p (t q) -> p t q", t=TT), in0=queries,
                                             scalar=-SCALE, in1=r_back, op0=ALU.mult, op1=ALU.mult).then_inc(acc_taken, 1)
                elif kind == "k":
                    if i:
                        dve.wait_ge(k_ready, 4 * i)
                    times_r(scratch[:, 1, :], bank[:, :]).then_inc(acc_taken, 1)
                elif kind == "x":
                    dve.tensor_tensor(x_t[:, i % KT, :], bank[:, :], x_t[:, i % KT, :], ALU.add).then_inc(x_ready, 1)
                elif kind in ("gate", "value"):
                    n = 2 * i + (kind == "value")
                    if n >= 3:
                        dve.wait_ge(tap0_ready, rnd * UP_ROUND + (n - 2))
                    times_r(scratch[:, n % 3, :], bank[:, :]).then_inc(acc_taken, 1)
                elif kind == "ple":
                    if i >= 3:
                        dve.wait_ge(x_ready, 2 * KT + i - 2)
                    times_r(conv_g[:, i % 3, :], bank[:, :]).then_inc(acc_taken, 1)

            def use(group, rnd=0):
                kind, i, unit = GROUPS[group]
                if kind == "x":
                    lo_x(i // KT, i % KT)
                elif kind == "z":
                    z, log1p = scratch[:, i % 2, :], scratch[:, 2 + i % 2, :]
                    part = slice((i % 2) * SEQ, (i % 2 + 1) * SEQ)
                    dve.wait_ge(z_chain, 3 * i + 3)
                    dve.scalar_tensor_tensor(out=b_kin[:, i // 2, part], in0=z, scalar=0.0, in1=log1p,
                                             op0=ALU.max, op1=ALU.add).then_inc(kin_arg, 1)
                    dve.scalar_tensor_tensor(out=b_fwd[:, i // 2, part], in0=z, scalar=0.0, in1=log1p,
                                             op0=ALU.min, op1=ALU.subtract).then_inc(log_f, 1)
                    dve.wait_ge(log_f, i + 1)
                    dve.tensor_scalar(b_fwd[:, i // 2, part], b_fwd[:, i // 2, part], LOG_FLOOR, None, ALU.max)\
                       .then_inc(g_ready, 1)
                elif kind in ("gate", "value"):
                    c = i if kind == "gate" else FT + i
                    dst = (conv_g if kind == "gate" else conv_v)[:, i % 3, :]
                    n = 2 * i + (kind == "value")
                    u = scratch[:, n % 3, :]
                    col = bass.ds(rnd * UP_PAIRS + c, 1)
                    if n == 0:
                        dve.wait_ge(conv_ready, 1)
                    dve.wait_ge(tap2_ready, rnd * UP_ROUND + (n + 1))
                    dve.scalar_tensor_tensor(out=dst[:, 1:SEQ], in0=u[:, 0:SEQ - 1], scalar=conv_cols[:, 1, col],
                                             in1=dst[:, 1:SEQ], op0=ALU.mult, op1=ALU.add).then_inc(tap1_ready, 1)
                    dve.wait_ge(tap1_ready, rnd * UP_ROUND + (n + 1))
                    dve.scalar_tensor_tensor(out=dst[:, 2:SEQ], in0=u[:, 0:SEQ - 2], scalar=conv_cols[:, 0, col],
                                             in1=dst[:, 2:SEQ], op0=ALU.mult, op1=ALU.add).then_inc(tap0_ready, 1)

            def split_piece(slot, hh):
                kind, i, _ = GROUPS[GROUP_OF[slot - 1]]
                own, other = (slice(h * HEAD, (h + 1) * HEAD) for h in (hh, 1 - hh))
                if kind == "q" and 0 <= hh < 2:
                    dve.wait_ge(q_hi_ready, 2 * i + hh + 1)
                    dve.tensor_tensor(q_both[other, i % 3, hh, :], scratch[own, 0, :],
                                      q_both[own, i % 3, hh, :].bitcast(F32), ALU.subtract).then_inc(q_ready, 1)
                elif kind == "k" and 0 <= hh < 2:
                    dve.wait_ge(k_hi_ready, 2 * i + hh + 1)
                    dve.tensor_copy(k_both[other, i % 3, hh, :], k_both[own, i % 3, hh, :].bitcast(F32)).then_inc(k_ready, 1)
                    dve.tensor_tensor(k_lo[own, i % 3, :], scratch[own, 1, :], k_both[own, i % 3, hh, :].bitcast(F32),
                                      ALU.subtract).then_inc(k_ready, 1)

            def add_gated(f):
                dve.wait_ge(sig_ready, f + 1)
                dve.wait_ge(pe_kept, f + 1)
                g = conv_g[:, f % 3, :]
                dve.tensor_tensor(g, g, pe_out[:, f, :], ALU.mult).then_inc(gated, 1)
                dve.wait_ge(gated, f + 1)
                dve.tensor_tensor(x_t[:, f, :], x_t[:, f, :], g, ALU.add).then_inc(x_ready, 1)

            def keep_result(f):
                dve.wait_ge(y_turned, f + 1)
                cols = slice(f * P, (f + 1) * P)
                dve.tensor_tensor(y_rows[:, :, cols], banks[(2, 3, 6)[f % 3]][:, :].rearrange("p (t c) -> p t c", t=TT),
                                  gain_row[:, cols].rearrange("p (o c) -> p o c", o=1).to_broadcast([P, TT, P]), ALU.mult)\
                   .then_inc(y_kept, 1)

            def split_act(j, rnd=0):
                count, value = rnd * UP_PAIRS + (j + 1), conv_v[:, j % 3, :]
                hi, lo = (t[:, bass.ds(rnd * UP_PAIRS + j, 1), :].rearrange("p o n -> p (o n)") for t in (act_hi, act_lo))
                dve.wait_ge(prod_ready, count)
                dve.tensor_copy(hi, value).then_inc(act_hi_ready, 1)
                dve.wait_ge(act_hi_ready, count)
                dve.tensor_tensor(lo, value, hi.bitcast(F32), ALU.subtract).then_inc(act_ready, 1)

            def decayed(n):
                level, pair = n // 2, n % 2
                dve.wait_ge(decay_ready, 2 * (n - 1))
                s = 1 << (level - 1)
                to, q, k = halves(b_qk, pair, s), halves(b_q, pair, s)[1], halves(b_kin, pair, s)[0]
                dve.tensor_tensor(to[1], to[1], q, ALU.mult).then_inc(qk_ready, 1)
                dve.tensor_tensor(to[0], to[0], k, ALU.mult).then_inc(qk_ready, 1)

            def keep_scores(n):
                level, pair = n // 2, n % 2
                for hh in range(2):
                    use = 2 * n + hh
                    att, bank = b_att[:, 2 * pair + hh, :], score[hh]
                    dve.wait_ge(b_scored, use + 1)
                    if level <= MASKED_LEVELS:
                        if use >= 4:
                            dve.wait_ge(b_kept, use - 3)
                        else:
                            dve.wait_ge(masks_in, 16)
                            dve.wait_ge(table_out, 16)
                        mask = masks[:, level * P:(level + 1) * P].rearrange("p (o i) -> p o i", o=1).to_broadcast([P, TT, P])
                        to = att[:, 0:TT * P].rearrange("p (b i) -> p b i", b=TT)
                        new = bank[:, :].rearrange("p (b i) -> p b i", b=TT)
                        if level == 0:
                            ins = dve.tensor_tensor(to, new, mask, ALU.mult)
                        else:
                            ins = dve.copy_predicated(to, mask, new)
                    elif level == HALF_LEVEL:
                        dve.wait_ge(b_kept, use - 3)
                        ins = dve.tensor_copy(att[0:P // 2, 0:TT * P].rearrange("p (b i) -> p b i", b=TT)[:, :, P // 2:P],
                                              bank[0:P // 2, 0:TT * P // 2].rearrange("p (b i) -> p b i", b=TT))
                    elif level == HALF_LEVEL + 1:
                        ins = dve.tensor_copy(att[:, 4 * P:6 * P], bank[:, 0:2 * P])
                    else:
                        ins = dve.tensor_copy(att[:, 6 * P:10 * P], bank[:, :])
                    ins.then_inc(b_kept, 1)

            def b_norm(pair):
                v, r, c = b_qk[:, pair, 0:SEQ], b_qk[:, pair, SEQ:2 * SEQ], b_bwd[:, pair, 0:SEQ]
                dve.wait_ge(b_rstd, pair + 1)
                dve.tensor_tensor(c, v, r, ALU.mult).then_inc(b_newton, 1)
                dve.wait_ge(b_newton, 3 * pair + 1)
                dve.tensor_tensor(c, c, r, ALU.mult).then_inc(b_newton, 1)
                dve.wait_ge(b_newton, 3 * pair + 2)
                dve.scalar_tensor_tensor(out=v, in0=c, scalar=-3.0, in1=r, op0=ALU.add, op1=ALU.mult).then_inc(b_newton, 1)
                dve.wait_ge(b_newton, 3 * pair + 3)
                t = scratch[:, 2 + pair, :]
                dve.scalar_tensor_tensor(out=t, in0=outs[pair][:, :], scalar=vec_cols[:, 4 * KT:4 * KT + 1], in1=v,
                                         op0=ALU.mult, op1=ALU.mult).then_inc(b_normed, 1)

            def b_mix(pair):
                t = scratch[:, 2 + pair, :]
                dve.wait_ge(b_normed, pair + 1)
                dve.wait_ge(gate_ready, 2)
                dve.tensor_tensor(t, t, b_gate[:, pair, :], ALU.mult).then_inc(b_gated, 1)
                dve.wait_ge(b_gated, pair + 1)
                dve.tensor_copy(mix_b_hi[:, pair, :], t).then_inc(b_hi_ready, 1)
                dve.wait_ge(b_hi_ready, pair + 1)
                dve.tensor_tensor(mix_b_lo[:, pair, :], t, mix_b_hi[:, pair, :].bitcast(F32), ALU.subtract).then_inc(b_mixed, 1)

            def keep_values(unit):
                g = V_UNITS.index(unit)
                dve.wait_ge(v_turned, g + 1)
                if g >= 5:
                    dve.wait_ge(weighted, 2 * TT * (g - 4))
                to = b_v[:, g, :, :] if g < 2 else v_tok[:, (g - 2) % 3, :, :]
                dve.tensor_copy(to, turned[0][:, :].rearrange("p (t c) -> p t c", t=TT)).then_inc(v_ready, 1)

            def step_logits(n):
                head, i = n // TT, tile_of(n)
                pair, keys = head // 2, (i + 1) * P
                if n % (2 * TT) == 0:
                    dve.wait_ge(bias_in[pair % 2], 16 * (pair // 2 + 1))
                dve.wait_ge(scored, n + 1)
                if n >= PROBS:
                    dve.wait_ge(probs_turned, n - PROBS + 1)
                dve.tensor_tensor_reduce(out=probs[:, n % PROBS, 0:keys], in0=score[n % 2][:, 0:keys],
                                         in1=bias[:, pair % 2, head % 2, SEQ - keys:SEQ], scale=1.0, scalar=3.0e38,
                                         op0=ALU.add, op1=ALU.min, accum_out=row_min[:, n:n + 1]).then_inc(logits, 1)

            def step_invert(n):
                dve.wait_ge(exped, n + 1)
                dve.reciprocal(row_inv[:, n:n + 1], row_sum[:, n:n + 1]).then_inc(inverted, 1)

            def keep_mixed(pair):
                dve.wait_ge(weighted, 2 * TT * (pair + 1))
                dve.tensor_copy(mix_a_hi[:, pair, :], outs[pair % 2][:, :]).then_inc(mix_hi_ready, 1)
                dve.wait_ge(mix_hi_ready, pair + 1)
                dve.tensor_tensor(mix_a_lo[:, pair, :], outs[pair % 2][:, :], mix_a_hi[:, pair, :].bitcast(F32), ALU.subtract)\
                   .then_inc(mix_ready, 1)

            def mixers(slot):
                for i, n in enumerate(rounds_in(slot)):
                    if 2 <= n + 1 < ROUNDS:
                        decayed(n + 1)
                    keep_scores(n)
                    split_piece(slot, i - 1)
                first = ticks_in(slot)[0] if slot in TICK_SLOTS else 0
                values_at = ticks_before_values(slot) - first if slot - 1 in V_UNITS else None
                if values_at == 0 or (values_at is not None and slot not in TICK_SLOTS):
                    keep_values(slot - 1)
                for i, m in enumerate(ticks_in(slot)):
                    if m < STEPS:
                        step_logits(m)
                    if 0 < m <= STEPS:
                        step_invert(m - 1)
                    if i == 0 and split_late(slot):
                        split_lo(slot + 2)
                    if values_at == i + 1:
                        keep_values(slot - 1)
                    if m - VALUE_LAG >= 0 and (m - VALUE_LAG) % (2 * TT) == 2 * TT - 1:
                        keep_mixed((m - VALUE_LAG) // (2 * TT))
                    if slot < PROJ - 1:
                        split_piece(slot, i - 1)
                    if (slot - B_OUT_SLOT, i) in ((1, 3), (2, 1)):
                        b_norm(slot - B_OUT_SLOT - 1)
                    if (slot - B_OUT_SLOT, i) in ((3, 3), (4, 3)):
                        b_mix(slot - B_OUT_SLOT - 3)
                if slot == TICK_SLOTS[-1]:
                    keep_mixed(PAIRS - 1)
                if ROUND_SLOT <= slot < PROJ - 1:
                    for hh in range(max(len(rounds_in(slot) or ticks_in(slot)) - 1, 0), 2):
                        split_piece(slot, hh)

            for t in range(TT):
                dve.wait_ge(x_turned, 2 * t + 1)
                dve.tensor_copy(x_t[:, 0:4, t * P:(t + 1) * P], banks[(2, 6)[t % 2]][:, :].rearrange("p (f c) -> p f c", f=4))\
                   .then_inc(x_kept_dve, 1)
            split_lo(0)
            dve.wait_ge(x_kept_dve, TT)
            dve.wait_ge(x_kept_act, TT)
            for f in range(KT):
                lo_x(0, f)
            split_lo(1)
            rstd_of_rows()
            dve.wait_ge(ident_in, 16)
            diagonal()

            def finish_table():
                dve.wait_ge(table_in, 16 * 3)
                dve.wait_ge(table_sum, 1)
                dve.scalar_tensor_tensor(out=table[:, 0:512], in0=outs[0][0:HEADS, :], scalar=-1.0, in1=extra[:, 0:512],
                                         op0=ALU.mult, op1=ALU.subtract).then_inc(table_ready, 1)
                dve.scalar_tensor_tensor(out=table[:, 512:TABLE], in0=outs[1][0:HEADS, 0:TABLE - 512], scalar=-1.0,
                                         in1=extra[:, 512:TABLE], op0=ALU.mult, op1=ALU.subtract).then_inc(table_ready, 1)

            def beside_unit(u):
                beside = u == PROJ + 1
                kind = GROUPS[GROUP_OF[u - 1]][0] if u - 1 in GROUP_OF else None
                if beside:
                    mixers(u)
                if u == UP + 1:
                    root_step(1)
                if u - 1 in GROUP_OF:
                    take(GROUP_OF[u - 1])
                if u == PROJ - 1:
                    for hh in range(2):
                        split_piece(u, hh)
                if u + 2 < N_UNITS and not split_late(u):
                    split_lo(u + 2)
                if kind:
                    use(GROUP_OF[u - 1])
                if u == 4:
                    finish_table()
                if UP + 2 < u <= DOWN + 1 and (u - UP) % 2 == 1:
                    split_act((u - UP) // 2 - 1)
                if u <= PROJ and not beside:
                    mixers(u)
                if u == DOWN + 10:
                    for c in range(2):
                        dve.wait_ge(p_hi_ready, c + 1)
                        dve.tensor_tensor(p_lo[:, c, :], turned[c][:, :], p_hi[:, c, :].bitcast(F32), ALU.subtract).then_inc(p_ready, 1)
                if u == PE_UNITS + 1:
                    root_step(2)
                if u > PG:
                    add_gated(u - 1 - PG)
                    if u > PG + 1:
                        if u == PG + 2:
                            dve.wait_ge(gain_in, 16)
                        keep_result(u - 2 - PG)
            for u in range(UP + UP_PEELED):
                beside_unit(u)
            with dve.Fori(0, UP_ROUNDS, 1) as rnd:
                for u in range(UP + UP_PEELED, UP + UP_PEELED + UP_ROUND):
                    take(GROUP_OF[u - 1], rnd)
                    split_lo(u + 2, rnd)
                    use(GROUP_OF[u - 1], rnd)
                    if (u - UP) % 2 == 1:
                        split_act((u - UP) // 2 - 1, rnd)
            for u in range(DOWN, N_UNITS):
                beside_unit(u)

            def take_half(h):
                half, f = slice(h * SEQ // 2, (h + 1) * SEQ // 2), KT - 1
                dve.wait_ge(half_done, h + 1)
                dve.tensor_tensor(conv_g[:, f % 3, half], acc[(GROUP_AT["ple", f] + h) % 2][:, half], r_row[:, half],
                                  ALU.mult).then_inc(half_taken, 1)

            def gate_half(h):
                half, f = slice(h * SEQ // 2, (h + 1) * SEQ // 2), KT - 1
                g = conv_g[:, f % 3, half]
                dve.wait_ge(half_sig, h + 1)
                dve.tensor_tensor(g, g, pe_out[:, f, half], ALU.mult).then_inc(half_gated, 1)
                dve.wait_ge(half_gated, h + 1)
                dve.tensor_tensor(x_t[:, f, half], x_t[:, f, half], g, ALU.add).then_inc(half_x, 1)

            def keep_half(h):
                tiles, cols = slice(2 * h, 2 * h + 2), slice((KT - 1) * P, KT * P)
                dve.wait_ge(half_turned, 2 * h + 1)
                dve.tensor_tensor(y_rows[:, tiles, cols],
                                  HALF_BANKS[h][0][:, h * SEQ // 2:(h + 1) * SEQ // 2].rearrange("p (t c) -> p t c", t=2),
                                  gain_row[:, cols].rearrange("p (o c) -> p o c", o=1).to_broadcast([P, 2, P]), ALU.mult)\
                   .then_inc(half_kept, 1)

            def mean_half(h):
                tiles = slice(2 * h, 2 * h + 2)
                dve.wait_ge(y_squared, TT * (KT - 1) + 2 * (h + 1))
                dve.tensor_reduce(out=stat[:, 0, tiles], in_=parts[:, tiles, :], axis=mybir.AxisListType.X, op=ALU.add)\
                   .then_inc(mean_sum, 1)
                dve.wait_ge(mean_sum, h + 1)
                dve.tensor_scalar(stat[:, 1, tiles], stat[:, 0, tiles], 1.0 / D, EPS, ALU.mult, ALU.add).then_inc(mean_ready, 1)

            def root_half(h):
                y, v, guess, t = (stat[:, n, 2 * h:2 * h + 2] for n in range(4))
                dve.wait_ge(y_guess, h + 1)
                dve.tensor_tensor(t, v, guess, ALU.mult).then_inc(y_rstd, 1)
                dve.wait_ge(y_rstd, 3 * h + 1)
                dve.scalar_tensor_tensor(out=t, in0=t, scalar=-0.5, in1=guess, op0=ALU.mult, op1=ALU.mult).then_inc(y_rstd, 1)
                dve.wait_ge(y_rstd, 3 * h + 2)
                dve.scalar_tensor_tensor(out=y, in0=t, scalar=1.5, in1=guess, op0=ALU.add, op1=ALU.mult).then_inc(y_rstd, 1)

            def scale_half(h):
                dve.wait_ge(half_kept, h + 1)
                dve.wait_ge(y_rstd, 3 * (h + 1))
                dve.tensor_scalar(y_rows[:, 2 * h, :], y_rows[:, 2 * h, :], stat[:, 0, 2 * h:2 * h + 1], None, ALU.mult)\
                   .then_inc(y_dve, 1)

            take_half(0)
            keep_result(KT - 2)
            gate_half(0)
            keep_half(0)
            take_half(1)
            mean_half(0)
            gate_half(1)
            root_half(0)
            scale_half(0)
            keep_half(1)
            mean_half(1)
            root_half(1)
            scale_half(1)

        @block.gpsimd
        def _(pool):
            pool.memset(eps_col[:, :], EPS).then_inc(filled, 1)
            pool.wait_ge(filled, 1)
            pool.memset(b_bwd[:, :, :], 0.0).then_inc(filled, 1)
            pool.wait_ge(filled, 2)

            def add_squares(stage, f):
                pool.wait_ge(sq_ready, (KT - 1) * stage + f)
                pool.wait_ge(sumsq_ready, KT * stage + f)
                pool.tensor_tensor(sumsq[:, :], sumsq[:, :], scratch[:, 2 + f % 2, :], ALU.add).then_inc(sumsq_ready, 1)

            for n in range(2, ROUNDS - 2):
                level, pair = n // 2, n % 2
                s = 1 << (level - 1)
                (fwd1, fwd2), back = halves(b_fwd, pair, s), halves(b_bwd, pair, s)[0]
                like = [P, SEQ // s, s]
                pool.wait_ge(decay_ready, 2 * (n - 1))
                pool.tensor_tensor(back, back, fwd2[:, :, s - 1:s].to_broadcast(like), ALU.add).then_inc(sums_ready, 1)
                pool.wait_ge(sums_ready, 2 * (n - 2) + 1)
                pool.tensor_tensor(fwd2, fwd2, fwd1[:, :, s - 1:s].to_broadcast(like), ALU.add).then_inc(sums_ready, 1)
            for n in range(STEPS):
                keys = (tile_of(n) + 1) * P
                pool.wait_ge(inverted, n + 1)
                pool.tensor_scalar(probs[:, n % PROBS, 0:keys], probs[:, n % PROBS, 0:keys], row_inv[:, n:n + 1], None, ALU.mult)\
                    .then_inc(normed, 1)
            for f in range(1, KT):
                add_squares(0, f)
            def multiply(j, rnd=0):
                pool.wait_ge(silu_ready, rnd * UP_PAIRS + (j + 1))
                pool.wait_ge(tap0_ready, rnd * UP_ROUND + (2 * j + 2))
                pool.tensor_tensor(conv_v[:, j % 3, :], conv_g[:, j % 3, :], conv_v[:, j % 3, :], ALU.mult).then_inc(prod_ready, 1)

            for j in range(UP_PEELED // 2):
                multiply(j)
            with pool.Fori(0, UP_ROUNDS, 1) as rnd:
                for j in range(UP_PEELED // 2, UP_PEELED // 2 + UP_PAIRS):
                    multiply(j, rnd)
            for f in range(1, KT):
                add_squares(1, f)


_INS = ["x", "p", "rel_bias", "norm_mix", "w_in", "w_out", "hgrn_gnorm", "norm_ffn", "w_up", "conv_w", "conv_b",
        "w_down", "norm_ple", "w_pe", "w_pg", "norm_final"]


def kernel(**inputs):
    import concourse.bacc as _bacc
    from concourse.bass_utils import run_bass_kernel_spmd as _run

    nc = _bacc.Bacc("TRN2", target_bir_lowering=False, num_devices=1)
    arrays = {f"in_{name}": np.ascontiguousarray(inputs[name]) for name in _INS}
    arrays.update({f"in_{name}": c for name, c in shape_constants().items()})
    aps = {name[3:]: nc.dram_tensor(name, v.shape, mybir.dt.from_np(v.dtype), kind="ExternalInput").ap()
           for name, v in arrays.items()}
    out = nc.dram_tensor("out", (1, SEQ, D), F32, kind="ExternalOutput").ap()
    build(nc, aps, out)
    return _run(nc, [arrays], core_ids=[0]).results[0]["out"]
```
